# Optimizing a Trainium2 kernel written in Bass

```python
import math
import jax, jax.numpy as jnp
from jax import lax
import numpy as np

D_MODEL = 1024
BATCH = 1
SEQ = 512
DEPTH = 1
DEC_BATCH = 8
DEC_SEQ = 8
PAST_LEN = 2048
PAGE_SIZE = 128

MIX_W = D_MODEL
ATT_W = MIX_W // 2
SGU_W = MIX_W - ATT_W
N_ATT_HEADS = 8
D_V = ATT_W // N_ATT_HEADS
D_QK = D_V // 2
N_SGU_GROUPS = 8
SGU_GC = SGU_W // N_SGU_GROUPS
CHUNK = 128
IN_W = 3 * ATT_W + 2 * SGU_W
N_EXPERT_GROUPS = 4
EXPERTS_PER_GROUP = 4
N_EXPERTS = N_EXPERT_GROUPS * EXPERTS_PER_GROUP
TOP_K_IN_GROUP = 2
D_EXPERT = D_MODEL // 2
Q_BLOCK = 128
KV_PAGES_PER_STEP = 8
EPS = 1e-6

kernel_name = "hymba_diffattn_sgu_hmoe_step"

F32 = jnp.float32

def rms_norm(x, g):
    xf = x.astype(F32)
    y = xf * lax.rsqrt(jnp.mean(xf * xf, axis=-1, keepdims=True) + EPS)
    return (y * g.astype(F32)).astype(x.dtype)

def layer_norm(x, g, b):
    xf = x.astype(F32)
    mu = jnp.mean(xf, axis=-1, keepdims=True)
    xc = xf - mu
    y = xc * lax.rsqrt(jnp.mean(xc * xc, axis=-1, keepdims=True) + EPS)
    return (y * g.astype(F32) + b.astype(F32)).astype(x.dtype)

def alibi_slopes(n_heads):
    return 2.0 ** (-8.0 * jnp.arange(1, n_heads + 1, dtype=F32) / n_heads)

def diff_lambda(lq1, lk1, lq2, lk2, lam_init):
    return (jnp.exp(jnp.sum(lq1.astype(F32) * lk1.astype(F32)))
            - jnp.exp(jnp.sum(lq2.astype(F32) * lk2.astype(F32))) + lam_init)

def diff_attn_prompt(q, k, v, lam, slopes):
    B, S, H = q.shape[:3]
    nb = S // Q_BLOCK
    qb = (q.astype(F32) * D_QK ** -0.5).reshape(B, nb, Q_BLOCK, H, 2, D_QK).transpose(1, 0, 2, 3, 4, 5)
    kf = k.astype(F32)
    vf = v.astype(F32)
    kpos = jnp.arange(S)

    def one_block(args):
        qi, i = args
        qpos = i * Q_BLOCK + jnp.arange(Q_BLOCK)
        dist = (qpos[:, None] - kpos[None, :]).astype(F32)
        s = jnp.einsum('bqhjd,bkhjd->bjhqk', qi, kf) - slopes[:, None, None] * dist
        s = jnp.where(dist >= 0, s, -jnp.inf)
        p = jax.nn.softmax(s, axis=-1)
        a = p[:, 0] - lam * p[:, 1]
        return jnp.einsum('bhqk,bkhd->bqhd', a, vf)

    o = lax.map(one_block, (qb, jnp.arange(nb)))
    return o.transpose(1, 0, 2, 3, 4).reshape(B, S, H, D_V).astype(v.dtype)

def diff_attn_sample(q, k, v, lam, cache_k, cache_v, page_table, slopes):
    Bd, T, H = q.shape[:3]
    n_pages = page_table.shape[1]
    pps = math.gcd(n_pages, KV_PAGES_PER_STEP)
    n_steps = n_pages // pps
    blk = pps * PAGE_SIZE
    past = n_pages * PAGE_SIZE
    qf = q.astype(F32) * D_QK ** -0.5
    qpos = past + jnp.arange(T)
    dist = (qpos[:, None] - qpos[None, :]).astype(F32)
    s = jnp.einsum('bqhjd,bkhjd->bjhqk', qf, k.astype(F32)) - slopes[:, None, None] * dist
    s = jnp.where(dist >= 0, s, -jnp.inf)
    m = jnp.max(s, axis=-1)
    p = jnp.exp(s - m[..., None])
    l = jnp.sum(p, axis=-1)
    acc = jnp.einsum('bjhqk,bkhd->bjhqd', p, v.astype(F32))
    pt = page_table.reshape(Bd, n_steps, pps).transpose(1, 0, 2)

    def step(carry, xs):
        m, l, acc = carry
        pages, j = xs
        kb = cache_k[pages].reshape(Bd, blk, H, 2, D_QK).astype(F32)
        vb = cache_v[pages].reshape(Bd, blk, H, D_V).astype(F32)
        kpos = j * blk + jnp.arange(blk)
        d = (qpos[:, None] - kpos[None, :]).astype(F32)
        sb = jnp.einsum('bqhjd,bkhjd->bjhqk', qf, kb) - slopes[:, None, None] * d
        m_new = jnp.maximum(m, jnp.max(sb, axis=-1))
        corr = jnp.exp(m - m_new)
        pb = jnp.exp(sb - m_new[..., None])
        l_new = l * corr + jnp.sum(pb, axis=-1)
        acc_new = acc * corr[..., None] + jnp.einsum('bjhqk,bkhd->bjhqd', pb, vb)
        return (m_new, l_new, acc_new), None

    (m, l, acc), _ = lax.scan(step, (m, l, acc), (pt, jnp.arange(n_steps)))
    o = acc / l[..., None]
    a = o[:, 0] - lam * o[:, 1]
    return a.transpose(0, 2, 1, 3).astype(v.dtype)

def spatial_gating(u, vs, ws, bs, chunk_len):
    B, S, _ = vs.shape
    n = S // chunk_len
    causal = jnp.tril(jnp.ones((chunk_len, chunk_len), dtype=ws.dtype))
    wm = ws[:, :chunk_len, :chunk_len] * causal
    vb = vs.reshape(B, n, chunk_len, N_SGU_GROUPS, SGU_GC)
    mixed = jnp.einsum('gts,bnsgc->bntgc', wm, vb) + bs[:, :chunk_len].T[None, None, :, :, None]
    return u * mixed.reshape(B, S, SGU_W)

def hier_moe(x, w_rg, b_rg, w_re, b_re, w_gate, w_up, w_down):
    N = x.shape[0]
    g_logits = (x @ w_rg).astype(F32) + b_rg.astype(F32)
    g_prob = jax.nn.softmax(g_logits, axis=-1)
    g_idx = jnp.argmax(g_logits, axis=-1)
    g_w = jnp.take_along_axis(g_prob, g_idx[:, None], axis=-1)
    e_logits = ((x @ w_re).astype(F32) + b_re.astype(F32)).reshape(N, N_EXPERT_GROUPS, EXPERTS_PER_GROUP)
    e_in = jnp.take_along_axis(e_logits, g_idx[:, None, None], axis=1)[:, 0]
    top_p, top_i = lax.top_k(jax.nn.softmax(e_in, axis=-1), TOP_K_IN_GROUP)
    wts = top_p / jnp.sum(top_p, axis=-1, keepdims=True) * g_w
    expert_id = g_idx[:, None] * EXPERTS_PER_GROUP + top_i
    gates = jnp.sum(jax.nn.one_hot(expert_id, N_EXPERTS, dtype=F32) * wts[..., None], axis=1).astype(x.dtype)
    y = jnp.zeros_like(x)
    for e in range(N_EXPERTS):
        hdn = jax.nn.silu(x @ w_gate[e]) * (x @ w_up[e])
        y = y + gates[:, e:e + 1] * (hdn @ w_down[e])
    return y

def run_layer(x, c, attend, chunk_len, lam_init,
              w_ada, b_ada, g_pre_mix, g_post_mix, g_pre_ffn, g_post_ffn,
              w_in, lam_q1, lam_k1, lam_q2, lam_k2, g_subln, sgu_ln_g, sgu_ln_b, sgu_ws, sgu_bs, w_out,
              w_rg, b_rg, w_re, b_re, w_gate, w_up, w_down):
    B, S, _ = x.shape
    mod = jax.nn.silu(c) @ w_ada + b_ada
    sh1, sc1, ga1, sh2, sc2, ga2 = [mm[:, None, :] for mm in jnp.split(mod, 6, axis=-1)]
    h = rms_norm(x, g_pre_mix) * (1 + sc1) + sh1
    z = h @ w_in
    zq, zk, zv, zu, zs = jnp.split(z, [ATT_W, 2 * ATT_W, 3 * ATT_W, 3 * ATT_W + SGU_W], axis=-1)
    q = zq.reshape(B, S, N_ATT_HEADS, 2, D_QK)
    k = zk.reshape(B, S, N_ATT_HEADS, 2, D_QK)
    v = zv.reshape(B, S, N_ATT_HEADS, D_V)
    lam = diff_lambda(lam_q1, lam_k1, lam_q2, lam_k2, lam_init)
    a = rms_norm(attend(q, k, v, lam), g_subln) * (1.0 - lam_init)
    u = jax.nn.gelu(zu)
    vs = layer_norm(jax.nn.gelu(zs), sgu_ln_g, sgu_ln_b)
    s_out = spatial_gating(u, vs, sgu_ws, sgu_bs, chunk_len)
    mix = jnp.concatenate([a.reshape(B, S, ATT_W), s_out], axis=-1) @ w_out
    x = x + ga1 * rms_norm(mix, g_post_mix)
    h2 = rms_norm(x, g_pre_ffn) * (1 + sc2) + sh2
    f = hier_moe(h2.reshape(B * S, D_MODEL), w_rg, b_rg, w_re, b_re, w_gate, w_up, w_down).reshape(B, S, D_MODEL)
    x = x + ga2 * rms_norm(f, g_post_ffn)
    return x, k.reshape(B, S, N_ATT_HEADS, 2 * D_QK), v, vs[:, S - chunk_len:]

def setup_inputs(seed: int = 0) -> dict:
    key = jax.random.key(seed)
    ks = iter(jax.random.split(key, 48))

    def nrm(shape, scale):
        return jax.random.normal(next(ks), shape, F32) * scale

    n_pages = PAST_LEN // PAGE_SIZE
    n_pool = (5 * DEC_BATCH * n_pages) // 4
    page_table = jax.random.permutation(next(ks), n_pool)[:DEC_BATCH * n_pages].reshape(DEC_BATCH, n_pages).astype(jnp.int32)
    L = DEPTH
    return {
        "x_prompt": nrm((BATCH, SEQ, D_MODEL), 1.0),
        "x_sample": nrm((DEC_BATCH, DEC_SEQ, D_MODEL), 1.0),
        "cache_k": nrm((L, n_pool, PAGE_SIZE, N_ATT_HEADS, 2 * D_QK), 1.0),
        "cache_v": nrm((L, n_pool, PAGE_SIZE, N_ATT_HEADS, D_V), 1.0),
        "page_table": page_table,
        "c_prompt": nrm((BATCH, D_MODEL), 1.0),
        "c_sample": nrm((DEC_BATCH, D_MODEL), 1.0),
        "w_ada": nrm((L, D_MODEL, 6 * D_MODEL), 0.5 * D_MODEL ** -0.5),
        "b_ada": nrm((L, 6 * D_MODEL), 0.02),
        "g_pre_mix": 1.0 + nrm((L, D_MODEL), 0.05),
        "g_post_mix": 1.0 + nrm((L, D_MODEL), 0.05),
        "g_pre_ffn": 1.0 + nrm((L, D_MODEL), 0.05),
        "g_post_ffn": 1.0 + nrm((L, D_MODEL), 0.05),
        "w_in": nrm((L, D_MODEL, IN_W), D_MODEL ** -0.5),
        "lam_q1": nrm((L, D_QK), 0.1),
        "lam_k1": nrm((L, D_QK), 0.1),
        "lam_q2": nrm((L, D_QK), 0.1),
        "lam_k2": nrm((L, D_QK), 0.1),
        "g_subln": 1.0 + nrm((L, D_V), 0.05),
        "sgu_ln_g": 1.0 + nrm((L, SGU_W), 0.05),
        "sgu_ln_b": nrm((L, SGU_W), 0.02),
        "sgu_ws": nrm((L, N_SGU_GROUPS, CHUNK, CHUNK), CHUNK ** -0.5),
        "sgu_bs": 1.0 + nrm((L, N_SGU_GROUPS, CHUNK), 0.02),
        "w_out": nrm((L, MIX_W, D_MODEL), MIX_W ** -0.5),
        "w_rg": nrm((L, D_MODEL, N_EXPERT_GROUPS), D_MODEL ** -0.5),
        "b_rg": nrm((L, N_EXPERT_GROUPS), 0.01),
        "w_re": nrm((L, D_MODEL, N_EXPERTS), D_MODEL ** -0.5),
        "b_re": nrm((L, N_EXPERTS), 0.01),
        "w_gate": nrm((L, N_EXPERTS, D_MODEL, D_EXPERT), D_MODEL ** -0.5),
        "w_up": nrm((L, N_EXPERTS, D_MODEL, D_EXPERT), D_MODEL ** -0.5),
        "w_down": nrm((L, N_EXPERTS, D_EXPERT, D_MODEL), D_EXPERT ** -0.5),
    }

def reference(x_prompt, x_sample, cache_k, cache_v, page_table, c_prompt, c_sample,
              w_ada, b_ada, g_pre_mix, g_post_mix, g_pre_ffn, g_post_ffn,
              w_in, lam_q1, lam_k1, lam_q2, lam_k2, g_subln, sgu_ln_g, sgu_ln_b, sgu_ws, sgu_bs, w_out,
              w_rg, b_rg, w_re, b_re, w_gate, w_up, w_down):
    slopes = alibi_slopes(N_ATT_HEADS)
    xp, xs = x_prompt, x_sample
    kp_all, vp_all, sp_all, ks_all, vs_all, ss_all = [], [], [], [], [], []
    for l in range(DEPTH):
        lam_init = 0.8 - 0.6 * math.exp(-0.3 * l)
        lp = (w_ada[l], b_ada[l], g_pre_mix[l], g_post_mix[l], g_pre_ffn[l], g_post_ffn[l],
              w_in[l], lam_q1[l], lam_k1[l], lam_q2[l], lam_k2[l], g_subln[l], sgu_ln_g[l], sgu_ln_b[l],
              sgu_ws[l], sgu_bs[l], w_out[l], w_rg[l], b_rg[l], w_re[l], b_re[l], w_gate[l], w_up[l], w_down[l])
        ck, cv = cache_k[l], cache_v[l]
        attend_p = lambda q, k, v, lam: diff_attn_prompt(q, k, v, lam, slopes)
        attend_s = lambda q, k, v, lam: diff_attn_sample(q, k, v, lam, ck, cv, page_table, slopes)
        xp, kp, vp, sp = run_layer(xp, c_prompt, attend_p, CHUNK, lam_init, *lp)
        xs, ksm, vsm, ssm = run_layer(xs, c_sample, attend_s, x_sample.shape[1], lam_init, *lp)
        kp_all.append(kp); vp_all.append(vp); sp_all.append(sp)
        ks_all.append(ksm); vs_all.append(vsm); ss_all.append(ssm)
    return (xp, xs, jnp.stack(kp_all), jnp.stack(vp_all), jnp.stack(sp_all),
            jnp.stack(ks_all), jnp.stack(vs_all), jnp.stack(ss_all))


_drawn_inputs = setup_inputs


def setup_inputs(seed=0):
    import zlib

    import numpy as np

    out = dict(_drawn_inputs(seed))
    spreads = {}
    factors = {'g_post_ffn': 4.085,
     'lam_q1': 3.72,
     'lam_k1': 4.334,
     'lam_q2': 3.919,
     'lam_k2': 3.804,
     'sgu_bs': 4.377,
     'b_re': 7.126}
    for name, (base, spread) in spreads.items():
        noise = np.random.default_rng([zlib.crc32(name.encode()), seed]).standard_normal(out[name].shape)
        drawn = base * np.exp(spread * noise) if base else spread * noise
        out[name] = __import__('jax').numpy.asarray(drawn.astype(out[name].dtype))
    for name, factor in factors.items():
        out[name] = (out[name] * factor).astype(out[name].dtype)
    return out
```

```python
import math
from contextlib import ExitStack

import numpy as np

import concourse.bass as bass
from concourse import mybir

ALU = mybir.AluOpType
ACT = mybir.ActivationFunctionType
F32 = mybir.dt.float32
I32 = mybir.dt.int32
AX = mybir.AxisListType.X

P = 128
D = 1024
KC = D // P
SEQ = 512
SB, ST, NS = 8, 8, 64
TOK = SEQ + NS
NT = 5
PAST, PAGE, NPAGE, NPOOL = 2048, 128, 16, 160
ROWKEYS = 8
PAGEROWS = PAGE // ROWKEYS
H, DV, DQK = 8, 64, 32
HP = H // 2
NE, DE = 16, 512
FC = DE // P
EPS = 1e-6
LAM_INIT = 0.8 - 0.6 * math.exp(0.0)
BIG = 1e37
UNIT = 4096
MAIN = NE
OVER = (2 * TOK + (P - 1) * NE) // P - NE
NTILE = MAIN + OVER


COLS = (0, 64)


def differs(b, value):
    return not isinstance(b, int) or b != value


def rows(t):
    return P if t < 4 else NS


def constant_table():
    p = np.arange(P)[:, None]
    cols = {}
    cols["ident"] = np.eye(P)
    x = np.arange(512)[None, :] - 384
    cols["dist"] = np.where(p - x >= 0, p - x, BIG)
    t, h = p % ST, p // 16
    slope = 2.0 ** -(h + 1.0)
    r = np.arange(120)[None, :] - 56
    cols["own"] = np.where((r >= 0) & (r <= t), -slope * (t - r), -BIG)
    cols["tril"] = (np.arange(P)[None, :] <= p) * 1.0
    c64 = np.arange(NS)[None, :]
    cols["sameseq"] = (c64 // ST == p // ST) * 1.0
    cols["repeat"] = (c64 % ST == p) * 1.0
    cols["before"] = (p < np.arange(P)[None, :]) * 1.0
    cols["ones"] = np.ones((P, P))
    e = np.arange(NE)
    cols["earlier"] = np.broadcast_to((e[None, :] < e[:, None]).reshape(1, -1), (P, NE * NE)) * 1.0
    cols["desc"] = np.broadcast_to([4.0, 3.0, 2.0, 1.0], (P, 4))
    cols["mainbase"] = np.broadcast_to(128.0 * e[None, :], (P, NE))
    cols["index"] = np.broadcast_to(np.arange(OVER)[None, :] * 1.0, (P, OVER))
    cols["group"] = (p // 32 == np.arange(4)[None, :]) * 1.0
    cols["diag"] = ((p // ST) % 4 == np.arange(4)[None, :]) * 1.0
    row = (p // 16) * ST + t
    first = (p // ST) % 2 == 0
    cols["sel1"] = ((row == c64) & first) * 1.0
    cols["sel2"] = ((row == c64) & ~first) * 1.0
    cols["half"] = np.full((P, H), -0.5)
    cols["pagerow"] = p % PAGEROWS * 1.0
    at, parts = {}, []
    n = 0
    for name, a in cols.items():
        a = np.broadcast_to(a, (P, a.shape[1]))
        at[name] = (n, a.shape[1])
        n += a.shape[1]
        parts.append(a)
    past = -slope * (PAST + t - np.arange(PAST).reshape(2, P, ROWKEYS).transpose(0, 2, 1).reshape(1, PAST))
    return at, np.ascontiguousarray(np.concatenate(parts, 1).astype(np.float32)), \
        np.ascontiguousarray(past.astype(np.float32))


class Layout:

    RING, X, HT, MP = 0, 6 * UNIT, 6 * UNIT + 5120, 6 * UNIT + 9728
    QKT, V, MIX, CST = MP + 4096, MP + 8704, MP + 11264, MP + 16384

    def __init__(self, sb, ps, where, ncst):
        self.sb, self.ps, self.where = sb, ps, where
        self.small = self.CST + ncst
        self.ring = [sb[:, s * UNIT:(s + 1) * UNIT] for s in range(6)]
        self.hT = self.at(self.HT, KC * TOK).rearrange("p (k t) -> p k t", k=KC)
        self.qT = self.at(self.QKT, HP * TOK).rearrange("p (h t) -> p h t", h=HP)
        self.kT = self.at(self.QKT + HP * TOK, HP * TOK).rearrange("p (h t) -> p h t", h=HP)
        self.v = self.at(self.V, NT * 512).rearrange("p (t n) -> p t n", t=NT)
        self.mix = self.at(self.MIX, NT * D).rearrange("p (t n) -> p t n", t=NT)
        self.n_small = 0

    def at(self, off, n, p0=0, p1=P):
        return self.sb[p0:p1, off:off + n]

    def cst(self, name, p1=P):
        off, n = self.where[name]
        return self.at(self.CST + off, n, 0, p1)

    def take(self, n):
        off = self.small + self.n_small
        self.n_small += n
        return off


def chain(eng, sem, start=0):
    count = [start]

    def link(ins):
        count[0] += 1
        ins.then_inc(sem, 1)
        eng.wait_ge(sem, count[0])
    link.count = count
    return link


ADA = [[0, 1, 2, 3], [3, 4, 5, 0], [1, 2, 3, 4]]
WIN = [4, 5, 0, 1, 2]
WIN_ORDER = ["s", "u", "v", "k", "q"]
WIN_COL = {"q": 0, "k": 1, "v": 2, "u": 3, "s": 4}
K_SLOT = [[0, 1], [2, 3]]
V_SLOT = [4, 5]
W_OUT = [0, 1]
EXPERT = [[2, 3, 4], [5, 0, 1]]
STATIC = [("ada", 0, j, s) for j, s in enumerate(ADA[0])] + [("win", 0, c, s) for c, s in enumerate(WIN)] + \
         [("ada", r, j, s) for r in (1, 2) for j, s in enumerate(ADA[r])]


def fills(kind, r, j):
    n = STATIC.index(next(u for u in STATIC if u[:3] == (kind, r, j)))
    return sum(u[3] == STATIC[n][3] for u in STATIC[:n + 1])


STATIC_USES = [sum(u[3] == s for u in STATIC) for s in range(6)]


class Program:
    def __init__(self, nc, a, o, where, ncst, ctx):
        self.passing = []
        self.nc, self.a, self.o, self.ctx, self.ncst = nc, a, o, ctx, ncst
        sb = ctx.enter_context(nc.sbuf_tensor("sb", [P, Layout.CST + ncst + 528], F32))
        self.PS = ctx.enter_context(nc.psum_tensor("ps", [P, 8, 512], F32))
        self.L = Layout(sb, self.PS, where, ncst)
        L = self.L
        self.ints = ctx.enter_context(nc.sbuf_tensor("ints", [P, 96], I32))
        self.ck, self.cv = (a[n].rearrange("l n (j r) h d -> (l n j) (r h d)", r=ROWKEYS)
                            for n in ("cache_k", "cache_v"))
        self.ring_full = [self.lasting(f"ring_full{s}") for s in range(6)]
        self.pages_full = [self.lasting(f"pages_full{s}") for s in range(6)]
        self.cst_in = self.lasting("cst_in")
        self.table_in = self.lasting("table_in")
        self.apart = self.lasting("apart")
        self.ada_done, self.mod_sb, self.mod_out, self.pages_in = (
            self.lasting(n) for n in ("ada_done", "mod_sb", "mod_out", "pages_in"))
        self.staged = self.lasting("staged")
        self.mod = nc.dram_tensor("mod_rows", (NS + 1, 6 * D), F32).ap()
        self.h2 = nc.dram_tensor("h2_rows", (TOK, D), F32).ap()
        self.slot_token = nc.dram_tensor("slot_token", (NTILE * P, 1), I32).ap()
        self.y_rows = nc.dram_tensor("y_rows", (NTILE * P, D), F32).ap()
        self.o_sample = nc.dram_tensor("o_sample", (SB, NS, DV), F32).ap()
        self.cS = L.at(L.take(72), 72).rearrange("p (c k) -> p c k", c=9)
        self.rstd = L.at(L.take(NT), NT)
        self.ssq = L.at(L.take(NT), NT)
        self.bsT = L.at(L.take(H), H)
        self.bs8 = L.at(L.take(H), H, 0, NS)
        self.lam = L.at(L.take(136), 136)
        self.w_r = L.at(L.take(160), 160).rearrange("p (k n) -> p k n", k=KC)
        self.gsub = L.at(L.take(DV), DV)
        self.stats = L.at(L.take(48), 48)
        self.row_f = L.at(L.take(16), 16)
        self.b_r = self.stats[:, 24:44]
        self.logits = self.lam[:, 0:100].rearrange("p (t n) -> p t n", t=NT)
        self.weights = self.lam[:, 100:110].rearrange("p (t j) -> p t j", t=NT)
        self.x1 = L.at(L.X, NT * D).rearrange("p (t n) -> p t n", t=NT)

    def sem(self, name):
        self.passing.append(self.nc.alloc_semaphore(name=name))
        return self.passing[-1]

    def stand_apart(self, eng):
        eng.sem_inc(self.apart, 1)

    def lasting(self, name):
        return self.ctx.enter_context(self.nc.semaphore(name))

    def forget(self):
        self.nc.clear_and_free_semaphores(self.passing)
        self.nc.all_engine_barrier()
        self.passing = []

    def condition(self):
        nc, a, L, PS = self.nc, self.a, self.L, self.PS
        c_in, x_in, g_in, ws_in = (self.sem(n) for n in ("c_in", "x_in0", "g_in", "ws_in"))
        x_ins = [x_in, self.sem("x_in1")]
        silu_c, mod_in = self.sem("silu_c"), self.sem("mod_in")
        ssq_done, rstd_done, h_done, tr_done, ev_a, ev_d = (self.sem(n) for n in
                                                            ("ssq_done", "rstd_done", "h_done", "tr_done",
                                                             "evac_act", "evac_dve"))
        dchain, pchain = self.sem("dve_chain_a"), self.sem("pool_chain_a")
        ws_masked, ws_tr, wmT_done, w8_done = (self.sem(n) for n in ("ws_masked", "ws_tr", "wmT_done", "w8_done"))
        self.wmT = L.at(L.V, H * P).rearrange("p (g t) -> p g t", g=H)
        self.w8 = L.at(L.V + 1024, 512, 0, NS).rearrange("p (g b t) -> p g b t", g=H, b=SB)
        xb = [L.at(L.MIX + 1024 * i, D) for i in range(2)]
        hb = [L.at(L.MIX + 2048 + 1024 * i, D) for i in range(2)]
        mp = [L.at(L.MP + 1024 * i, D) for i in range(4)]
        gpre = L.at(L.QKT + 1024, D)
        self.bada = L.at(L.X + 2048, 3 * 512).rearrange("p (r n) -> p r n", r=3)
        self.modst = L.at(L.X + 2048 + 1536, 3 * 512).rearrange("p (r n) -> p r n", r=3)
        wsraw = L.at(L.QKT, H * P).rearrange("p (g s) -> p g s", g=H)
        x_of = [a["x_prompt"][0, t * P:(t + 1) * P, :] for t in range(4)] + \
            [a["x_sample"].rearrange("b t n -> (b t) n")]

        def evac(eng, t, half, done):
            n = rows(t)
            eng.wait_ge(tr_done, t + 1)
            src = PS[:, 2 * (t % 2) + half, :].rearrange("p (k t) -> p k t", k=4)[:, :, 0:n]
            dst = L.hT[:, 4 * half:4 * half + 4, t * P:t * P + n]
            if half == 0:
                eng.activation(dst, src, ACT.Copy).then_inc(done, 1)
            else:
                eng.tensor_copy(dst, src).then_inc(done, 1)

        with nc.Block() as block:
            @block.sync
            def _(sp):
                for u in STATIC[:6]:
                    self.load_unit(sp, u)
                sp.wait_ge(self.ada_done, 1)
                for u in STATIC[6:10]:
                    self.load_unit(sp, u)

            @block.gpsimd
            def _(pool):
                pool.dma_start(L.at(L.CST, self.ncst), a["constants"]).then_inc(self.cst_in, 16)
                pool.dma_start(gpre, a["g_pre_mix"].partition_broadcast(P)).then_inc(g_in, 16)
                for j in range(4):
                    src = a["b_ada"].rearrange("a (r j n) -> a j r n", r=3, j=4)[:, j]
                    for r in range(3):
                        pool.dma_start(self.bada[32 * j:32 * j + 9, r, :],
                                       src[0, r].partition_broadcast(9)).then_inc(g_in, 16)
                pool.dma_start(wsraw, a["sgu_ws"][0].rearrange("g t s -> t g s")).then_inc(ws_in, 16)
                for n, c0, c1 in (("rg", 0, 4), ("re", 4, 20)):
                    pool.dma_start(self.w_r[:, :, c0:c1], a["w_" + n][0].rearrange("(p k) n -> p k n", k=KC)
                                   ).then_inc(self.table_in, 16)
                    pool.dma_start(self.b_r[:, c0:c1], a["b_" + n].partition_broadcast(P)).then_inc(self.table_in, 16)
                with nc.allow_non_contiguous_dma(reason="8 x 128 bias values, once"):
                    pool.dma_start(self.bsT, a["sgu_bs"][0].rearrange("g t -> t g")).then_inc(ws_in, 16)
                link = chain(pool, pchain)
                link(pool.memset(self.ints[:, 0:NTILE], 0))
                pool.iota(self.ints[:, 24:24 + NT], pattern=[[P, NT]], base=0, channel_multiplier=1)
                pool.dma_start(self.slot_token.rearrange("(p e) o -> p (e o)", p=P),
                               self.ints[:, 0:NTILE]).then_inc(self.table_in, 16)
                pool.wait_ge(self.cst_in, 16)
                for t in range(NT):
                    n = rows(t)
                    pool.wait_ge(ssq_done, t + 1)
                    link(pool.tensor_scalar(self.rstd[0:n, t:t + 1], self.ssq[0:n, t:t + 1], 1.0 / D, EPS,
                                            ALU.mult, ALU.add))
                    pool.tensor_tensor(self.rstd[0:n, t:t + 1], self.rstd[0:n, t:t + 1],
                                       L.cst("half", n)[:, 0:1], ALU.pow).then_inc(rstd_done, 1)

            @block.scalar
            def _(act):
                act.dma_start(self.cS[:, 0, :], a["c_prompt"].rearrange("c (p k) -> p (c k)", k=KC)).then_inc(c_in, 16)
                act.dma_start(self.cS[:, 1:9, :], a["c_sample"].rearrange("c (p k) -> p c k", k=KC)).then_inc(c_in, 16)
                for t in range(2):
                    act.dma_start(xb[t], x_of[t]).then_inc(x_ins[t], 16)
                act.wait_ge(c_in, 32)
                act.activation(self.cS, self.cS, ACT.Silu).then_inc(silu_c, 1)
                for t in range(NT):
                    n = rows(t)
                    act.wait_ge(x_ins[t % 2], 16 * (t // 2 + 1))
                    if t >= 2:
                        act.wait_ge(tr_done, t - 1)
                    act.activation(hb[t % 2][0:n], xb[t % 2][0:n], ACT.Square,
                                   accum_out=self.ssq[0:n, t:t + 1]).then_inc(ssq_done, 1)
                    if t == 1:
                        self.mod_store(act, 0)
                        act.wait_ge(self.mod_out, 16 * 8)
                        act.dma_start(mp[0], self.mod[NS, D:2 * D].partition_broadcast(P)).then_inc(mod_in, 16)
                        act.dma_start(mp[1], self.mod[NS, 0:D].partition_broadcast(P)).then_inc(mod_in, 16)
                        act.dma_start(mp[2][0:NS], self.mod[0:NS, D:2 * D]).then_inc(mod_in, 16)
                        act.dma_start(mp[3][0:NS], self.mod[0:NS, 0:D]).then_inc(mod_in, 16)
                    if t >= 1:
                        evac(act, t - 1, 0, ev_a)
                    if t + 1 < NT and t >= 1:
                        act.wait_ge(h_done, t)
                        nn = rows(t + 1)
                        act.dma_start(xb[(t + 1) % 2][0:nn], x_of[t + 1]).then_inc(x_ins[(t + 1) % 2], 16)
                evac(act, NT - 1, 0, ev_a)

            @block.vector
            def _(dve):
                link = chain(dve, dchain)
                dve.wait_ge(self.cst_in, 16)
                dve.wait_ge(ws_in, 32)
                dve.tensor_tensor(wsraw, wsraw, L.cst("tril").unsqueeze(1).to_broadcast([P, H, P]),
                                  ALU.mult).then_inc(ws_masked, 1)
                dve.wait_ge(g_in, 16 * 13)
                self.mod_evac(dve, 0)
                dve.wait_ge(ws_tr, 1)
                dve.tensor_copy(self.wmT, PS[:, 4:6, :].rearrange("p b (g t) -> p (b g) t", g=4)).then_inc(wmT_done, 1)
                dve.wait_ge(w8_done, 1)
                dve.tensor_tensor(self.w8, PS[0:NS, 6, 0:64].rearrange("p (g t) -> p g t", g=H).unsqueeze(2)
                                  .to_broadcast([NS, H, SB, ST]),
                                  L.cst("sameseq", NS).rearrange("p (b t) -> p b t", b=SB).unsqueeze(1)
                                  .to_broadcast([NS, H, SB, ST]), ALU.mult)
                dve.tensor_copy(self.bs8, PS[0:NS, 6, 64:72])
                dve.wait_ge(mod_in, 64)
                dve.scalar_tensor_tensor(mp[2][0:NS], mp[2][0:NS], 1.0, gpre[0:NS], ALU.add, ALU.mult)
                link(dve.scalar_tensor_tensor(mp[0], mp[0], 1.0, gpre, ALU.add, ALU.mult))
                for t in range(NT):
                    n = rows(t)
                    A, sh = (mp[0], mp[1]) if t < 4 else (mp[2], mp[3])
                    dve.wait_ge(rstd_done, t + 1)
                    link(dve.scalar_tensor_tensor(hb[t % 2][0:n], xb[t % 2][0:n], self.rstd[0:n, t:t + 1], A[0:n],
                                                  ALU.mult, ALU.mult))
                    dve.tensor_tensor(hb[t % 2][0:n], hb[t % 2][0:n], sh[0:n], ALU.add).then_inc(h_done, 1)
                    if t >= 1:
                        evac(dve, t - 1, 1, ev_d)
                evac(dve, NT - 1, 1, ev_d)

            @block.tensor
            def _(pe):
                pe.wait_ge(silu_c, 1)
                self.ada_round(pe, 0)
                pe.wait_ge(self.cst_in, 16)
                pe.wait_ge(ws_masked, 1)
                for g in range(H):
                    last = pe.transpose(PS[:, 4 + g // 4, (g % 4) * P:(g % 4 + 1) * P], wsraw[:, g, :], L.cst("ident"))
                last.then_inc(ws_tr, 1)
                pe.wait_ge(wmT_done, 1)
                pe.matmul(PS[0:NS, 6, 0:64], L.cst("repeat", ST), self.wmT[0:ST, :, 0:ST], start=True, stop=True)
                pe.matmul(PS[0:NS, 6, 64:72], L.cst("repeat", ST), self.bsT[0:ST, :], start=True,
                          stop=True).then_inc(w8_done, 1)
                for t in range(NT):
                    n = rows(t)
                    pe.wait_ge(h_done, t + 1)
                    if t >= 2:
                        pe.wait_ge(ev_a, t - 1)
                        pe.wait_ge(ev_d, t - 1)
                    for k in range(KC):
                        last = pe.transpose(PS[:, 2 * (t % 2) + k // 4, (k % 4) * P:(k % 4) * P + n],
                                            hb[t % 2][0:n, k::KC], L.cst("ident", n)[:, 0:n])
                    last.then_inc(tr_done, 1)

    def load_unit(self, sp, unit):
        kind, r, j, slot = unit
        w = self.a["w_ada"] if kind == "ada" else self.a["w_in"]
        col = 512 * (4 * r + j) if kind == "ada" else 512 * WIN_COL[WIN_ORDER[j]]
        dst = self.L.ring[slot].rearrange("p (k n) -> p k n", k=KC)
        sp.dma_start(dst, w[0, :, col:col + 512].rearrange("(p k) n -> p k n", k=KC)).then_inc(self.ring_full[slot], 16)

    def ada_round(self, pe, r):
        bank = 7
        w = [self.L.ring[s].rearrange("p (k n) -> p k n", k=KC) for s in ADA[r]]
        for j, s in enumerate(ADA[r]):
            pe.wait_ge(self.ring_full[s], 16 * fills("ada", r, j))
        if r:
            pe.wait_ge(self.mod_sb, 4 * r)
        for k in range(KC):
            for j, s in enumerate(ADA[r]):
                ins = pe.matmul(self.PS[32 * j:32 * j + 9, bank, :], self.cS[:, :, k], w[j][:, k, :],
                                start=k == 0, stop=k == KC - 1)
        ins.then_inc(self.ada_done, 1)

    def mod_evac(self, dve, r):
        dve.wait_ge(self.ada_done, r + 1)
        for j in range(4):
            q = slice(32 * j, 32 * j + 9)
            dve.tensor_tensor(self.modst[q, r, :], self.PS[q, 7, :], self.bada[q, r, :], ALU.add).then_inc(self.mod_sb, 1)

    def mod_store(self, eng, r):
        eng.wait_ge(self.mod_sb, 4 * (r + 1))
        for j in range(4):
            col = slice(512 * (4 * r + j), 512 * (4 * r + j + 1))
            eng.dma_start(self.mod[NS:NS + 1, col], self.modst[32 * j:32 * j + 1, r, :]).then_inc(self.mod_out, 16)
            eng.dma_start(self.mod[0:NS, col].rearrange("(b t) n -> b t n", t=ST),
                          self.modst[32 * j + 1:32 * j + 9, r, :].unsqueeze(1).to_broadcast([SB, ST, 512])
                          ).then_inc(self.mod_out, 16)



    def project(self):
        nc, a, o, L, PS = self.nc, self.a, self.o, self.L, self.PS
        grp_done, evac_done, post_done, post_ev = (self.sem(n) for n in ("grp_done", "evac_done", "post_done",
                                                                         "post_evac"))
        bn_done, rs_done, vs_ready, u_done, k_out, v_out, vs_out, ln_in = (
            self.sem(n) for n in ("bn_done", "rs_done", "vs_ready", "u_done", "k_out", "v_out", "vs_out", "ln_in"))
        dchain, pchain = self.sem("dve_chain_b"), self.sem("pool_chain_b")
        self.grp_done = grp_done
        k_outs = [k_out] + [self.sem(f"k_out{i}") for i in range(1, 4)]
        E = [L.at(L.X + 512 * i, 512) for i in range(4)]
        lng, lnb = L.at(L.MP, 512), L.at(L.MP + 512, 512)
        groups = [(c, t) for c in WIN_ORDER for t in range(NT)]
        posts = [n for n, (c, t) in enumerate(groups) if c in "skq"]
        mv = self.stats[:, 8:10]
        k_o = [o["k_prompt"][0, 0, t * P:(t + 1) * P].rearrange("t h d -> t (h d)") for t in range(4)] + \
            [o["k_sample"][0].rearrange("b t h d -> (b t) (h d)")]
        v_o = [o["v_prompt"][0, 0, t * P:(t + 1) * P].rearrange("t h d -> t (h d)") for t in range(4)] + \
            [o["v_sample"][0].rearrange("b t h d -> (b t) (h d)")]

        def posts_to(n):
            return sum(m <= n for m in posts)

        with nc.Block() as block:
            @block.sync
            def _(sp):
                for u in STATIC[10:]:
                    before = [x for x in STATIC[:STATIC.index(u)] if x[3] == u[3]][-1]
                    if before[0] == "win":
                        sp.wait_ge(grp_done, NT * (before[2] + 1))
                    else:
                        sp.wait_ge(self.ada_done, before[1] + 1)
                    self.load_unit(sp, u)

            @block.gpsimd
            def _(pool):
                link = chain(pool, pchain)
                with nc.allow_non_contiguous_dma(reason="128 page numbers, once"):
                    for g in range(NPAGE // 2):
                        pool.dma_start(self.ints[PAGEROWS * g:PAGEROWS * (g + 1), 64:80],
                                       a["page_table"].rearrange("b (h g) -> g (b h)", h=2)[g].partition_broadcast(
                                           PAGEROWS)).then_inc(self.pages_in, 16)
                pool.dma_start(lng, a["sgu_ln_g"].partition_broadcast(P)).then_inc(ln_in, 16)
                pool.dma_start(lnb, a["sgu_ln_b"].partition_broadcast(P)).then_inc(ln_in, 16)
                for t in range(NT):
                    n = rows(t)
                    pool.wait_ge(bn_done, t + 1)
                    link(pool.tensor_scalar(self.stats[0:n, 10:11], self.stats[0:n, 9:10], 1.0, EPS, ALU.mult, ALU.add))
                    pool.tensor_tensor(self.stats[0:n, 11:12], self.stats[0:n, 10:11], L.cst("half", n)[:, 0:1],
                                       ALU.pow).then_inc(rs_done, 1)
                pool.wait_ge(vs_ready, 4)
                pool.dma_start(o["sgu_prompt"][0, 0], E[3]).then_inc(vs_out, 16)
                pool.wait_ge(vs_ready, 5)
                pool.dma_start(o["sgu_sample"][0].rearrange("b t n -> (b t) n"), E[0][0:NS]).then_inc(vs_out, 16)

            @block.scalar
            def _(act):
                for n, (c, t) in enumerate(groups):
                    r = rows(t)
                    act.wait_ge(grp_done, n + 1)
                    src = PS[0:r, n % 4, :]
                    if n >= 4:
                        cb, tb = groups[n - 4]
                        if cb in "skq":
                            act.wait_ge(post_done, posts_to(n - 4))
                        if cb == "s" and tb >= 3:
                            act.wait_ge(vs_out, 32)
                        if cb == "u":
                            act.wait_ge(u_done, tb + 1)
                        if cb == "k":
                            act.wait_ge(k_outs[n % 4], 16 * sum(groups[m][0] == "k" for m in range(n % 4, n, 4)))
                    if c in "su":
                        act.activation(E[n % 4][0:r], src, ACT.Gelu_apprx_tanh).then_inc(evac_done, 1)
                    elif c == "v":
                        if t == 0:
                            act.wait_ge(post_done, NT)
                        act.activation(L.v[0:r, t, :], src, ACT.Copy).then_inc(evac_done, 1)
                        act.wait_ge(evac_done, n + 1)
                        act.dma_start(v_o[t], L.v[0:r, t, :]).then_inc(v_out, 16)
                    else:
                        act.activation(E[n % 4][0:r], src, ACT.Copy,
                                       scale=DQK ** -0.5 if c == "q" else 1.0).then_inc(evac_done, 1)
                        if c == "k":
                            act.wait_ge(evac_done, n + 1)
                            act.dma_start(k_o[t], E[n % 4][0:r]).then_inc(k_outs[n % 4], 16)
                for r in (1, 2):
                    self.mod_store(act, r)
                act.wait_ge(self.mod_out, 16 * 24)
                act.wait_ge(v_out, 16 * NT)
                for i in range(4):
                    act.wait_ge(k_outs[i], 16 * sum(c == "k" and m % 4 == i for m, (c, _) in enumerate(groups)))

            @block.vector
            def _(dve):
                link = chain(dve, dchain)

                def post(m):
                    c, t = groups[m]
                    r, i = rows(t), posts_to(m) - 1
                    dve.wait_ge(post_done, i + 1)
                    bank = PS[:, 4 + i % 2, :]
                    if c == "s":
                        bias = self.bsT if t < 4 else self.bs8
                        dve.tensor_tensor(L.mix[0:r, t, 512:].rearrange("p (g n) -> p g n", g=H),
                                          bank[0:r].rearrange("p (g n) -> p g n", g=H),
                                          bias[0:r].unsqueeze(2).to_broadcast([r, H, 64]), ALU.add).then_inc(post_ev, 1)
                    else:
                        dst = L.kT if c == "k" else L.qT
                        dve.tensor_copy(dst[:, :, t * P:t * P + r],
                                        bank.rearrange("p (h t) -> p h t", h=HP)[:, :, 0:r]).then_inc(post_ev, 1)

                dve.wait_ge(self.pages_in, 16 * NPAGE // 2)
                link(dve.tensor_copy(self.row_f, self.ints[:, 64:80]))
                link(dve.scalar_tensor_tensor(self.row_f, self.row_f, float(PAGEROWS),
                                              L.cst("pagerow").to_broadcast([P, 16]), ALU.mult, ALU.add))
                link(dve.tensor_copy(self.ints[:, 64:80], self.row_f))
                dve.wait_ge(ln_in, 32)
                for n, (c, t) in enumerate(groups):
                    r = rows(t)
                    e = E[n % 4][0:r]
                    if c == "s":
                        dve.wait_ge(evac_done, n + 1)
                        link(dve.bn_stats(self.stats[0:r, 0:6], e))
                        dve.bn_aggr(mv[0:r], self.stats[0:r, 0:6]).then_inc(bn_done, 1)
                        dve.wait_ge(rs_done, t + 1)
                        link(dve.tensor_scalar(e, e, mv[0:r, 0:1], self.stats[0:r, 11:12], ALU.subtract, ALU.mult))
                        link(dve.tensor_tensor(e, e, lng[0:r], ALU.mult))
                        dve.tensor_tensor(e, e, lnb[0:r], ALU.add).then_inc(vs_ready, 1)
                    elif c == "u":
                        if t == 0:
                            post(n - 1)
                            dve.wait_ge(post_ev, NT)
                        dve.wait_ge(evac_done, n + 1)
                        dve.tensor_tensor(L.mix[0:r, t, 512:], e, L.mix[0:r, t, 512:], ALU.mult).then_inc(u_done, 1)
                    if n - 1 in posts and not (c == "u" and t == 0):
                        post(n - 1)
                post(len(groups) - 1)
                for r in (1, 2):
                    self.mod_evac(dve, r)

            @block.tensor
            def _(pe):
                def post(m):
                    c, t = groups[m]
                    r, i = rows(t), posts_to(m) - 1
                    if i >= 2:
                        pe.wait_ge(post_ev, i - 1)
                    bank = PS[:, 4 + i % 2, :]
                    if c == "s":
                        pe.wait_ge(vs_ready, t + 1)
                        for g in range(H):
                            w = self.wmT[:, g, :] if t < 4 else self.w8[:, g, :, :]
                            w = w.rearrange("p b t -> p (b t)") if t == 4 else w
                            for c in COLS[:-(-r // 64)]:
                                last = pe.matmul(bank[c:c + 64, 64 * g:64 * g + 64], w[:, c:c + 64],
                                                 E[m % 4][0:r, 64 * g:64 * g + 64], start=True, stop=True)
                    else:
                        pe.wait_ge(evac_done, m + 1)
                        for h in range(HP):
                            last = pe.transpose(bank[:, P * h:P * h + r], E[m % 4][0:r, P * h:P * h + P],
                                                L.cst("ident", r)[:, 0:r])
                    last.then_inc(post_done, 1)

                for n, (c, t) in enumerate(groups):
                    r = rows(t)
                    slot = WIN[n // NT]
                    if t == 0:
                        pe.wait_ge(self.ring_full[slot], 16 * fills("win", 0, n // NT))
                    if n >= 4:
                        pe.wait_ge(evac_done, n - 3)
                    w = L.ring[slot].rearrange("p (k n) -> p k n", k=KC)
                    for k in range(KC):
                        last = pe.matmul(PS[0:r, n % 4, :], L.hT[:, k, t * P:t * P + r], w[:, k, :],
                                         start=k == 0, stop=k == KC - 1)
                    last.then_inc(grp_done, 1)
                    if n - 1 in posts:
                        post(n - 1)
                post(len(groups) - 1)
                for r in (1, 2):
                    self.ada_round(pe, r)


    def load_pages(self, pool, cache, b, half, slot, k):
        index = self.ints[:, 80 + slot:81 + slot]
        pool.tensor_copy(index, self.ints[:, bass.ds(64 + 2 * b + half, 1)]).then_inc(self.staged, 1)
        pool.wait_ge(self.staged, k + 1)
        self.stand_apart(pool)
        pool.indirect_dma_start(self.L.ring[slot], None, cache,
                                bass.IndirectOffsetOnAxis(ap=index, axis=0)).then_inc(self.pages_full[slot], 16)

    def head_norm(self, dve, link, o, sq, ss, dst, r, need, give, k):
        heads = o.rearrange("p (h d) -> p h d", h=H)
        link(dve.tensor_tensor(sq, o, o, ALU.mult))
        dve.tensor_reduce(ss[0:r], sq.rearrange("p (h d) -> p h d", h=H), AX, ALU.add).then_inc(need, 1)
        dve.wait_ge(give, k)
        link(dve.tensor_tensor(heads, heads, ss[0:r].unsqueeze(2).to_broadcast([r, H, DV]), ALU.mult))
        dve.tensor_tensor(dst.rearrange("p (h d) -> p h d", h=H), heads,
                          self.gsub[0:r].unsqueeze(1).to_broadcast([r, H, DV]), ALU.mult)

    def power(self, pool, link, ss, n, r, scale, done):
        link(pool.tensor_scalar(ss[0:r], ss[0:r], scale, EPS, ALU.mult, ALU.add))
        pool.tensor_tensor(ss[0:r], ss[0:r], self.L.cst("half", r)[:, 0:n], ALU.pow).then_inc(done, 1)

    def attend_prompt(self):
        nc, a, L, PS = self.nc, self.a, self.L, self.PS
        (s_done, s_read, m_ready, exp_done, a_ready, t_done, at_done, pv_done, o_read, lam_in, lam_sum, lam_exp,
         lam_ready, ss_ready, ss_power) = (self.sem("c_" + n) for n in (
             "scores", "scores_read", "max", "exp", "weights", "transposed", "evacuated", "pv", "o_read", "lam_in",
             "lam_sum", "lam_exp", "lam_ready", "ss_ready", "ss_power"))
        dchain, pchain, zeroed = self.sem("dve_chain_c"), self.sem("pool_chain_c"), self.sem("c_zeroed")
        n0 = L.X
        bias = L.at(n0, 4096).rearrange("p (h n) -> p h n", h=H)
        pb = [[L.at(n0 + 4096 + 1024 * i + 512 * j, 512) for j in range(2)] for i in range(3)]
        at = [L.at(n0 + 7168 + 512 * i, 512).rearrange("p (b q) -> p b q", b=4) for i in range(2)]
        osb, sq = L.at(n0 + 8192, 512), L.at(n0 + 8704, 512)
        ss = self.stats[:, 16:24]
        mx, nm, sums, cf, r1 = (L.at(n0 + 9216 + 64 * i, 64) for i in range(5))
        qz = [L.at(n0 + 9536 + 2048 * i, 2048).rearrange("p (h g q) -> p h g q", h=HP, g=4) for i in range(2)]
        q_zero = self.sem("c_q_zero")
        lam = self.lam
        work = [(i, h) for i in range(4) for h in range(H)]
        N = len(work)

        with nc.Block() as block:
            @block.gpsimd
            def _(pool):
                link = chain(pool, pchain)
                for k, (cache, b, slots) in enumerate(((self.ck, 0, K_SLOT[0]), (self.ck, 1, K_SLOT[1]),
                                                       (self.cv, 0, V_SLOT))):
                    for half in range(2):
                        self.load_pages(pool, cache, b, half, slots[half], 2 * k + half)
                link(pool.memset(L.mix[:, 4, 0:512], 0.0))
                pool.dma_start(self.y_rows[MAIN * P:].rearrange("(p r) (c n) -> p (r c) n", p=P, n=512),
                               L.mix[:, 4:5, 0:512].to_broadcast([P, 2 * OVER, 512])).then_inc(zeroed, 16)
                for i in range(4):
                    pool.wait_ge(ss_ready, i + 1)
                    self.power(pool, link, ss, H, P, 1.0 / DV, ss_power)
                pool.wait_ge(zeroed, 16)

            @block.scalar
            def _(act):
                for i, n in enumerate(("lam_q1", "lam_k1", "lam_q2", "lam_k2")):
                    act.dma_start(lam[:, 32 * i:32 * i + 32], a[n].partition_broadcast(P)).then_inc(lam_in, 16)
                act.dma_start(self.gsub, a["g_subln"].partition_broadcast(P)).then_inc(lam_in, 16)

                def place_q(i):
                    if i >= 2:
                        act.wait_ge(s_done, 2 * H * (i - 1))
                    for g in range(4):
                        act.activation(qz[i % 2][:, :, g, :], L.qT[:, :, P * i:P * i + P], ACT.Copy,
                                       scale=L.cst("group")[:, g:g + 1]).then_inc(q_zero, 1)

                place_q(0)
                act.wait_ge(lam_sum, 1)
                act.activation(lam[:, 130:132], lam[:, 128:130], ACT.Exp).then_inc(lam_exp, 1)
                for n in range(N + 2):
                    if n < N:
                        act.wait_ge(m_ready, n + 1)
                        w = P * (work[n][0] + 1)
                        for j in range(2):
                            q = 2 * n + j
                            act.activation(pb[n % 3][j][:, 0:w], pb[n % 3][j][:, 0:w], ACT.Exp, bias=nm[:, q:q + 1],
                                           accum_out=sums[:, q:q + 1]).then_inc(exp_done, 1)
                    if n % H == 3 and n // H < 3:
                        place_q(n // H + 1)
                    if n >= 2:
                        m = n - 2
                        i, h = work[m]
                        act.wait_ge(t_done, m + 1)
                        if m >= 2:
                            act.wait_ge(pv_done, m - 1)
                        act.activation(at[m % 2][:, 0:i + 1, :],
                                       PS[:, 4 + m % 2, 0:P * (i + 1)].rearrange("p (b q) -> p b q", q=P),
                                       ACT.Copy).then_inc(at_done, 1)

            @block.vector
            def _(dve):
                link = chain(dve, dchain)
                for h in range(H):
                    last = dve.tensor_scalar_mul(bias[:, h, :], L.cst("dist"), -2.0 ** -(h + 1))
                link(last)
                dve.wait_ge(lam_in, 80)
                for j in range(2):
                    last = dve.tensor_tensor_reduce(out=sq[:, 32 * j:32 * j + 32], in0=lam[:, 64 * j:64 * j + 32],
                                                    in1=lam[:, 64 * j + 32:64 * j + 64], scale=1.0, scalar=0.0,
                                                    op0=ALU.mult, op1=ALU.add, accum_out=lam[:, 128 + j:129 + j])
                last.then_inc(lam_sum, 1)
                link(dve.tensor_scalar_mul(self.gsub, self.gsub, 1.0 - LAM_INIT))
                dve.wait_ge(lam_exp, 1)
                link(dve.tensor_tensor(lam[:, 132:133], lam[:, 130:131], lam[:, 131:132], ALU.subtract))
                link(dve.tensor_scalar(lam[:, 133:134], lam[:, 132:133], -1.0, -LAM_INIT, ALU.mult, ALU.add))

                def weights(m):
                    w, q = P * (work[m][0] + 1), 2 * m
                    p1, p2 = pb[m % 3][0][:, 0:w], pb[m % 3][1][:, 0:w]
                    dve.wait_ge(exp_done, 2 * m + 2)
                    link(dve.reciprocal(cf[:, q:q + 1], sums[:, q + 1:q + 2]))
                    link(dve.scalar_tensor_tensor(cf[:, q:q + 1], sums[:, q:q + 1], lam[:, 133:134], cf[:, q:q + 1],
                                                  ALU.mult, ALU.mult))
                    dve.scalar_tensor_tensor(p1, p2, cf[:, q:q + 1], p1, ALU.mult, ALU.add).then_inc(a_ready, 1)

                def finish(i):
                    dve.wait_ge(pv_done, H * (i + 1))
                    l1 = sums[:, 16 * i:16 * i + 16].rearrange("p (h j) -> p h j", j=2)[:, :, 0]
                    link(dve.reciprocal(r1[:, 0:H], l1))
                    dve.tensor_tensor(osb.rearrange("p (h d) -> p h d", h=H),
                                      PS[:, 6 + i % 2, :].rearrange("p (h d) -> p h d", h=H),
                                      r1[:, 0:H].unsqueeze(2).to_broadcast([P, H, DV]), ALU.mult).then_inc(o_read, 1)
                    dve.wait_ge(o_read, i + 1)
                    self.head_norm(dve, link, osb, sq, ss, L.mix[:, i, 0:512], P, ss_ready, ss_power, i + 1)

                for n in range(N + 1):
                    if n < N:
                        i, h = work[n]
                        w, q = P * (i + 1), 2 * n
                        if n >= 3:
                            dve.wait_ge(t_done, n - 2)
                        for j in range(2):
                            dve.wait_ge(s_done, 2 * n + j + 1)
                            dve.tensor_tensor_reduce(out=pb[n % 3][j][:, 0:w], in0=PS[:, 2 * (n % 2) + j, 0:w],
                                                     in1=bias[:, h, 384 - P * i:512], scale=1.0, scalar=-3e38,
                                                     op0=ALU.add, op1=ALU.max,
                                                     accum_out=mx[:, q + j:q + j + 1]).then_inc(s_read, 1)
                        dve.wait_ge(s_read, 2 * n + 2)
                        dve.tensor_scalar_mul(nm[:, q:q + 2], mx[:, q:q + 2], -1.0).then_inc(m_ready, 1)
                    if n >= 1:
                        weights(n - 1)
                    if n % H == 4 and n // H >= 1:
                        finish(n // H - 1)
                finish(3)

            @block.tensor
            def _(pe):
                for n in range(N + 3):
                    if n < N:
                        i, h = work[n]
                        if n >= 2:
                            pe.wait_ge(s_read, 2 * (n - 1))
                        if h == 0:
                            pe.wait_ge(q_zero, 4 * (i + 1))
                        for j in range(2):
                            pe.matmul(PS[:, 2 * (n % 2) + j, 0:P * (i + 1)], qz[i % 2][:, h // 2, 2 * (h % 2) + j, :],
                                      L.kT[:, h // 2, 0:P * (i + 1)], start=True, stop=True).then_inc(s_done, 1)
                    if 2 <= n < N + 2:
                        m = n - 2
                        pe.wait_ge(a_ready, m + 1)
                        if m >= 2:
                            pe.wait_ge(at_done, m - 1)
                        for b in range(work[m][0] + 1):
                            last = pe.transpose(PS[:, 4 + m % 2, P * b:P * b + P], pb[m % 3][0][:, P * b:P * b + P],
                                                L.cst("ident"))
                        last.then_inc(t_done, 1)
                    if n >= 3:
                        m = n - 3
                        i, h = work[m]
                        pe.wait_ge(at_done, m + 1)
                        if h == 0 and i >= 2:
                            pe.wait_ge(o_read, i - 1)
                        for c in COLS:
                            for b in range(i + 1):
                                last = pe.matmul(PS[c:c + 64, 6 + i % 2, DV * h:DV * h + DV],
                                                 at[m % 2][:, b, c:c + 64],
                                                 L.v[:, b, DV * h:DV * h + DV], start=b == 0, stop=b == i)
                        last.then_inc(pv_done, 1)

    def attend_sample(self):
        nc, a, L, PS = self.nc, self.a, self.L, self.PS
        names = ("k_tr", "kt_act", "kt_dve", "scores", "s_read", "q_st", "max", "exp", "coef", "pt", "at_act",
                 "at_dve", "pv", "o_hi", "o_lo", "o_ready", "past_in")
        (k_tr, kt_act, kt_dve, s_done, s_read, q_st, m_ready, exp_done, c_ready, pt_done, at_act, at_dve, pv_done,
         o_hi, o_lo, o_ready, past_in) = (self.sem("d_" + n) for n in names)
        o_out = [self.sem("d_o_out0"), self.sem("d_o_out1")]
        dchain, own_st, rs_done, o_own = (self.sem("d_" + n) for n in ("setup", "own_st", "reciprocal", "o_own"))
        n0 = L.X
        past = L.at(n0, PAST)
        S = [L.at(n0 + 2048 + 2112 * i, 2112) for i in range(2)]
        kt = [L.at(n0 + 6272 + 2048 * i, 2048).rearrange("p (h n) -> p h n", h=HP) for i in range(2)]
        at = L.at(n0 + 10368, 17 * NS).rearrange("p (g n) -> p g n", g=17)
        osb = L.at(n0 + 11456, 256, 0, NS)
        osum = L.at(n0 + 11712, 256, 0, NS).rearrange("p (g d) -> p g d", g=4)
        om = [L.at(n0 + 11968 + DV * i, DV, 0, NS) for i in range(2)]
        coef = [L.at(n0 + 12096 + NS * i, NS) for i in range(2)]
        base = L.at(n0 + 12224, NS)
        qst = [L.at(n0 + 12288 + P * i, P).rearrange("p (h n) -> p h n", h=HP) for i in range(2)]
        own = L.at(n0 + 12544, NS)
        qbd = L.at(n0 + 12608, SB * P).rearrange("p (b h g t) -> p b h g t", b=SB, h=HP, g=4)
        mx, nm, sums, rs = self.stats[:, 0:5], self.stats[:, 8:10], self.stats[:, 10:12], self.stats[:, 12:14]

        with nc.Block() as block:
            def looped(eng, step):
                step(0, 0, True, False)
                step(1, 1, True, True)
                step(2, 0, True, True)
                with eng.Fori(0, SB // 2 - 2) as i:
                    step(2 * i + 3, 1, True, True)
                    step(2 * i + 4, 0, True, True)
                step(SB - 1, 1, True, True)
                step(SB, 0, False, True)

            @block.sync
            def _(sp):
                sp.wait_ge(k_tr, 16 * (SB - 1))
                for c in range(2):
                    sp.dma_start(L.ring[W_OUT[c]].rearrange("p (k n) -> p k n", k=KC),
                                 a["w_out"][0, :, 512 * c:512 * c + 512].rearrange("(p k) n -> p k n", k=KC)
                                 ).then_inc(self.ring_full[W_OUT[c]], 16)
                sp.wait_ge(k_tr, 16 * SB)
                self.load_expert(sp, 0, 0, 0)
                self.load_expert(sp, 0, 0, 1)

            @block.gpsimd
            def _(pool):
                def refill(b, par, k, count):
                    if k:
                        for half in range(2):
                            pool.wait_ge(k_tr, 16 * b + 8 * half + 8)
                            self.load_pages(pool, self.ck, b + 2, half, K_SLOT[par][half], count + half)
                    if differs(b, 0):
                        for half in range(2):
                            if half == 0:
                                pool.wait_ge(pv_done, b)
                            if differs(b, SB):
                                self.load_pages(pool, self.cv, b, half, V_SLOT[half], count + (2 if k else 0) + half)
                        pool.wait_ge(o_ready, b)
                        self.stand_apart(pool)
                        pool.dma_start(self.o_sample[bass.ds(b - 1, 1)].rearrange("a r d -> r (a d)"),
                                       om[1 - par]).then_inc(o_out[1 - par], 16)

                refill(0, 0, True, 6)
                with pool.Fori(0, 2) as i:
                    refill(2 * i + 1, 1, True, 8 * i + 8)
                    refill(2 * i + 2, 0, True, 8 * i + 12)
                refill(5, 1, True, 24)
                refill(6, 0, False, 28)
                refill(7, 1, False, 30)
                refill(8, 0, False, 32)
                pool.wait_ge(o_out[0], 16 * 4)
                pool.wait_ge(o_out[1], 16 * 4)

            @block.scalar
            def _(act):
                act.dma_start(past, a["past_bias"]).then_inc(past_in, 16)

                def evac(b, ch):
                    for h in range(2):
                        act.wait_ge(k_tr, 16 * b + 4 * ch + h + 1)
                        if ch >= 2:
                            act.wait_ge(s_done, 5 * b + ch - 1)
                        elif differs(b, 0):
                            act.wait_ge(s_done, 5 * b - 2 + ch)
                        act.activation(kt[ch % 2][:, h, :], PS[:, h, :], ACT.Copy).then_inc(kt_act, 1)

                def step(b, par, keys, vals):
                    f = b - 1
                    if keys:
                        evac(b, 0)
                        evac(b, 1)
                        evac(b, 2)
                    if vals:
                        act.wait_ge(pt_done, 3 * f + 1)
                        if differs(f, 0):
                            act.wait_ge(pv_done, f)
                        act.activation(at[:, 0:8, :], PS[:, 6, :].rearrange("p (g n) -> p g n", g=8),
                                       ACT.Copy).then_inc(at_act, 1)
                    if keys:
                        evac(b, 3)
                    if vals:
                        act.wait_ge(pt_done, 3 * f + 3)
                        act.activation(at[0:NS, 16, :], PS[0:NS, 6, 0:NS], ACT.Copy).then_inc(at_act, 1)
                        act.wait_ge(pv_done, f + 1)
                        act.activation(osb, PS[NS:P, 7, 0:256], ACT.Copy).then_inc(o_hi, 1)
                    if keys:
                        act.wait_ge(m_ready, b + 1)
                        act.activation(S[par], S[par], ACT.Exp, bias=nm[:, par:par + 1],
                                       accum_out=sums[:, par:par + 1]).then_inc(exp_done, 1)
                looped(act, step)

            @block.vector
            def _(dve):
                for h in range(HP):
                    last = dve.tensor_tensor(qbd[:, :, h, :, :],
                                             L.qT[:, h, SEQ:TOK].rearrange("p (b t) -> p b t", b=SB).unsqueeze(2)
                                             .to_broadcast([P, SB, 4, ST]),
                                             L.cst("group").unsqueeze(1).unsqueeze(3).to_broadcast([P, SB, 4, ST]),
                                             ALU.mult)
                last = dve.scalar_tensor_tensor(base, L.cst("sel2"), self.lam[:, 133:134], L.cst("sel1"),
                                                ALU.mult, ALU.add)
                last.then_inc(dchain, 1)
                dve.wait_ge(dchain, 1)

                def evac(b, ch):
                    for h in (2, 3):
                        dve.wait_ge(k_tr, 16 * b + 4 * ch + h + 1)
                        if ch >= 2:
                            dve.wait_ge(s_done, 5 * b + ch - 1)
                        elif differs(b, 0):
                            dve.wait_ge(s_done, 5 * b - 2 + ch)
                        dve.tensor_copy(kt[ch % 2][:, h, :], PS[:, h, :]).then_inc(kt_dve, 1)

                def bias_max(b, ch, par):
                    n = 512 if ch < 4 else NS
                    dve.wait_ge(s_done, 5 * b + ch + 1)
                    self.stand_apart(dve)
                    dve.tensor_tensor_reduce(out=S[par][:, 512 * ch:512 * ch + n],
                                             in0=PS[:, 4 + (par + ch) % 2, 0:n],
                                             in1=past[:, 512 * ch:512 * ch + n] if ch < 4 else own,
                                             scale=1.0, scalar=-3e38, op0=ALU.add, op1=ALU.max,
                                             accum_out=mx[:, ch:ch + 1]).then_inc(s_read, 1)

                dve.wait_ge(past_in, 16)

                def step(b, par, keys, vals):
                    f = b - 1
                    if keys:
                        if differs(b, 0) and differs(b, 1):
                            dve.wait_ge(s_done, 5 * b - 5)
                        dve.tensor_copy(qst[par], qbd[:, bass.ds(b, 1)].rearrange("p b h g t -> p (b h) (g t)")
                                        ).then_inc(q_st, 1)
                        if differs(b, 0):
                            dve.wait_ge(s_read, 5 * b)
                        dve.tensor_copy(own, L.cst("own")[:, bass.ds(56 - ST * b, NS)]).then_inc(own_st, 1)
                    if vals:
                        dve.wait_ge(exp_done, f + 1)
                        dve.reciprocal(rs[:, 1 - par:2 - par], sums[:, 1 - par:2 - par]).then_inc(rs_done, 1)
                        dve.wait_ge(rs_done, f + 1)
                        if differs(f, 0) and differs(f, 1):
                            dve.wait_ge(pt_done, 3 * (f - 1))
                        dve.tensor_scalar_mul(coef[1 - par], base, rs[:, 1 - par:2 - par]).then_inc(c_ready, 1)
                    if keys:
                        evac(b, 0)
                        evac(b, 1)
                        if not isinstance(b, int) or b >= 2:
                            dve.wait_ge(pt_done, 3 * (b - 1))
                        bias_max(b, 0, par)
                        evac(b, 2)
                        bias_max(b, 1, par)
                        evac(b, 3)
                        bias_max(b, 2, par)
                    if vals:
                        dve.wait_ge(pt_done, 3 * f + 2)
                        if differs(f, 0):
                            dve.wait_ge(pv_done, f)
                        dve.tensor_copy(at[:, 8:16, :], PS[:, 6, :].rearrange("p (g n) -> p g n", g=8)
                                        ).then_inc(at_dve, 1)
                    if keys:
                        bias_max(b, 3, par)
                        dve.wait_ge(own_st, b + 1)
                        bias_max(b, 4, par)
                        dve.wait_ge(s_read, 5 * b + 5)
                        dve.tensor_reduce(nm[:, par:par + 1], mx, AX, ALU.max, negate=True).then_inc(m_ready, 1)
                    if vals:
                        dve.wait_ge(o_hi, f + 1)
                        dve.wait_ge(pv_done, f + 1)
                        dve.tensor_tensor(osum.rearrange("p g d -> p (g d)"), PS[0:NS, 7, 0:256], osb,
                                          ALU.add).then_inc(o_lo, 1)
                        dve.wait_ge(o_lo, f + 1)
                        dve.tensor_tensor(osum, osum, L.cst("diag", NS).unsqueeze(2).to_broadcast([NS, 4, DV]),
                                          ALU.mult).then_inc(o_own, 1)
                        dve.wait_ge(o_own, f + 1)
                        if not isinstance(f, int) or f >= 2:
                            dve.wait_ge(o_out[1 - par], 8 * (f - (1 - par)))
                        dve.tensor_reduce(om[1 - par], osum.rearrange("p g d -> p d g"), AX, ALU.add
                                          ).then_inc(o_ready, 1)
                looped(dve, step)

            @block.tensor
            def _(pe):
                def transposes(b, ch, par):
                    slot = K_SLOT[par][ch // 2]
                    if ch % 2 == 0:
                        pe.wait_ge(self.pages_full[slot], 16 + 8 * (b - par))
                    kp = L.ring[slot].rearrange("p (g n) -> p g n", g=NPAGE // 2)
                    for h in range(HP):
                        done = kt_act if h < 2 else kt_dve
                        if ch or differs(b, 0):
                            pe.wait_ge(done, 2 * (4 * b + ch) - 1 + h % 2)
                        for g in range(4):
                            last = pe.transpose(PS[:, h, P * g:P * g + P], kp[:, 4 * (ch % 2) + g, P * h:P * h + P],
                                                L.cst("ident"))
                        last.then_inc(k_tr, 1)

                def scores(b, ch, par):
                    bank = PS[:, 4 + (par + ch) % 2, :]
                    if ch < 4:
                        pe.wait_ge(kt_act, 2 * (4 * b + ch + 1))
                        pe.wait_ge(kt_dve, 2 * (4 * b + ch + 1))
                    if ch >= 2 or differs(b, 0):
                        pe.wait_ge(s_read, 5 * b + ch - 1)
                    for h in range(HP):
                        rhs = kt[ch % 2][:, h, :] if ch < 4 else L.kT[:, h, SEQ:TOK]
                        last = pe.matmul(bank[32 * h:32 * h + 32, 0:512 if ch < 4 else NS], qst[par][:, h, :], rhs,
                                         start=True, stop=True)
                    last.then_inc(s_done, 1)

                def weights(f, part, par):
                    if part:
                        pe.wait_ge(at_act if part == 1 else at_dve, 2 * f + 1 if part == 1 else f + 1)
                    else:
                        pe.wait_ge(c_ready, f + 1)
                        if differs(f, 0):
                            pe.wait_ge(at_act, 2 * f)
                    if part < 2:
                        for g in range(8):
                            page = 8 * part + g
                            for c in COLS:
                                last = pe.matmul(PS[c:c + 64, 6, NS * g:NS * g + NS],
                                                 S[par][:, P * page + c:P * page + c + 64], coef[par],
                                                 start=True, stop=True)
                    else:
                        last = pe.matmul(PS[0:NS, 6, 0:NS], S[par][:, PAST:PAST + NS], coef[par], start=True, stop=True)
                    last.then_inc(pt_done, 1)

                def values(f):
                    if differs(f, 0):
                        pe.wait_ge(o_lo, f)
                        pe.wait_ge(o_hi, f)
                    pe.wait_ge(at_act, 2 * f + 2)
                    pe.wait_ge(at_dve, f + 1)
                    for half in range(2):
                        pe.wait_ge(self.pages_full[V_SLOT[half]], 16 + 16 * f)
                        vp = L.ring[V_SLOT[half]].rearrange("p (g n) -> p g n", g=NPAGE // 2)
                        for g in range(NPAGE // 2):
                            page = half * 8 + g
                            for quad in range(2):
                                c = 64 * (g % 2) + 32 * quad
                                pe.matmul(PS[c:c + 32, 7, 0:256], at[:, page, 32 * quad:32 * quad + 32],
                                          vp[:, g, 256 * quad:256 * quad + 256], start=page < 2, stop=page == 15)
                    for quad in range(2):
                        last = pe.matmul(PS[32 * quad:32 * quad + 32, 7, 0:256], at[0:NS, 16, 32 * quad:32 * quad + 32],
                                         L.v[0:NS, 4, 256 * quad:256 * quad + 256], start=False, stop=True)
                    last.then_inc(pv_done, 1)

                def step(b, par, keys, vals):
                    f = b - 1
                    if keys:
                        transposes(b, 0, par)
                        transposes(b, 1, par)
                        pe.wait_ge(q_st, b + 1)
                        scores(b, 0, par)
                        transposes(b, 2, par)
                        scores(b, 1, par)
                    if vals:
                        weights(f, 0, 1 - par)
                    if keys:
                        transposes(b, 3, par)
                        scores(b, 2, par)
                    if vals:
                        weights(f, 1, 1 - par)
                    if keys:
                        scores(b, 3, par)
                    if vals:
                        weights(f, 2, 1 - par)
                    if keys:
                        scores(b, 4, par)
                    if vals:
                        values(f)
                looped(pe, step)


    def load_expert(self, sp, e, par, kind):
        w = self.a[("w_gate", "w_up", "w_down")[kind]][0]
        slot = EXPERT[par][kind]
        k = FC if kind == 2 else KC
        sp.dma_start(self.L.ring[slot], w[bass.ds(e, 1)].rearrange("a (p k) n -> p (a k n)", k=k)
                     ).then_inc(self.ring_full[slot], 16)

    def merge(self):
        nc, a, L, PS = self.nc, self.a, self.L, self.PS
        (o_in, ss_ready, ss_power, mix_ready, mod_in, mod_ready, tr_done, ev_a, ev_d, proj_done, sq1, rs1, x1_done,
         sq2, rs2, h2_done, h2_tr, h2_ev, log_done, log_read, h2_out, group_in, exp_in, exp_out, hot_done, rank_done,
         slots_done, scattered, table_back) = (
             self.sem("e_" + n) for n in (
                 "o_in", "ss_ready", "ss_power", "mix_ready", "mod_in", "mod_ready", "tr", "ev_a", "ev_d", "proj",
                 "sq1", "rs1", "x1", "sq2", "rs2", "h2", "h2_tr", "h2_ev", "log", "log_read", "h2_out", "group_in",
                 "exp_in", "exp_out", "hot", "rank", "slots", "scattered", "table_back"))
        x_in = self.sem("e_x_in")
        h2_ev2 = self.sem("e_h2_ev_dve")
        h2_out2 = [h2_out, self.sem("e_h2_out1")]
        dchain, pchain = self.sem("dve_chain_e"), self.sem("pool_chain_e")
        mod = [L.at(L.MP + D * i, D) for i in range(6)]
        g_post, g_pre = L.at(L.QKT + 2048, D), L.at(L.QKT + 3072, D)
        sq = L.at(L.QKT + 4096, 512, 0, NS)
        hv = [L.at(L.V + D * i, D) for i in range(2)]
        osb = L.at(L.V + 2048, 512, 0, NS)
        mixT = [L.at(L.HT + D * i, D).rearrange("p (k t) -> p k t", k=KC) for i in range(2)]
        h2T = [L.at(L.HT + 2048 + D * i, D).rearrange("p (k t) -> p k t", k=KC) for i in range(2)]
        st = self.stats
        ss8, ss1, ss2 = st[:, 16:24], self.ssq, self.rstd
        x_of = [a["x_prompt"][0, t * P:(t + 1) * P, :] for t in range(4)] + \
            [a["x_sample"].rearrange("b t n -> (b t) n")]
        r0 = L.QKT + 4096
        buf = {}

        def take(name, n, base=[r0, L.HT + 4096]):
            room = buf.setdefault("", [0, 0])
            k = 0 if room[0] + n <= 512 else 1
            v = L.at(base[k] + room[k], n)
            room[k] += n
            assert room[k] <= 512
            return v

        t4 = lambda x: x.rearrange("p (t n) -> p t n", t=NT)
        eg, ee = t4(take("eg", 20)), t4(take("ee", 20))
        og, o1, o2 = (t4(take(n, 20)) for n in ("og", "o1", "o2"))
        gm, gs, rk = take("gm", 5), take("gs", 5), take("rk", 5)
        m12 = take("m12", 10).rearrange("p (t j) -> p t j", t=NT)
        ws = take("ws", 5)
        hot = take("hot", 240).rearrange("p (j t e) -> p j t e", j=3, t=NT)
        prod = take("prod", 80).rearrange("p (t e) -> p t e", t=NT)
        over, ovpre, delta = take("over", 16), take("ovpre", 16), take("delta", 16)
        ovall = take("ovall", 256)
        slotf = take("slotf", 10).rearrange("p (t j) -> p t j", t=NT)
        eid = take("eid", OVER + 1)

        with nc.Block() as block:
            @block.sync
            def _(sp):
                self.load_expert(sp, 0, 0, 2)
                self.load_expert(sp, 1, 1, 0)
                sp.wait_ge(proj_done, NT)
                self.load_expert(sp, 1, 1, 1)
                self.load_expert(sp, 1, 1, 2)

            @block.gpsimd
            def _(pool):
                link = chain(pool, pchain)
                pool.wait_ge(ss_ready, 1)
                self.power(pool, link, ss8, H, NS, 1.0 / DV, ss_power)
                for t in range(NT):
                    n = rows(t)
                    for s, ready, done in ((ss1, sq1, rs1), (ss2, sq2, rs2)):
                        pool.wait_ge(ready, t + 1)
                        self.power(pool, link, s[:, t:t + 1], 1, n, 1.0 / D, done)
                pool.wait_ge(slots_done, 1)
                for t in range(NT):
                    n = rows(t)
                    for j in range(2):
                        pool.indirect_dma_start(
                            self.slot_token, bass.IndirectOffsetOnAxis(ap=self.ints[0:n, 32 + 2 * t + j:33 + 2 * t + j], axis=0),
                            self.ints[0:n, 24 + t:25 + t], None).then_inc(scattered, 16)
                pool.wait_ge(scattered, 16 * 2 * NT)
                with nc.allow_non_contiguous_dma(reason="3072 row numbers, once"):
                    pool.dma_start(self.ints[:, 0:NTILE], self.slot_token.rearrange("(e p) o -> p (e o)", p=P)
                                   ).then_inc(table_back, 16)
                pool.wait_ge(table_back, 16)

            @block.scalar
            def _(act):
                for b in range(SB):
                    act.dma_start(osb[ST * b:ST * b + ST].rearrange("t (h d) -> t h d", h=H),
                                  self.o_sample[b].rearrange("(h t) d -> t h d", h=H)).then_inc(o_in, 16)
                act.dma_start(g_post, a["g_post_mix"].partition_broadcast(P)).then_inc(mod_in, 16)
                act.dma_start(g_pre, a["g_pre_ffn"].partition_broadcast(P)).then_inc(mod_in, 16)
                for i, c in enumerate((2, 4, 3)):
                    act.dma_start(mod[i], self.mod[NS, c * D:(c + 1) * D].partition_broadcast(P)).then_inc(mod_in, 16)
                    act.dma_start(mod[3 + i][0:NS], self.mod[0:NS, c * D:(c + 1) * D]).then_inc(mod_in, 16)
                for t in range(NT):
                    act.dma_start(self.x1[0:rows(t), t, :], x_of[t]).then_inc(x_in, 16)

                def second(t):
                    n = rows(t)
                    act.wait_ge(x1_done, t + 1)
                    if t >= 2:
                        act.wait_ge(h2_tr, t - 1)
                        act.wait_ge(h2_out2[t % 2], 16 * (t // 2))
                    act.activation(hv[t % 2][0:n], self.x1[0:n, t, :], ACT.Square,
                                   accum_out=ss2[0:n, t:t + 1]).then_inc(sq2, 1)
                    act.wait_ge(h2_done, t + 1)
                    act.dma_start(self.h2[P * t:P * t + n, :], hv[t % 2][0:n]).then_inc(h2_out2[t % 2], 16)

                def evac_h2(t):
                    m = rows(t)
                    act.wait_ge(h2_tr, t + 1)
                    act.activation(h2T[t % 2][:, 0:4, 0:m],
                                   PS[:, 4, :].rearrange("p (k t) -> p k t", k=4)[:, :, 0:m], ACT.Copy).then_inc(h2_ev, 1)

                for t in range(NT + 1):
                    if t < NT:
                        n = rows(t)
                        act.wait_ge(tr_done, t + 1)
                        act.activation(mixT[t % 2][:, 0:4, 0:n],
                                       PS[:, 0, :].rearrange("p (k t) -> p k t", k=4)[:, :, 0:n], ACT.Copy).then_inc(ev_a, 1)
                        if t >= 1:
                            evac_h2(t - 1)
                        act.wait_ge(proj_done, t + 1)
                        if t >= 2:
                            act.wait_ge(h2_out2[t % 2], 16 * (t // 2))
                            act.wait_ge(h2_tr, t - 1)
                        act.activation(hv[t % 2][0:n], PS[0:n, 2:4, :].rearrange("p b n -> p (b n)"), ACT.Square,
                                       accum_out=ss1[0:n, t:t + 1]).then_inc(sq1, 1)
                        second(t)
                    if t == NT:
                        evac_h2(t - 1)
                act.wait_ge(exp_in, 1)
                act.activation(eg, eg, ACT.Exp).then_inc(exp_out, 1)
                act.wait_ge(exp_in, 2)
                act.activation(ee, ee, ACT.Exp).then_inc(exp_out, 1)
                act.wait_ge(h2_out2[0], 48)
                act.wait_ge(h2_out2[1], 32)

            @block.vector
            def _(dve):
                link = chain(dve, dchain)
                dve.wait_ge(o_in, 16 * SB)
                self.head_norm(dve, link, osb, sq, ss8, L.mix[0:NS, 4, 0:512], NS, ss_ready, ss_power, 1)
                dve.wait_ge(mod_in, 16 * 8)
                for i, n in ((0, P), (3, NS)):
                    dve.tensor_tensor(mod[i][0:n], mod[i][0:n], g_post[0:n], ALU.mult)
                    link(dve.scalar_tensor_tensor(mod[i + 1][0:n], mod[i + 1][0:n], 1.0, g_pre[0:n], ALU.add, ALU.mult))
                dve.tensor_copy(st[0:1, 44:45], st[0:1, 16:17]).then_inc(mix_ready, 1)
                dve.wait_ge(x_in, 16 * NT)
                dve.wait_ge(self.table_in, 80)
                dve.memset(self.logits, 0.0).then_inc(dchain, 1)
                link.count[0] += 1
                dve.wait_ge(dchain, link.count[0])

                def second(t):
                    n = rows(t)
                    dve.wait_ge(h2_tr, t + 1)
                    dve.tensor_copy(h2T[t % 2][:, 4:8, 0:n],
                                    PS[:, 5, :].rearrange("p (k t) -> p k t", k=4)[:, :, 0:n]).then_inc(h2_ev2, 1)
                    dve.wait_ge(log_done, t + 1)
                    dve.tensor_tensor(self.logits[0:n, t, :], PS[0:n, 6, 0:20], self.b_r[0:n], ALU.add
                                      ).then_inc(log_read, 1)

                for t in range(NT):
                    n = rows(t)
                    i = 0 if t < 4 else 3
                    x1 = self.x1[0:n, t, :]
                    h = hv[t % 2][0:n]
                    dve.wait_ge(tr_done, t + 1)
                    dve.tensor_copy(mixT[t % 2][:, 4:8, 0:n],
                                    PS[:, 1, :].rearrange("p (k t) -> p k t", k=4)[:, :, 0:n]).then_inc(ev_d, 1)
                    if t >= 1:
                        second(t - 1)
                    dve.wait_ge(rs1, t + 1)
                    link(dve.scalar_tensor_tensor(h, PS[0:n, 2:4, :].rearrange("p b n -> p (b n)"), ss1[0:n, t:t + 1],
                                                  mod[i][0:n], ALU.mult, ALU.mult))
                    dve.tensor_tensor(x1, x1, h, ALU.add).then_inc(x1_done, 1)
                    dve.wait_ge(rs2, t + 1)
                    link(dve.scalar_tensor_tensor(h, x1, ss2[0:n, t:t + 1], mod[i + 1][0:n], ALU.mult, ALU.mult))
                    dve.tensor_tensor(h, h, mod[i + 2][0:n], ALU.add).then_inc(h2_done, 1)
                second(NT - 1)
                dve.wait_ge(log_read, NT)

                def bc(x, k):
                    return x.unsqueeze(2).to_broadcast([P, NT, k])

                def first_max(dst, vals, top):
                    link(dve.tensor_tensor(dst, vals, bc(top, 4), ALU.is_equal))
                    link(dve.tensor_tensor(dst, dst, L.cst("desc").unsqueeze(1).to_broadcast([P, NT, 4]), ALU.mult))
                    link(dve.tensor_reduce(rk, dst, AX, ALU.max))
                    link(dve.tensor_tensor(dst, dst, bc(rk, 4), ALU.is_equal))

                lg, le = self.logits[:, :, 0:4], self.logits[:, :, 4:20]
                link(dve.tensor_reduce(gm, lg, AX, ALU.max))
                dve.tensor_tensor(eg, lg, bc(gm, 4), ALU.subtract).then_inc(exp_in, 1)
                first_max(og, lg, gm)
                by_group = lambda x: x.rearrange("p t (g j) -> p t g j", g=4)
                ogb = og.unsqueeze(3).to_broadcast([P, NT, 4, 4])
                link(dve.tensor_tensor(by_group(prod), by_group(le), ogb, ALU.mult))
                link(dve.tensor_reduce(ee, prod.rearrange("p t (g j) -> p t j g", g=4), AX, ALU.add))
                link(dve.tensor_reduce(gs, ee, AX, ALU.max))
                dve.tensor_tensor(ee, ee, bc(gs, 4), ALU.subtract).then_inc(exp_in, 1)
                dve.wait_ge(exp_out, 2)
                link(dve.tensor_reduce(m12[:, :, 0], ee, AX, ALU.max))
                first_max(o1, ee, m12[:, :, 0])
                link(dve.scalar_tensor_tensor(ee, o1, -2.0, ee, ALU.mult, ALU.add))
                link(dve.tensor_reduce(m12[:, :, 1], ee, AX, ALU.max))
                first_max(o2, ee, m12[:, :, 1])
                link(dve.tensor_tensor(ws, m12[:, :, 0], m12[:, :, 1], ALU.add))
                link(dve.tensor_reduce(gs, eg, AX, ALU.add))
                link(dve.tensor_tensor(ws, ws, gs, ALU.mult))
                link(dve.reciprocal(ws, ws))
                link(dve.tensor_tensor(self.weights, m12, bc(ws, 2), ALU.mult))
                for j, oj in ((0, o1), (1, o2)):
                    link(dve.tensor_tensor(by_group(hot[:, j]), ogb, oj.unsqueeze(2).to_broadcast([P, NT, 4, 4]), ALU.mult))
                    link(dve.memset(hot[NS:P, j, 4, :], 0.0))
                dve.tensor_tensor(hot[:, 2], hot[:, 0], hot[:, 1], ALU.add).then_inc(hot_done, 1)
                dve.wait_ge(rank_done, 1)
                total = PS[:, 7, 80:96]
                link(dve.tensor_scalar(over, total, float(P), None, ALU.is_gt))
                for i in range(2, -(-TOK // P)):
                    link(dve.tensor_scalar(delta, total, float(P * i), None, ALU.is_gt))
                    link(dve.tensor_tensor(over, over, delta, ALU.add))
                oa = ovall.rearrange("p (e f) -> p e f", e=NE)
                link(dve.tensor_tensor(oa, over.unsqueeze(1).to_broadcast([P, NE, NE]),
                                       L.cst("earlier").rearrange("p (e f) -> p e f", e=NE), ALU.mult))
                link(dve.tensor_reduce(ovpre, oa, AX, ALU.add))
                link(dve.tensor_scalar(delta, ovpre, float(P), float(P * (MAIN - 1)), ALU.mult, ALU.add))
                link(dve.tensor_tensor(delta, delta, L.cst("mainbase"), ALU.subtract))
                rank = PS[:, 7, 0:80].rearrange("p (t e) -> p t e", t=NT)
                link(dve.tensor_scalar(prod, rank, float(P), None, ALU.is_ge))
                link(dve.tensor_tensor(prod, prod, delta.unsqueeze(1).to_broadcast([P, NT, NE]), ALU.mult))
                link(dve.tensor_tensor(prod, rank, prod, ALU.add))
                link(dve.tensor_tensor(prod, prod, L.cst("mainbase").unsqueeze(1).to_broadcast([P, NT, NE]), ALU.add))
                for j in range(2):
                    link(dve.tensor_tensor(hot[:, j], hot[:, j], prod, ALU.mult))
                    link(dve.tensor_reduce(slotf[:, :, j], hot[:, j], AX, ALU.add))
                dve.tensor_copy(self.ints[:, 32:42], slotf.rearrange("p t j -> p (t j)")).then_inc(slots_done, 1)
                link(dve.tensor_tensor(ovpre, ovpre, over, ALU.add))
                ob = ovall[:, 0:OVER * NE].rearrange("p (j e) -> p j e", j=OVER)
                link(dve.tensor_tensor(ob, ovpre.unsqueeze(1).to_broadcast([P, OVER, NE]),
                                       L.cst("index").unsqueeze(2).to_broadcast([P, OVER, NE]), ALU.is_le))
                link(dve.tensor_reduce(eid[:, 0:OVER], ob, AX, ALU.add))
                link(dve.tensor_scalar_min(eid[:, 0:OVER], eid[:, 0:OVER], float(NE - 1)))
                link(dve.tensor_copy(eid[:, OVER:OVER + 1], ovpre[:, NE - 1:NE]))
                link(dve.tensor_copy(self.ints[:, 48:49 + OVER], eid))

            @block.tensor
            def _(pe):
                pe.wait_ge(mix_ready, 1)

                def second(t):
                    n = rows(t)
                    pe.wait_ge(h2_done, t + 1)
                    if t >= 1:
                        pe.wait_ge(h2_ev, t)
                        pe.wait_ge(h2_ev2, t)
                    for k in range(KC):
                        last = pe.transpose(PS[:, 4 + k // 4, (k % 4) * P:(k % 4) * P + n], hv[t % 2][0:n, k::KC],
                                            L.cst("ident", n)[:, 0:n])
                    last.then_inc(h2_tr, 1)
                    pe.wait_ge(h2_ev, t + 1)
                    pe.wait_ge(h2_ev2, t + 1)
                    if t >= 1:
                        pe.wait_ge(log_read, t)
                    for k in range(KC):
                        last = pe.matmul(PS[0:n, 6, 0:20], h2T[t % 2][:, k, 0:n], self.w_r[:, k, :],
                                         start=k == 0, stop=k == KC - 1)
                    last.then_inc(log_done, 1)

                for t in range(NT):
                    n = rows(t)
                    if t >= 1:
                        pe.wait_ge(ev_a, t)
                        pe.wait_ge(ev_d, t)
                    for k in range(KC):
                        last = pe.transpose(PS[:, k // 4, (k % 4) * P:(k % 4) * P + n], L.mix[0:n, t, k::KC],
                                            L.cst("ident", n)[:, 0:n])
                    last.then_inc(tr_done, 1)
                    pe.wait_ge(ev_a, t + 1)
                    pe.wait_ge(ev_d, t + 1)
                    if t >= 1:
                        pe.wait_ge(x1_done, t)
                    for c in range(2):
                        if t == 0:
                            pe.wait_ge(self.ring_full[W_OUT[c]], 16 * STATIC_USES[W_OUT[c]] + 16)
                        w = L.ring[W_OUT[c]].rearrange("p (k n) -> p k n", k=KC)
                        for k in range(KC):
                            last = pe.matmul(PS[0:n, 2 + c, :], mixT[t % 2][:, k, 0:n], w[:, k, :],
                                             start=k == 0, stop=k == KC - 1)
                    last.then_inc(proj_done, 1)
                    if t >= 1:
                        second(t - 1)
                second(NT - 1)
                pe.wait_ge(hot_done, 1)
                for t in range(NT + 1):
                    out = PS[:, 7, 16 * t:16 * t + 16]
                    for u in range(min(t, NT)):
                        last = pe.matmul(out, L.cst("ones"), hot[:, 2, u, :], start=u == 0, stop=t == NT and u == NT - 1)
                    if t < NT:
                        last = pe.matmul(out, L.cst("before"), hot[:, 2, t, :], start=t == 0, stop=True)
                last.then_inc(rank_done, 1)

    def expert_buffers(self):
        L = self.L
        n = L.HT
        out = {}
        for name, size in (("xg", D), ("xT", D), ("sg", DE), ("h", DE), ("hT", DE), ("y", D)):
            out[name] = [L.at(n + size * i, size) for i in range(2)]
            n += 2 * size
        return out

    def experts(self):
        nc, L, PS = self.nc, self.L, self.PS
        (x_tr, xt_a, xt_d, g_done, u_done, sg_done, h_done, h_tr, ht_ev, d_done, y_a, y_d, ix_done) = (
            self.sem("f_" + n) for n in ("x_tr", "xt_a", "xt_d", "gate", "up", "silu", "h", "h_tr", "ht_ev", "down",
                                         "y_a", "y_d", "index"))
        xg_in = [self.sem("f_xg_in0"), self.sem("f_xg_in1")]
        y_out = [self.sem("f_y_out0"), self.sem("f_y_out1")]
        B = self.expert_buffers()
        k3 = lambda x, k: x.rearrange("p (k t) -> p k t", k=k)
        xT, hT = [k3(x, KC) for x in B["xT"]], [k3(x, FC) for x in B["hT"]]
        full0 = [16 * (STATIC_USES[s] + (s in W_OUT)) for s in range(6)]

        def looped(eng, step):
            for e in range(3):
                step(e, e % 2, True, True)
            with eng.Fori(0, (MAIN - 4) // 2) as i:
                step(2 * i + 3, 1, True, True)
                step(2 * i + 4, 0, True, True)
            step(MAIN - 1, 1, True, False)
            step(MAIN, 0, False, False)

        with nc.Block() as block:
            @block.sync
            def _(sp):
                def store(e, par):
                    sp.wait_ge(y_a, e + 1)
                    sp.wait_ge(y_d, e + 1)
                    sp.dma_start(self.y_rows[bass.ds(e * P, P)], B["y"][par]).then_inc(y_out[par], 16)

                def step(e, par):
                    for kind, free in ((0, g_done), (1, u_done), (2, d_done)):
                        sp.wait_ge(free, e + 1)
                        self.load_expert(sp, e + 2, par, kind)
                    store(e, par)
                with sp.Fori(0, (MAIN - 2) // 2) as i:
                    step(2 * i, 0)
                    step(2 * i + 1, 1)
                store(MAIN - 2, 0)
                store(MAIN - 1, 1)
                sp.wait_ge(y_out[0], 16 * MAIN // 2)
                sp.wait_ge(y_out[1], 16 * MAIN // 2)

            @block.gpsimd
            def _(pool):
                def gather(e, par):
                    if differs(e, 0) and differs(e, 1):
                        pool.wait_ge(x_tr, e - 1)
                    index = self.ints[:, 60 + par:61 + par]
                    pool.tensor_copy(index, self.ints[:, bass.ds(e, 1)]).then_inc(ix_done, 1)
                    pool.wait_ge(ix_done, e + 1)
                    self.stand_apart(pool)
                    pool.indirect_dma_start(B["xg"][par], None, self.h2,
                                            bass.IndirectOffsetOnAxis(ap=index, axis=0)).then_inc(xg_in[par], 16)

                gather(0, 0)

                def step(e, par, here, ahead):
                    if ahead:
                        gather(e + 1, 1 - par)
                looped(pool, step)

            @block.scalar
            def _(act):
                def evac_x(e, par):
                    act.wait_ge(x_tr, e + 1)
                    act.activation(xT[par][:, 0:4, :], k3(PS[:, 2, :], 4), ACT.Copy).then_inc(xt_a, 1)

                evac_x(0, 0)

                def step(e, par, here, ahead):
                    if here:
                        act.wait_ge(g_done, e + 1)
                        if differs(e, 0) and differs(e, 1):
                            act.wait_ge(h_done, e - 1)
                        act.activation(B["sg"][par], PS[:, 0, :], ACT.Silu).then_inc(sg_done, 1)
                    if differs(e, 0):
                        act.wait_ge(d_done, e)
                        if differs(e, 1) and differs(e, 2):
                            act.wait_ge(y_out[1 - par], 8 * (e - 1 - (1 - par)))
                        act.activation(B["y"][1 - par][:, 0:512], PS[:, 5, :], ACT.Copy).then_inc(y_a, 1)
                    if here:
                        act.wait_ge(h_tr, e + 1)
                        act.activation(hT[par], k3(PS[:, 4, :], FC), ACT.Copy).then_inc(ht_ev, 1)
                    if ahead:
                        evac_x(e + 1, 1 - par)
                looped(act, step)

            @block.vector
            def _(dve):
                def evac_x(e, par):
                    dve.wait_ge(x_tr, e + 1)
                    dve.tensor_copy(xT[par][:, 4:8, :], k3(PS[:, 3, :], 4)).then_inc(xt_d, 1)

                evac_x(0, 0)

                def step(e, par, here, ahead):
                    if here:
                        dve.wait_ge(sg_done, e + 1)
                        dve.wait_ge(u_done, e + 1)
                        if differs(e, 0) and differs(e, 1):
                            dve.wait_ge(h_tr, e - 1)
                        dve.tensor_tensor(B["h"][par], B["sg"][par], PS[:, 1, :], ALU.mult).then_inc(h_done, 1)
                    if differs(e, 0):
                        dve.wait_ge(d_done, e)
                        if differs(e, 1) and differs(e, 2):
                            dve.wait_ge(y_out[1 - par], 8 * (e - 1 - (1 - par)))
                        dve.tensor_copy(B["y"][1 - par][:, 512:1024], PS[:, 6, :]).then_inc(y_d, 1)
                    if ahead:
                        evac_x(e + 1, 1 - par)
                looped(dve, step)

            @block.tensor
            def _(pe):
                def tokens(e, par):
                    pe.wait_ge(xg_in[par], 16 + 8 * (e - par))
                    if differs(e, 0):
                        pe.wait_ge(xt_a, e)
                        pe.wait_ge(xt_d, e)
                    for k in range(KC):
                        last = pe.transpose(PS[:, 2 + k // 4, (k % 4) * P:(k % 4 + 1) * P], B["xg"][par][:, k::KC],
                                            L.cst("ident"))
                    last.then_inc(x_tr, 1)

                def gate_up(e, par):
                    pe.wait_ge(xt_a, e + 1)
                    pe.wait_ge(xt_d, e + 1)
                    if differs(e, 0):
                        pe.wait_ge(h_done, e)
                    for kind, done in ((0, g_done), (1, u_done)):
                        slot = EXPERT[par][kind]
                        pe.wait_ge(self.ring_full[slot], full0[slot] + 16 + 8 * (e - par))
                        w = k3(L.ring[slot], KC)
                        for k in range(KC):
                            last = pe.matmul(PS[:, kind, :], xT[par][:, k, :], w[:, k, :], start=k == 0, stop=k == KC - 1)
                        last.then_inc(done, 1)

                def down(e, par):
                    pe.wait_ge(ht_ev, e + 1)
                    if differs(e, 0):
                        pe.wait_ge(y_a, e)
                        pe.wait_ge(y_d, e)
                    slot = EXPERT[par][2]
                    pe.wait_ge(self.ring_full[slot], full0[slot] + 16 + 8 * (e - par))
                    w = k3(L.ring[slot], FC)
                    for c in range(2):
                        for k in range(FC):
                            last = pe.matmul(PS[:, 5 + c, :], hT[par][:, k, :], w[:, k, 512 * c:512 * c + 512],
                                             start=k == 0, stop=k == FC - 1)
                    last.then_inc(d_done, 1)

                def step(e, par, here, ahead):
                    if here:
                        gate_up(e, par)
                    if differs(e, 0):
                        down(e - 1, 1 - par)
                    if here:
                        pe.wait_ge(h_done, e + 1)
                        if differs(e, 0):
                            pe.wait_ge(ht_ev, e)
                        for k in range(FC):
                            last = pe.transpose(PS[:, 4, P * k:P * k + P], B["h"][par][:, k::FC], L.cst("ident"))
                        last.then_inc(h_tr, 1)
                    if ahead:
                        tokens(e + 1, 1 - par)
                tokens(0, 0)
                looped(pe, step)

    def later_tiles(self):
        nc, L, PS = self.nc, self.L, self.PS
        (ix, xg_in, x_tr, xt, gate, silu, h_done, h_tr, ht, down, y_ready, y_out, up) = (
            self.sem("g_" + n) for n in ("index", "xg_in", "x_tr", "xt", "gate", "silu", "h", "h_tr", "ht", "down",
                                         "y_ready", "y_out", "up"))
        B = self.expert_buffers()
        k3 = lambda x, k: x.rearrange("p (k t) -> p k t", k=k)
        xg, xT, sg, h, hT, y = (B[n][0] for n in ("xg", "xT", "sg", "h", "hT", "y"))
        w_in = [self.sem("g_w_in" + str(i)) for i in range(3)]

        def looped(eng, tile):
            many = eng.value_load(self.ints[0:1, 48 + OVER:49 + OVER], min_val=0, max_val=OVER)
            with eng.Fori(0, OVER) as j:
                with eng.If(many > j):
                    tile(j)
                    eng.wait_ge(y_out, 16 * j + 16)
                    self.stand_apart(eng)

        with nc.Block() as block:
            @block.sync
            def _(sp):
                def tile(j):
                    e = sp.value_load(self.ints[0:1, bass.ds(48 + j, 1)], min_val=0, max_val=NE - 1)
                    for kind, n in enumerate(("w_gate", "w_up", "w_down")):
                        sp.dma_start(L.ring[EXPERT[0][kind]], self.a[n][0][bass.ds(e, 1)].rearrange(
                            "a (p k) n -> p (a k n)", k=FC if kind == 2 else KC)).then_inc(w_in[kind], 16)
                    sp.wait_ge(y_ready, 2 * j + 2)
                    sp.dma_start(self.y_rows[bass.ds((j + MAIN) * P, P)], y).then_inc(y_out, 16)
                looped(sp, tile)

            @block.gpsimd
            def _(pool):
                def tile(j):
                    index = self.ints[:, 60:61]
                    pool.tensor_copy(index, self.ints[:, bass.ds(j + MAIN, 1)]).then_inc(ix, 1)
                    pool.wait_ge(ix, j + 1)
                    self.stand_apart(pool)
                    pool.indirect_dma_start(xg, None, self.h2,
                                            bass.IndirectOffsetOnAxis(ap=index, axis=0)).then_inc(xg_in, 16)
                looped(pool, tile)

            @block.scalar
            def _(act):
                def tile(j):
                    act.wait_ge(x_tr, j + 1)
                    act.activation(xT[:, 0:512], PS[:, 2, :], ACT.Copy).then_inc(xt, 1)
                    act.wait_ge(gate, j + 1)
                    act.activation(sg, PS[:, 0, :], ACT.Silu).then_inc(silu, 1)
                    act.wait_ge(h_tr, j + 1)
                    act.activation(hT, PS[:, 4, :], ACT.Copy).then_inc(ht, 1)
                    act.wait_ge(down, j + 1)
                    act.activation(y[:, 0:512], PS[:, 5, :], ACT.Copy).then_inc(y_ready, 1)
                looped(act, tile)

            @block.vector
            def _(dve):
                def tile(j):
                    dve.wait_ge(x_tr, j + 1)
                    dve.tensor_copy(xT[:, 512:1024], PS[:, 3, :]).then_inc(xt, 1)
                    dve.wait_ge(silu, j + 1)
                    dve.wait_ge(up, j + 1)
                    dve.tensor_tensor(h, sg, PS[:, 1, :], ALU.mult).then_inc(h_done, 1)
                    dve.wait_ge(down, j + 1)
                    dve.tensor_copy(y[:, 512:1024], PS[:, 6, :]).then_inc(y_ready, 1)
                looped(dve, tile)

            @block.tensor
            def _(pe):
                def tile(j):
                    pe.wait_ge(xg_in, 16 * j + 16)
                    for k in range(KC):
                        last = pe.transpose(PS[:, 2 + k // 4, (k % 4) * P:(k % 4 + 1) * P], xg[:, k::KC], L.cst("ident"))
                    last.then_inc(x_tr, 1)
                    pe.wait_ge(xt, 2 * j + 2)
                    for kind, done in ((0, gate), (1, up)):
                        pe.wait_ge(w_in[kind], 16 * j + 16)
                        for k in range(KC):
                            last = pe.matmul(PS[:, kind, :], k3(xT, KC)[:, k, :], k3(L.ring[EXPERT[0][kind]], KC)[:, k, :],
                                             start=k == 0, stop=k == KC - 1)
                        last.then_inc(done, 1)
                    pe.wait_ge(h_done, j + 1)
                    for k in range(FC):
                        last = pe.transpose(PS[:, 4, P * k:P * k + P], h[:, k::FC], L.cst("ident"))
                    last.then_inc(h_tr, 1)
                    pe.wait_ge(ht, j + 1)
                    pe.wait_ge(w_in[2], 16 * j + 16)
                    for c in range(2):
                        for k in range(FC):
                            last = pe.matmul(PS[:, 5 + c, :], k3(hT, FC)[:, k, :],
                                             k3(L.ring[EXPERT[0][2]], FC)[:, k, 512 * c:512 * c + 512],
                                             start=k == 0, stop=k == FC - 1)
                    last.then_inc(down, 1)
                looped(pe, tile)

    def combine(self):
        nc, a, o, L = self.nc, self.a, self.o, self.L
        y_in = [self.sem(f"h_y_in{t}") for t in range(NT)]
        sq, rs, out_done, stored, mod_in = (self.sem("h_" + n) for n in ("sq", "rs", "out", "stored", "mod_in"))
        dchain, pchain, y_done = self.sem("dve_chain_h"), self.sem("pool_chain_h"), self.sem("h_y")
        yb = [[L.at(D * (2 * t + j), D) for j in range(2)] for t in range(NT)]
        ga = [L.at(L.MIX + D * i, D) for i in range(2)]
        g = L.at(L.MIX + 2 * D, D)
        y_o = [o["y_prompt"][0, t * P:(t + 1) * P, :] for t in range(4)] + [o["y_sample"].rearrange("b t n -> (b t) n")]
        with nc.Block() as block:
            @block.gpsimd
            def _(pool):
                link = chain(pool, pchain)
                for t in range(NT):
                    n = rows(t)
                    for j in range(2):
                        pool.indirect_dma_start(yb[t][j][0:n], None, self.y_rows, bass.IndirectOffsetOnAxis(
                            ap=self.ints[0:n, 32 + 2 * t + j:33 + 2 * t + j], axis=0)).then_inc(y_in[t], 16)
                for t in range(NT):
                    pool.wait_ge(sq, t + 1)
                    self.power(pool, link, self.rstd[:, t:t + 1], 1, rows(t), 1.0 / D, rs)

            @block.scalar
            def _(act):
                act.dma_start(ga[0], self.mod[NS, 5 * D:6 * D].partition_broadcast(P)).then_inc(mod_in, 16)
                act.dma_start(ga[1][0:NS], self.mod[0:NS, 5 * D:6 * D]).then_inc(mod_in, 16)
                act.dma_start(g, a["g_post_ffn"].partition_broadcast(P)).then_inc(mod_in, 16)
                for t in range(NT):
                    n = rows(t)
                    act.wait_ge(y_done, t + 1)
                    act.activation(yb[t][1][0:n], yb[t][0][0:n], ACT.Square,
                                   accum_out=self.rstd[0:n, t:t + 1]).then_inc(sq, 1)

            @block.vector
            def _(dve):
                link = chain(dve, dchain)
                dve.wait_ge(mod_in, 48)
                dve.tensor_tensor(ga[0], ga[0], g, ALU.mult)
                link(dve.tensor_tensor(ga[1][0:NS], ga[1][0:NS], g[0:NS], ALU.mult))

                def finish(t):
                    n = rows(t)
                    dve.wait_ge(rs, t + 1)
                    y = yb[t][0][0:n]
                    link(dve.scalar_tensor_tensor(y, y, self.rstd[0:n, t:t + 1], ga[t // 4][0:n], ALU.mult, ALU.mult))
                    dve.tensor_tensor(y, y, self.x1[0:n, t, :], ALU.add).then_inc(out_done, 1)
                for t in range(NT):
                    n = rows(t)
                    dve.wait_ge(y_in[t], 32)
                    link(dve.tensor_scalar_mul(yb[t][0][0:n], yb[t][0][0:n], self.weights[0:n, t, 0:1]))
                    dve.scalar_tensor_tensor(yb[t][0][0:n], yb[t][1][0:n], self.weights[0:n, t, 1:2], yb[t][0][0:n],
                                             ALU.mult, ALU.add).then_inc(y_done, 1)
                    if t >= 1:
                        finish(t - 1)
                finish(NT - 1)

            @block.sync
            def _(sp):
                for t in range(NT):
                    sp.wait_ge(out_done, t + 1)
                    sp.dma_start(y_o[t], yb[t][0][0:rows(t)]).then_inc(stored, 16)
                sp.wait_ge(stored, 16 * NT)


INS = ["x_prompt", "x_sample", "cache_k", "cache_v", "page_table", "c_prompt", "c_sample", "w_ada", "b_ada",
       "g_pre_mix", "g_post_mix", "g_pre_ffn", "g_post_ffn", "w_in", "lam_q1", "lam_k1", "lam_q2", "lam_k2",
       "g_subln", "sgu_ln_g", "sgu_ln_b", "sgu_ws", "sgu_bs", "w_out", "w_rg", "b_rg", "w_re", "b_re",
       "w_gate", "w_up", "w_down"]
OUTS = {"y_prompt": (1, SEQ, D), "y_sample": (SB, ST, D), "k_prompt": (1, 1, SEQ, H, 2 * DQK),
        "v_prompt": (1, 1, SEQ, H, DV), "sgu_prompt": (1, 1, P, 512), "k_sample": (1, SB, ST, H, 2 * DQK),
        "v_sample": (1, SB, ST, H, DV), "sgu_sample": (1, SB, ST, 512)}


def build(nc, a, o):
    where, table, _ = constant_table()
    with ExitStack() as ctx:
        p = Program(nc, a, o, where, table.shape[1], ctx)
        p.condition()
        p.project()
        p.attend_prompt()
        p.attend_sample()
        p.forget()
        p.merge()
        p.experts()
        p.later_tiles()
        p.combine()


def kernel(**inputs):
    from concourse import bacc
    from concourse.bass_utils import run_bass_kernel_spmd

    nc = bacc.Bacc("TRN2", target_bir_lowering=False, num_devices=1)
    _, table, past = constant_table()
    arrays = {n: np.ascontiguousarray(inputs[n]) for n in INS}
    arrays["constants"], arrays["past_bias"] = table, past
    a = {n: nc.dram_tensor("in_" + n, x.shape, mybir.dt.from_np(x.dtype), kind="ExternalInput").ap()
         for n, x in arrays.items()}
    o = {n: nc.dram_tensor("out_" + n, s, F32, kind="ExternalOutput").ap() for n, s in OUTS.items()}
    build(nc, a, o)
    r = run_bass_kernel_spmd(nc, [{"in_" + n: x for n, x in arrays.items()}], core_ids=[0])
    return tuple(r.results[0]["out_" + n] for n in OUTS)
```

```python
import math
from contextlib import ExitStack

import numpy as np

import concourse.bass as bass
from concourse import mybir

ALU = mybir.AluOpType
ACT = mybir.ActivationFunctionType
F32 = mybir.dt.float32
I32 = mybir.dt.int32
AX = mybir.AxisListType.X

P = 128
D = 1024
KC = D // P
SEQ = 512
SB, ST, NS = 8, 8, 64
TOK = SEQ + NS
NT = 5
PAST, PAGE, NPAGE, NPOOL = 2048, 128, 16, 160
ROWKEYS = 8
PAGEROWS = PAGE // ROWKEYS
H, DV, DQK = 8, 64, 32
HP = H // 2
NE, DE = 16, 512
FC = DE // P
EPS = 1e-6
LAM_INIT = 0.8 - 0.6 * math.exp(0.0)
BIG = 1e37
UNIT = 4096
MAIN = NE
OVER = (2 * TOK + (P - 1) * NE) // P - NE
NTILE = MAIN + OVER


COLS = (0, 64)


def differs(b, value):
    return not isinstance(b, int) or b != value


def rows(t):
    return P if t < 4 else NS


def constant_table():
    p = np.arange(P)[:, None]
    cols = {}
    cols["ident"] = np.eye(P)
    x = np.arange(512)[None, :] - 384
    cols["dist"] = np.where(p - x >= 0, p - x, BIG)
    t, h = p % ST, p // 16
    slope = 2.0 ** -(h + 1.0)
    r = np.arange(120)[None, :] - 56
    cols["own"] = np.where((r >= 0) & (r <= t), -slope * (t - r), -BIG)
    cols["tril"] = (np.arange(P)[None, :] <= p) * 1.0
    c64 = np.arange(NS)[None, :]
    cols["sameseq"] = (c64 // ST == p // ST) * 1.0
    cols["repeat"] = (c64 % ST == p) * 1.0
    cols["before"] = (p < np.arange(P)[None, :]) * 1.0
    cols["ones"] = np.ones((P, P))
    e = np.arange(NE)
    cols["earlier"] = np.broadcast_to((e[None, :] < e[:, None]).reshape(1, -1), (P, NE * NE)) * 1.0
    cols["desc"] = np.broadcast_to([4.0, 3.0, 2.0, 1.0], (P, 4))
    cols["mainbase"] = np.broadcast_to(128.0 * e[None, :], (P, NE))
    cols["index"] = np.broadcast_to(np.arange(OVER)[None, :] * 1.0, (P, OVER))
    cols["group"] = (p // 32 == np.arange(4)[None, :]) * 1.0
    cols["diag"] = ((p // ST) % 4 == np.arange(4)[None, :]) * 1.0
    row = (p // 16) * ST + t
    first = (p // ST) % 2 == 0
    cols["sel1"] = ((row == c64) & first) * 1.0
    cols["sel2"] = ((row == c64) & ~first) * 1.0
    cols["half"] = np.full((P, H), -0.5)
    cols["token"] = p + P * np.arange(NT)[None, :] * 1.0
    cols["row"] = np.broadcast_to(np.arange(P)[None, :] * 1.0, (P, P))
    cols["tilestart"] = np.broadcast_to(P * np.arange(NTILE + 1)[None, :] * 1.0, (P, NTILE + 1))
    cols["pagerow"] = p % PAGEROWS * 1.0
    at, parts = {}, []
    n = 0
    for name, a in cols.items():
        a = np.broadcast_to(a, (P, a.shape[1]))
        at[name] = (n, a.shape[1])
        n += a.shape[1]
        parts.append(a)
    past = -slope * (PAST + t - np.arange(PAST).reshape(2, P, ROWKEYS).transpose(0, 2, 1).reshape(1, PAST))
    return at, np.ascontiguousarray(np.concatenate(parts, 1).astype(np.float32)), \
        np.ascontiguousarray(past.astype(np.float32))


class Layout:

    RING, X, HT, MP = 0, 6 * UNIT, 6 * UNIT + 5120, 6 * UNIT + 9728
    QKT, V, MIX, CST = MP + 4096, MP + 8704, MP + 11264, MP + 16384

    def __init__(self, sb, ps, where, ncst):
        self.sb, self.ps, self.where = sb, ps, where
        self.small = self.CST + ncst
        self.ring = [sb[:, s * UNIT:(s + 1) * UNIT] for s in range(6)]
        self.hT = self.at(self.HT, KC * TOK).rearrange("p (k t) -> p k t", k=KC)
        self.qT = self.at(self.QKT, HP * TOK).rearrange("p (h t) -> p h t", h=HP)
        self.kT = self.at(self.QKT + HP * TOK, HP * TOK).rearrange("p (h t) -> p h t", h=HP)
        self.v = self.at(self.V, NT * 512).rearrange("p (t n) -> p t n", t=NT)
        self.mix = self.at(self.MIX, NT * D).rearrange("p (t n) -> p t n", t=NT)
        self.n_small = 0

    def at(self, off, n, p0=0, p1=P):
        return self.sb[p0:p1, off:off + n]

    def cst(self, name, p1=P):
        off, n = self.where[name]
        return self.at(self.CST + off, n, 0, p1)

    def take(self, n):
        off = self.small + self.n_small
        self.n_small += n
        return off


def chain(eng, sem, start=0):
    count = [start]

    def link(ins):
        count[0] += 1
        ins.then_inc(sem, 1)
        eng.wait_ge(sem, count[0])
    link.count = count
    return link


ADA = [[0, 1, 2, 3], [3, 4, 5, 0], [3, 4, 5, 0]]
WIN = [4, 5, 0, 1, 2]
WIN_ORDER = ["s", "u", "v", "k", "q"]
WIN_COL = {"q": 0, "k": 1, "v": 2, "u": 3, "s": 4}
ADA_AFTER = [("k", 2), ("q", 2)]
K_SLOT = [[0, 1], [2, 3]]
V_SLOT = [4, 5]
W_OUT = [0, 1]
EXPERT = [[2, 3, 4], [5, 0, 1]]
STATIC = [("ada", 0, j, s) for j, s in enumerate(ADA[0])] + [("win", 0, c, s) for c, s in enumerate(WIN)] + \
         [("ada", r, j, s) for r in (1, 2) for j, s in enumerate(ADA[r])]


def fills(kind, r, j):
    n = STATIC.index(next(u for u in STATIC if u[:3] == (kind, r, j)))
    return sum(u[3] == STATIC[n][3] for u in STATIC[:n + 1])


STATIC_USES = [sum(u[3] == s for u in STATIC) for s in range(6)]


class Program:
    def __init__(self, nc, a, o, where, ncst, ctx):
        self.passing = []
        self.nc, self.a, self.o, self.ctx, self.ncst = nc, a, o, ctx, ncst
        sb = ctx.enter_context(nc.sbuf_tensor("sb", [P, Layout.CST + ncst + 528], F32))
        self.PS = ctx.enter_context(nc.psum_tensor("ps", [P, 8, 512], F32))
        self.L = Layout(sb, self.PS, where, ncst)
        L = self.L
        self.ints = ctx.enter_context(nc.sbuf_tensor("ints", [P, 96], I32))
        self.ck, self.cv = (a[n].rearrange("l n (j r) h d -> (l n j) (r h d)", r=ROWKEYS)
                            for n in ("cache_k", "cache_v"))
        self.ring_full = [self.lasting(f"ring_full{s}") for s in range(6)]
        self.pages_full = [self.lasting(f"pages_full{s}") for s in range(6)]
        self.cst_in = self.lasting("cst_in")
        self.table_in = self.lasting("table_in")
        self.apart = self.lasting("apart")
        self.ada_done, self.mod_sb, self.mod_out, self.pages_in = (
            self.lasting(n) for n in ("ada_done", "mod_sb", "mod_out", "pages_in"))
        self.staged = self.lasting("staged")
        self.mod_outs = self.lasting("mod_outs")
        self.mod = nc.dram_tensor("mod_rows", (NS + 1, 6 * D), F32).ap()
        self.h2 = nc.dram_tensor("h2_rows", (TOK, D), F32).ap()
        self.y_rows = nc.dram_tensor("y_rows", (NTILE * P, D), F32).ap()
        self.o_sample = nc.dram_tensor("o_sample", (SB, NS, DV), F32).ap()
        self.cS = L.at(L.take(72), 72).rearrange("p (c k) -> p c k", c=9)
        self.rstd = L.at(L.take(NT), NT)
        self.ssq = L.at(L.take(NT), NT)
        self.bsT = L.at(L.take(H), H)
        self.bs8 = L.at(L.take(H), H, 0, NS)
        self.lam = L.at(L.take(136), 136)
        self.w_r = L.at(L.take(160), 160).rearrange("p (k n) -> p k n", k=KC)
        self.gsub = L.at(L.take(DV), DV)
        self.stats = L.at(L.take(48), 48)
        self.row_f = L.at(L.take(16), 16)
        self.b_r = self.stats[:, 24:44]
        self.logits = self.lam[:, 0:100].rearrange("p (t n) -> p t n", t=NT)
        self.weights = self.lam[:, 100:110].rearrange("p (t j) -> p t j", t=NT)
        self.x1 = L.at(L.X, NT * D).rearrange("p (t n) -> p t n", t=NT)

    def sem(self, name):
        self.passing.append(self.nc.alloc_semaphore(name=name))
        return self.passing[-1]

    def stand_apart(self, eng):
        eng.sem_inc(self.apart, 1)

    def lasting(self, name):
        return self.ctx.enter_context(self.nc.semaphore(name))

    def forget(self):
        self.nc.clear_and_free_semaphores(self.passing)
        self.nc.all_engine_barrier()
        self.passing = []

    def condition(self, block):
        nc, a, L, PS = self.nc, self.a, self.L, self.PS
        c_in, g_in, ws_in, bs_in = (self.sem(n) for n in ("c_in", "g_in", "ws_in", "bs_in"))
        x_ins = [self.sem(f"x_in{t}") for t in range(NT)]
        silu_c, mod_in, mod_in_s = self.sem("silu_c"), self.sem("mod_in"), self.sem("mod_in_s")
        ssq_done, rstd_done, h_done, tr_done, ev_a, ev_d = (self.sem(n) for n in
                                                            ("ssq_done", "rstd_done", "h_done", "tr_done",
                                                             "evac_act", "evac_dve"))
        dchain, pchain = self.sem("dve_chain_a"), self.sem("pool_chain_a")
        self.ev_a, self.ev_d, self.tr_done, self.h_done = ev_a, ev_d, tr_done, h_done
        self.w8_made = self.sem("w8_made")
        gpre_in = self.sem("gpre_in")
        mod_asked = self.sem("mod_asked")
        ws_masked, ws_tr, wmT_done, w8_done = (self.sem(n) for n in ("ws_masked", "ws_tr", "wmT_done", "w8_done"))
        self.wmT = L.at(L.V, H * P).rearrange("p (g t) -> p g t", g=H)
        self.w8 = L.at(L.V + 1024, 512, 0, NS).rearrange("p (g b t) -> p g b t", g=H, b=SB)
        xb = [L.at(L.MIX + D * t, D) for t in range(NT)]
        hb = self.hb = [L.at(L.QKT + 2048 + D * i, D) for i in range(2)]
        mp = [L.at(L.MP + 1024 * i, D) for i in range(4)]
        gpre = L.at(L.QKT + 1024, D)
        self.bada = L.at(L.X + 2048, 3 * 512).rearrange("p (r n) -> p r n", r=3)
        self.modst = L.at(L.X + 2048 + 1536, 3 * 512).rearrange("p (r n) -> p r n", r=3)
        wsraw = L.at(L.QKT, H * P).rearrange("p (g s) -> p g s", g=H)
        x_of = [a["x_prompt"][0, t * P:(t + 1) * P, :] for t in range(4)] + \
            [a["x_sample"].rearrange("b t n -> (b t) n")]

        def evac(eng, t, half, done):
            n = rows(t)
            eng.wait_ge(tr_done, t + 1)
            src = PS[:, 6 + half, :].rearrange("p (k t) -> p k t", k=4)[:, :, 0:n]
            dst = L.hT[:, 4 * half:4 * half + 4, t * P:t * P + n]
            if half == 0:
                eng.activation(dst, src, ACT.Copy).then_inc(done, 1)
            else:
                eng.tensor_copy(dst, src).then_inc(done, 1)

        @block.sync
        def _(sp):
            self.load_unit(sp, STATIC[0])
            sp.wait_ge(c_in, 32)
            for u in STATIC[1:4]:
                self.load_unit(sp, u)
            sp.wait_ge(mod_asked, 1)
            self.load_unit(sp, STATIC[4])
            self.mod_store_samples(sp, 0)
            sp.wait_ge(self.mod_outs, 16 * 4)
            sp.dma_start(mp[2][0:NS], self.mod[0:NS, D:2 * D]).then_inc(mod_in_s, 16)
            sp.dma_start(mp[3][0:NS], self.mod[0:NS, 0:D]).then_inc(mod_in_s, 16)
            self.load_unit(sp, STATIC[5])

        @block.gpsimd
        def _(pool):
            for n, c0, c1 in (("rg", 0, 4), ("re", 4, 20)):
                pool.dma_start(self.w_r[:, :, c0:c1], a["w_" + n][0].rearrange("(p k) n -> p k n", k=KC)
                               ).then_inc(self.table_in, 16)
                pool.dma_start(self.b_r[:, c0:c1], a["b_" + n].partition_broadcast(P)).then_inc(self.table_in, 16)
            with nc.allow_non_contiguous_dma(reason="8 x 128 bias values, once"):
                pool.dma_start(self.bsT, a["sgu_bs"][0].rearrange("g t -> t g")).then_inc(bs_in, 16)
            link = chain(pool, pchain)
            pool.wait_ge(self.cst_in, 16)
            for t in range(NT):
                n = rows(t)
                pool.wait_ge(ssq_done, t + 1)
                link(pool.tensor_scalar(self.rstd[0:n, t:t + 1], self.ssq[0:n, t:t + 1], 1.0 / D, EPS,
                                        ALU.mult, ALU.add))
                pool.tensor_tensor(self.rstd[0:n, t:t + 1], self.rstd[0:n, t:t + 1],
                                   L.cst("half", n)[:, 0:1], ALU.pow).then_inc(rstd_done, 1)

        @block.scalar
        def _(act):
            act.dma_start(self.cS[:, 0, :], a["c_prompt"].rearrange("c (p k) -> p (c k)", k=KC)).then_inc(c_in, 16)
            act.dma_start(self.cS[:, 1:9, :], a["c_sample"].rearrange("c (p k) -> p c k", k=KC)).then_inc(c_in, 16)
            act.wait_ge(c_in, 32)
            act.activation(self.cS, self.cS, ACT.Silu).then_inc(silu_c, 1)
            act.wait_ge(self.ring_full[ADA[0][1]], 16)
            for j in range(4):
                src = a["b_ada"].rearrange("a (r j n) -> a j r n", r=3, j=4)[:, j]
                for r in range(3):
                    act.dma_start(self.bada[32 * j:32 * j + 9, r, :],
                                  src[0, r].partition_broadcast(9)).then_inc(g_in, 16)
            act.dma_start(L.at(L.CST, self.ncst), a["constants"]).then_inc(self.cst_in, 16)
            for t in range(NT):
                act.dma_start(xb[t][0:rows(t)], x_of[t]).then_inc(x_ins[t], 16)
            act.dma_start(gpre, a["g_pre_mix"].partition_broadcast(P)).then_inc(gpre_in, 16)
            act.dma_start(wsraw, a["sgu_ws"][0].rearrange("g t s -> t g s")).then_inc(ws_in, 16)
            for t in range(NT):
                n = rows(t)
                act.wait_ge(x_ins[t], 16)
                if t >= 2:
                    act.wait_ge(ssq_done, t - 1)
                act.activation(hb[t % 2][0:n], xb[t][0:n], ACT.Square, accum_out=self.ssq[0:n, t:t + 1]
                               ).then_inc(ssq_done, 1)
            self.mod_store_prompt(act, 0)
            act.wait_ge(self.mod_out, 16)
            act.dma_start(mp[0], self.mod[NS, D:2 * D].partition_broadcast(P)).then_inc(mod_in, 16)
            act.dma_start(mp[1], self.mod[NS, 0:D].partition_broadcast(P)).then_inc(mod_in, 16)
            act.sem_inc(mod_asked, 1)
            for t in range(NT):
                evac(act, t, 0, ev_a)

        @block.vector
        def _(dve):
            link = chain(dve, dchain)
            dve.wait_ge(g_in, 16 * 12)
            self.mod_evac(dve, 0)
            dve.wait_ge(self.cst_in, 16)
            dve.wait_ge(ws_in, 16)
            dve.tensor_tensor(wsraw, wsraw, L.cst("tril").unsqueeze(1).to_broadcast([P, H, P]),
                              ALU.mult).then_inc(ws_masked, 1)
            dve.wait_ge(ws_tr, 1)
            dve.tensor_copy(self.wmT, PS[:, 4:6, :].rearrange("p b (g t) -> p (b g) t", g=4)).then_inc(wmT_done, 1)
            dve.wait_ge(w8_done, 1)
            dve.tensor_tensor(self.w8, PS[0:NS, 6, 0:64].rearrange("p (g t) -> p g t", g=H).unsqueeze(2)
                              .to_broadcast([NS, H, SB, ST]),
                              L.cst("sameseq", NS).rearrange("p (b t) -> p b t", b=SB).unsqueeze(1)
                              .to_broadcast([NS, H, SB, ST]), ALU.mult).then_inc(self.w8_made, 1)
            dve.tensor_copy(self.bs8, PS[0:NS, 6, 64:72]).then_inc(self.w8_made, 1)
            dve.wait_ge(ssq_done, NT)
            dve.wait_ge(mod_in, 32)
            dve.wait_ge(gpre_in, 16)
            link(dve.scalar_tensor_tensor(mp[0], mp[0], 1.0, gpre, ALU.add, ALU.mult))
            for t in range(NT):
                n = rows(t)
                if t == 3:
                    dve.wait_ge(mod_in_s, 32)
                    dve.scalar_tensor_tensor(mp[2][0:NS], mp[2][0:NS], 1.0, gpre[0:NS], ALU.add, ALU.mult
                                             ).then_inc(dchain, 1)
                    link.count[0] += 1
                if t == 4:
                    dve.wait_ge(dchain, link.count[0])
                A, sh = (mp[0], mp[1]) if t < 4 else (mp[2], mp[3])
                dve.wait_ge(rstd_done, t + 1)
                if t >= 2:
                    dve.wait_ge(tr_done, t - 1)
                link(dve.scalar_tensor_tensor(hb[t % 2][0:n], xb[t][0:n], self.rstd[0:n, t:t + 1], A[0:n],
                                              ALU.mult, ALU.mult))
                dve.tensor_tensor(hb[t % 2][0:n], hb[t % 2][0:n], sh[0:n], ALU.add).then_inc(h_done, 1)
                if t >= 1:
                    evac(dve, t - 1, 1, ev_d)
            evac(dve, NT - 1, 1, ev_d)

        @block.tensor
        def _(pe):
            pe.wait_ge(silu_c, 1)
            self.ada_round(pe, 0)
            pe.wait_ge(self.cst_in, 16)
            pe.wait_ge(ws_masked, 1)
            for g in range(H):
                last = pe.transpose(PS[:, 4 + g // 4, (g % 4) * P:(g % 4 + 1) * P], wsraw[:, g, :], L.cst("ident"))
            last.then_inc(ws_tr, 1)
            pe.wait_ge(wmT_done, 1)
            pe.wait_ge(bs_in, 16)
            pe.matmul(PS[0:NS, 6, 0:64], L.cst("repeat", ST), self.wmT[0:ST, :, 0:ST], start=True, stop=True)
            pe.matmul(PS[0:NS, 6, 64:72], L.cst("repeat", ST), self.bsT[0:ST, :], start=True,
                      stop=True).then_inc(w8_done, 1)

    def tokens_h(self, pe, t):
        n = rows(t)
        pe.wait_ge(self.h_done, t + 1)
        if t:
            pe.wait_ge(self.ev_a, t)
            pe.wait_ge(self.ev_d, t)
        else:
            pe.wait_ge(self.w8_made, 2)
        for k in range(KC):
            last = pe.transpose(self.PS[:, 6 + k // 4, (k % 4) * P:(k % 4) * P + n],
                                self.hb[t % 2][0:n, k::KC], self.L.cst("ident", n)[:, 0:n])
        last.then_inc(self.tr_done, 1)

    def load_unit(self, sp, unit):
        kind, r, j, slot = unit
        w = self.a["w_ada"] if kind == "ada" else self.a["w_in"]
        col = 512 * (4 * r + j) if kind == "ada" else 512 * WIN_COL[WIN_ORDER[j]]
        dst = self.L.ring[slot].rearrange("p (k n) -> p k n", k=KC)
        sp.dma_start(dst, w[0, :, col:col + 512].rearrange("(p k) n -> p k n", k=KC)).then_inc(self.ring_full[slot], 16)

    def ada_round(self, pe, r):
        bank = 7
        w = [self.L.ring[s].rearrange("p (k n) -> p k n", k=KC) for s in ADA[r]]
        for j, s in enumerate(ADA[r]):
            pe.wait_ge(self.ring_full[s], 16 * fills("ada", r, j))
        if r:
            pe.wait_ge(self.mod_sb, 4 * r)
        for k in range(KC):
            for j, s in enumerate(ADA[r]):
                ins = pe.matmul(self.PS[32 * j:32 * j + 9, bank, :], self.cS[:, :, k], w[j][:, k, :],
                                start=k == 0, stop=k == KC - 1)
        ins.then_inc(self.ada_done, 1)

    def mod_evac(self, dve, r):
        dve.wait_ge(self.ada_done, r + 1)
        for j in range(4):
            q = slice(32 * j, 32 * j + 9)
            dve.tensor_tensor(self.modst[q, r, :], self.PS[q, 7, :], self.bada[q, r, :],
                              ALU.add).then_inc(self.mod_sb, 1)

    def mod_store_prompt(self, eng, r):
        eng.wait_ge(self.mod_sb, 4 * (r + 1))
        eng.dma_start(self.mod[NS, 2048 * r:2048 * (r + 1)].rearrange("(j n) -> j n", j=4),
                      self.modst[0:P:32, r, :]).then_inc(self.mod_out, 16)

    def mod_store_samples(self, eng, r):
        eng.wait_ge(self.mod_sb, 4 * (r + 1))
        for j in range(4):
            col = slice(512 * (4 * r + j), 512 * (4 * r + j + 1))
            eng.dma_start(self.mod[0:NS, col].rearrange("(b t) n -> b t n", t=ST),
                          self.modst[32 * j + 1:32 * j + 9, r, :].unsqueeze(1).to_broadcast([SB, ST, 512])
                          ).then_inc(self.mod_outs, 16)

    def project(self, block):
        nc, a, o, L, PS = self.nc, self.a, self.o, self.L, self.PS
        grp_done, evac_done, post_done, post_ev = (self.sem(n) for n in ("grp_done", "evac_done", "post_done",
                                                                         "post_evac"))
        bn_done, rs_done, vs_ready, u_done, k_out, v_out, vs_out, ln_in = (
            self.sem(n) for n in ("bn_done", "rs_done", "vs_ready", "u_done", "k_out", "v_out", "vs_out", "ln_in"))
        dchain, pchain = self.sem("dve_chain_b"), self.sem("pool_chain_b")
        lam_in, lam_sum, lam_exp = (self.sem(n) for n in ("lam_in", "lam_sum", "lam_exp"))
        self.grp_done, self.evac_done, self.post_ev, self.posts = grp_done, evac_done, post_ev, 3 * NT
        summed = self.sem("summed")
        half = L.mix[0:NS, 3, 0:512]
        lam = self.lam
        self.dist_bias = L.at(L.MP, 4096).rearrange("p (h n) -> p h n", h=H)
        k_outs = [k_out] + [self.sem(f"k_out{i}") for i in range(1, 4)]
        E = [L.at(L.X + 512 * i, 512) for i in range(4)]
        lng, lnb = L.at(L.V + 1536, 512), L.at(L.V + 2048, 512)
        groups = [(c, t) for c in WIN_ORDER for t in range(NT)]
        posts = [n for n, (c, t) in enumerate(groups) if c in "skq"]
        mv = self.stats[:, 8:10]
        k_o = [o["k_prompt"][0, 0, t * P:(t + 1) * P].rearrange("t h d -> t (h d)") for t in range(4)] + \
            [o["k_sample"][0].rearrange("b t h d -> (b t) (h d)")]
        v_o = [o["v_prompt"][0, 0, t * P:(t + 1) * P].rearrange("t h d -> t (h d)") for t in range(4)] + \
            [o["v_sample"][0].rearrange("b t h d -> (b t) (h d)")]

        def posts_to(n):
            return sum(m <= n for m in posts)

        @block.sync
        def _(sp):
            for u in STATIC[6:]:
                before = [x for x in STATIC[:STATIC.index(u)] if x[3] == u[3]][-1]
                if before[0] == "win":
                    sp.wait_ge(grp_done, NT * (before[2] + 1))
                else:
                    sp.wait_ge(self.ada_done, before[1] + 1)
                self.load_unit(sp, u)
            for r in (1, 2):
                self.mod_store_prompt(sp, r)
                self.mod_store_samples(sp, r)
            sp.wait_ge(self.mod_out, 16 * 3)
            sp.wait_ge(self.mod_outs, 16 * 12)

        @block.gpsimd
        def _(pool):
            link = chain(pool, pchain)
            for i, n in enumerate(("lam_q1", "lam_k1", "lam_q2", "lam_k2")):
                pool.dma_start(self.lam[:, 32 * i:32 * i + 32], a[n].partition_broadcast(P)).then_inc(lam_in, 16)
            pool.dma_start(self.gsub, a["g_subln"].partition_broadcast(P)).then_inc(lam_in, 16)
            with nc.allow_non_contiguous_dma(reason="128 page numbers, once"):
                for g in range(NPAGE // 2):
                    pool.dma_start(self.ints[PAGEROWS * g:PAGEROWS * (g + 1), 64:80],
                                   a["page_table"].rearrange("b (h g) -> g (b h)", h=2)[g].partition_broadcast(
                                       PAGEROWS)).then_inc(self.pages_in, 16)
            pool.dma_start(lng, a["sgu_ln_g"].partition_broadcast(P)).then_inc(ln_in, 16)
            pool.dma_start(lnb, a["sgu_ln_b"].partition_broadcast(P)).then_inc(ln_in, 16)
            for t in range(NT):
                n = rows(t)
                pool.wait_ge(bn_done, t + 1)
                link(pool.tensor_scalar(self.stats[0:n, 10:11], self.stats[0:n, 9:10], 1.0, EPS, ALU.mult, ALU.add))
                pool.tensor_tensor(self.stats[0:n, 11:12], self.stats[0:n, 10:11], L.cst("half", n)[:, 0:1],
                                   ALU.pow).then_inc(rs_done, 1)
            pool.wait_ge(vs_ready, 4)
            pool.dma_start(o["sgu_prompt"][0, 0], E[3]).then_inc(vs_out, 16)
            pool.wait_ge(vs_ready, 5)
            pool.dma_start(o["sgu_sample"][0].rearrange("b t n -> (b t) n"), E[0][0:NS]).then_inc(vs_out, 16)

        @block.scalar
        def _(act):
            for n, (c, t) in enumerate(groups):
                r = rows(t)
                if c == "k" and t == 0:
                    act.wait_ge(lam_sum, 1)
                    act.activation(self.lam[:, 130:132], self.lam[:, 128:130], ACT.Exp).then_inc(lam_exp, 1)
                act.wait_ge(grp_done, n + 1)
                if t == 4:
                    act.wait_ge(summed, n // NT + 1)
                src = PS[0:r, n % 4, :]
                if n >= 4:
                    cb, tb = groups[n - 4]
                    if cb in "skq":
                        act.wait_ge(post_done, posts_to(n - 4))
                    if cb == "s" and tb >= 3:
                        act.wait_ge(vs_out, 32)
                    if cb == "u":
                        act.wait_ge(u_done, tb + 1)
                    if cb == "k":
                        act.wait_ge(k_outs[n % 4], 16 * sum(groups[m][0] == "k" for m in range(n % 4, n, 4)))
                if c in "su":
                    act.activation(E[n % 4][0:r], src, ACT.Gelu_apprx_tanh).then_inc(evac_done, 1)
                elif c == "v":
                    if t == 0:
                        act.wait_ge(post_done, NT)
                    act.activation(L.v[0:r, t, :], src, ACT.Copy).then_inc(evac_done, 1)
                    act.wait_ge(evac_done, n + 1)
                    act.dma_start(v_o[t], L.v[0:r, t, :]).then_inc(v_out, 16)
                else:
                    act.activation(E[n % 4][0:r], src, ACT.Copy,
                                   scale=DQK ** -0.5 if c == "q" else 1.0).then_inc(evac_done, 1)
                    if c == "k":
                        act.wait_ge(evac_done, n + 1)
                        act.dma_start(k_o[t], E[n % 4][0:r]).then_inc(k_outs[n % 4], 16)
            act.wait_ge(v_out, 16 * NT)
            for i in range(4):
                act.wait_ge(k_outs[i], 16 * sum(c == "k" and m % 4 == i for m, (c, _) in enumerate(groups)))

        @block.vector
        def _(dve):
            link = chain(dve, dchain)

            def post(m):
                c, t = groups[m]
                r, i = rows(t), posts_to(m) - 1
                dve.wait_ge(post_done, i + 1)
                if c == "s" and t == 4:
                    dve.wait_ge(self.w8_made, 2)
                bank = PS[:, 4 + i % 2, :]
                if c == "s":
                    bias = self.bsT if t < 4 else self.bs8
                    dve.tensor_tensor(L.mix[0:r, t, 512:].rearrange("p (g n) -> p g n", g=H),
                                      bank[0:r].rearrange("p (g n) -> p g n", g=H),
                                      bias[0:r].unsqueeze(2).to_broadcast([r, H, 64]), ALU.add).then_inc(post_ev, 1)
                else:
                    dst = L.kT if c == "k" else L.qT
                    dve.tensor_copy(dst[:, :, t * P:t * P + r],
                                    bank.rearrange("p (h t) -> p h t", h=HP)[:, :, 0:r]).then_inc(post_ev, 1)

            dve.wait_ge(self.pages_in, 16 * NPAGE // 2)
            link(dve.tensor_copy(self.row_f, self.ints[:, 64:80]))
            link(dve.scalar_tensor_tensor(self.row_f, self.row_f, float(PAGEROWS),
                                          L.cst("pagerow").to_broadcast([P, 16]), ALU.mult, ALU.add))
            link(dve.tensor_copy(self.ints[:, 64:80], self.row_f))
            dve.wait_ge(ln_in, 32)
            for n, (c, t) in enumerate(groups):
                r = rows(t)
                e = E[n % 4][0:r]
                if t == 4:
                    dve.wait_ge(grp_done, n + 1)
                    link(dve.tensor_copy(half, PS[NS:P, n % 4, :]))
                    dve.tensor_tensor(PS[0:NS, n % 4, :], PS[0:NS, n % 4, :], half, ALU.add).then_inc(summed, 1)
                if c == "s":
                    dve.wait_ge(evac_done, n + 1)
                    link(dve.bn_stats(self.stats[0:r, 0:6], e))
                    dve.bn_aggr(mv[0:r], self.stats[0:r, 0:6]).then_inc(bn_done, 1)
                    dve.wait_ge(rs_done, t + 1)
                    link(dve.tensor_scalar(e, e, mv[0:r, 0:1], self.stats[0:r, 11:12], ALU.subtract, ALU.mult))
                    link(dve.tensor_tensor(e, e, lng[0:r], ALU.mult))
                    dve.tensor_tensor(e, e, lnb[0:r], ALU.add).then_inc(vs_ready, 1)
                elif c == "u":
                    if t == 0:
                        post(n - 1)
                        dve.wait_ge(post_ev, NT)
                    dve.wait_ge(evac_done, n + 1)
                    dve.tensor_tensor(L.mix[0:r, t, 512:], e, L.mix[0:r, t, 512:], ALU.mult).then_inc(u_done, 1)
                elif c == "v" and t == 0:
                    for h in range(H):
                        last = dve.tensor_scalar_mul(self.dist_bias[:, h, :], L.cst("dist"), -2.0 ** -(h + 1))
                    link(last)
                    dve.wait_ge(lam_in, 80)
                    for j in range(2):
                        last = dve.tensor_tensor_reduce(out=L.mix[:, j, 0:32], in0=lam[:, 64 * j:64 * j + 32],
                                                        in1=lam[:, 64 * j + 32:64 * j + 64], scale=1.0, scalar=0.0,
                                                        op0=ALU.mult, op1=ALU.add, accum_out=lam[:, 128 + j:129 + j])
                    last.then_inc(lam_sum, 1)
                    link(dve.tensor_scalar_mul(self.gsub, self.gsub, 1.0 - LAM_INIT))
                elif c == "k" and t == 1:
                    dve.wait_ge(lam_exp, 1)
                    link(dve.tensor_tensor(lam[:, 132:133], lam[:, 130:131], lam[:, 131:132], ALU.subtract))
                    link(dve.tensor_scalar(lam[:, 133:134], lam[:, 132:133], -1.0, -LAM_INIT, ALU.mult, ALU.add))
                if (c, t) in ADA_AFTER:
                    self.mod_evac(dve, ADA_AFTER.index((c, t)) + 1)
                if n - 1 in posts and not (c == "u" and t == 0):
                    post(n - 1)
            post(len(groups) - 1)

        @block.tensor
        def _(pe):
            def post(m):
                c, t = groups[m]
                r, i = rows(t), posts_to(m) - 1
                if i >= 2:
                    pe.wait_ge(post_ev, i - 1)
                bank = PS[:, 4 + i % 2, :]
                if c == "s":
                    pe.wait_ge(vs_ready, t + 1)
                    if t == 4:
                        pe.wait_ge(self.w8_made, 2)
                    for g in range(H):
                        w = self.wmT[:, g, :] if t < 4 else self.w8[:, g, :, :]
                        w = w.rearrange("p b t -> p (b t)") if t == 4 else w
                        for c in COLS[:-(-r // 64)]:
                            last = pe.matmul(bank[c:c + 64, 64 * g:64 * g + 64], w[:, c:c + 64],
                                             E[m % 4][0:r, 64 * g:64 * g + 64], start=True, stop=True)
                else:
                    pe.wait_ge(evac_done, m + 1)
                    for h in range(HP):
                        last = pe.transpose(bank[:, P * h:P * h + r], E[m % 4][0:r, P * h:P * h + P],
                                            L.cst("ident", r)[:, 0:r])
                last.then_inc(post_done, 1)

            self.tokens_h(pe, 0)
            for n, (c, t) in enumerate(groups):
                r = rows(t)
                slot = WIN[n // NT]
                if c == "s":
                    if t + 1 < NT:
                        self.tokens_h(pe, t + 1)
                    pe.wait_ge(self.ev_a, t + 1)
                    pe.wait_ge(self.ev_d, t + 1)
                if t == 0:
                    pe.wait_ge(self.ring_full[slot], 16 * fills("win", 0, n // NT))
                if n >= 4:
                    pe.wait_ge(evac_done, n - 3)
                w = L.ring[slot].rearrange("p (k n) -> p k n", k=KC)
                if t < 4:
                    for k in range(KC):
                        last = pe.matmul(PS[:, n % 4, :], L.hT[:, k, t * P:t * P + P], w[:, k, :],
                                         start=k == 0, stop=k == KC - 1)
                else:
                    for k in range(KC // 2):
                        for c0, kk in ((0, k), (NS, k + KC // 2)):
                            last = pe.matmul(PS[c0:c0 + NS, n % 4, :], L.hT[:, kk, SEQ:TOK], w[:, kk, :],
                                             start=k == 0, stop=k == KC // 2 - 1)
                last.then_inc(grp_done, 1)
                if n >= 3 and groups[n - 3][0] == "s":
                    post(n - 3)
                if n - 1 in posts and groups[n - 1][0] != "s":
                    post(n - 1)
                if (c, t) in ADA_AFTER:
                    self.ada_round(pe, ADA_AFTER.index((c, t)) + 1)
            post(len(groups) - 1)


    def load_pages(self, pool, cache, b, half, slot, k):
        index = self.ints[:, 80 + slot:81 + slot]
        pool.tensor_copy(index, self.ints[:, bass.ds(64 + 2 * b + half, 1)]).then_inc(self.staged, 1)
        pool.wait_ge(self.staged, k + 1)
        self.stand_apart(pool)
        pool.indirect_dma_start(self.L.ring[slot], None, cache,
                                bass.IndirectOffsetOnAxis(ap=index, axis=0)).then_inc(self.pages_full[slot], 16)

    def head_norm(self, dve, link, o, sq, ss, dst, r, need, give, k):
        heads = o.rearrange("p (h d) -> p h d", h=H)
        link(dve.tensor_tensor(sq, o, o, ALU.mult))
        dve.tensor_reduce(ss[0:r], sq.rearrange("p (h d) -> p h d", h=H), AX, ALU.add).then_inc(need, 1)
        dve.wait_ge(give, k)
        link(dve.tensor_tensor(heads, heads, ss[0:r].unsqueeze(2).to_broadcast([r, H, DV]), ALU.mult))
        return dve.tensor_tensor(dst.rearrange("p (h d) -> p h d", h=H), heads,
                                 self.gsub[0:r].unsqueeze(1).to_broadcast([r, H, DV]), ALU.mult)

    def power(self, pool, link, ss, n, r, scale, done):
        link(pool.tensor_scalar(ss[0:r], ss[0:r], scale, EPS, ALU.mult, ALU.add))
        pool.tensor_tensor(ss[0:r], ss[0:r], self.L.cst("half", r)[:, 0:n], ALU.pow).then_inc(done, 1)

    def attend_prompt(self, block):
        nc, a, L, PS = self.nc, self.a, self.L, self.PS
        (s_done, s_read, m_ready, exp_done, a_ready, t_done, at_done, pv_done, o_read, ss_ready, ss_power) = (
            self.sem("c_" + n) for n in ("scores", "scores_read", "max", "exp", "weights", "transposed", "evacuated",
                                         "pv", "o_read", "ss_ready", "ss_power"))
        dchain, pchain, zeroed = self.sem("dve_chain_c"), self.sem("pool_chain_c"), self.sem("c_zeroed")
        n0 = L.X
        pb = [[L.at(n0 + 4096 + 1024 * i + 512 * j, 512) for j in range(2)] for i in range(3)]
        at = [L.at(n0 + 7168 + 512 * i, 512).rearrange("p (b q) -> p b q", b=4) for i in range(2)]
        osb, sq = L.at(n0 + 8192, 512), L.at(n0 + 8704, 512)
        ss = self.stats[:, 16:24]
        mx, nm, sums, cf, r1 = (L.at(n0 + 9216 + 64 * i, 64) for i in range(5))
        qz = [L.at(n0 + 2048 * i, 2048).rearrange("p (h g q) -> p h g q", h=HP, g=4) for i in range(2)]
        q_zero = self.sem("c_q_zero")
        lam = self.lam
        work = [(i, h) for i in range(4) for h in range(H)]
        N = len(work)

        @block.gpsimd
        def _(pool):
            link = chain(pool, pchain)
            pool.wait_ge(self.ada_done, 3)
            pool.wait_ge(self.grp_done, 5 * NT)
            for k, (cache, b, slots) in enumerate(((self.ck, 0, K_SLOT[0]), (self.ck, 1, K_SLOT[1]),
                                                   (self.cv, 0, V_SLOT))):
                for half in range(2):
                    self.load_pages(pool, cache, b, half, slots[half], 2 * k + half)
            link(pool.memset(L.mix[:, 4, 0:512], 0.0))
            pool.dma_start(self.y_rows[MAIN * P:].rearrange("(p r) (c n) -> p (r c) n", p=P, n=512),
                           L.mix[:, 4:5, 0:512].to_broadcast([P, 2 * OVER, 512])).then_inc(zeroed, 16)
            for i in range(4):
                pool.wait_ge(ss_ready, i + 1)
                self.power(pool, link, ss, H, P, 1.0 / DV, ss_power)
            pool.wait_ge(zeroed, 16)

        @block.scalar
        def _(act):
            def place_q(i):
                if i >= 2:
                    act.wait_ge(s_done, 2 * H * (i - 1))
                for g in range(4):
                    act.activation(qz[i % 2][:, :, g, :], L.qT[:, :, P * i:P * i + P], ACT.Copy,
                                   scale=L.cst("group")[:, g:g + 1]).then_inc(q_zero, 1)

            act.wait_ge(self.post_ev, self.posts)
            act.wait_ge(self.mod_out, 16 * 3)
            act.wait_ge(self.mod_outs, 16 * 12)
            place_q(0)
            for n in range(N + 2):
                if n < N:
                    act.wait_ge(m_ready, n + 1)
                    w = P * (work[n][0] + 1)
                    for j in range(2):
                        q = 2 * n + j
                        act.activation(pb[n % 3][j][:, 0:w], pb[n % 3][j][:, 0:w], ACT.Exp, bias=nm[:, q:q + 1],
                                       accum_out=sums[:, q:q + 1]).then_inc(exp_done, 1)
                if n % H == 3 and n // H < 3:
                    place_q(n // H + 1)
                if n >= 2:
                    m = n - 2
                    i, h = work[m]
                    act.wait_ge(t_done, m + 1)
                    if m >= 2:
                        act.wait_ge(pv_done, m - 1)
                    act.activation(at[m % 2][:, 0:i + 1, :],
                                   PS[:, 4 + m % 2, 0:P * (i + 1)].rearrange("p (b q) -> p b q", q=P),
                                   ACT.Copy).then_inc(at_done, 1)

        @block.vector
        def _(dve):
            link = chain(dve, dchain)
            dve.wait_ge(self.mod_out, 16 * 3)
            dve.wait_ge(self.mod_outs, 16 * 12)

            def weights(m):
                w, q = P * (work[m][0] + 1), 2 * m
                p1, p2 = pb[m % 3][0][:, 0:w], pb[m % 3][1][:, 0:w]
                dve.wait_ge(exp_done, 2 * m + 2)
                link(dve.reciprocal(cf[:, q:q + 1], sums[:, q + 1:q + 2]))
                link(dve.scalar_tensor_tensor(cf[:, q:q + 1], sums[:, q:q + 1], lam[:, 133:134], cf[:, q:q + 1],
                                              ALU.mult, ALU.mult))
                dve.scalar_tensor_tensor(p1, p2, cf[:, q:q + 1], p1, ALU.mult, ALU.add).then_inc(a_ready, 1)

            def finish(i):
                dve.wait_ge(pv_done, H * (i + 1))
                l1 = sums[:, 16 * i:16 * i + 16].rearrange("p (h j) -> p h j", j=2)[:, :, 0]
                link(dve.reciprocal(r1[:, 0:H], l1))
                dve.tensor_tensor(osb.rearrange("p (h d) -> p h d", h=H),
                                  PS[:, 6 + i % 2, :].rearrange("p (h d) -> p h d", h=H),
                                  r1[:, 0:H].unsqueeze(2).to_broadcast([P, H, DV]), ALU.mult).then_inc(o_read, 1)
                dve.wait_ge(o_read, i + 1)
                self.head_norm(dve, link, osb, sq, ss, L.mix[:, i, 0:512], P, ss_ready, ss_power, i + 1)

            for n in range(N + 1):
                if n < N:
                    i, h = work[n]
                    w, q = P * (i + 1), 2 * n
                    if n >= 3:
                        dve.wait_ge(t_done, n - 2)
                    for j in range(2):
                        dve.wait_ge(s_done, 2 * n + j + 1)
                        dve.tensor_tensor_reduce(out=pb[n % 3][j][:, 0:w], in0=PS[:, 2 * (n % 2) + j, 0:w],
                                                 in1=self.dist_bias[:, h, 384 - P * i:512], scale=1.0, scalar=-3e38,
                                                 op0=ALU.add, op1=ALU.max,
                                                 accum_out=mx[:, q + j:q + j + 1]).then_inc(s_read, 1)
                    dve.wait_ge(s_read, 2 * n + 2)
                    dve.tensor_scalar_mul(nm[:, q:q + 2], mx[:, q:q + 2], -1.0).then_inc(m_ready, 1)
                if n >= 1:
                    weights(n - 1)
                if n % H == 4 and n // H >= 1:
                    finish(n // H - 1)
            finish(3)

        @block.tensor
        def _(pe):
            pe.wait_ge(self.evac_done, 5 * NT)
            pe.wait_ge(self.post_ev, self.posts)
            pe.wait_ge(self.mod_sb, 12)
            for n in range(N + 3):
                if n < N:
                    i, h = work[n]
                    if n >= 2:
                        pe.wait_ge(s_read, 2 * (n - 1))
                    if h == 0:
                        pe.wait_ge(q_zero, 4 * (i + 1))
                    for j in range(2):
                        pe.matmul(PS[:, 2 * (n % 2) + j, 0:P * (i + 1)], qz[i % 2][:, h // 2, 2 * (h % 2) + j, :],
                                  L.kT[:, h // 2, 0:P * (i + 1)], start=True, stop=True).then_inc(s_done, 1)
                if 2 <= n < N + 2:
                    m = n - 2
                    pe.wait_ge(a_ready, m + 1)
                    if m >= 2:
                        pe.wait_ge(at_done, m - 1)
                    for b in range(work[m][0] + 1):
                        last = pe.transpose(PS[:, 4 + m % 2, P * b:P * b + P], pb[m % 3][0][:, P * b:P * b + P],
                                            L.cst("ident"))
                    last.then_inc(t_done, 1)
                if n >= 3:
                    m = n - 3
                    i, h = work[m]
                    pe.wait_ge(at_done, m + 1)
                    if h == 0 and i >= 2:
                        pe.wait_ge(o_read, i - 1)
                    for c in COLS:
                        for b in range(i + 1):
                            last = pe.matmul(PS[c:c + 64, 6 + i % 2, DV * h:DV * h + DV],
                                             at[m % 2][:, b, c:c + 64],
                                             L.v[:, b, DV * h:DV * h + DV], start=b == 0, stop=b == i)
                    last.then_inc(pv_done, 1)

    def attend_sample(self):
        nc, a, L, PS = self.nc, self.a, self.L, self.PS
        names = ("k_tr", "kt_act", "kt_dve", "scores", "s_read", "q_st", "max", "exp", "coef", "pt", "at_act",
                 "at_dve", "pv", "o_hi", "o_lo", "o_ready", "past_in")
        (k_tr, kt_act, kt_dve, s_done, s_read, q_st, m_ready, exp_done, c_ready, pt_done, at_act, at_dve, pv_done,
         o_hi, o_lo, o_ready, past_in) = (self.sem("d_" + n) for n in names)
        o_out = [self.sem("d_o_out0"), self.sem("d_o_out1")]
        dchain, own_st, rs_done, o_own = (self.sem("d_" + n) for n in ("setup", "own_st", "reciprocal", "o_own"))
        n0 = L.X
        past = L.at(n0, PAST)
        S = [L.at(n0 + 2048 + 2112 * i, 2112) for i in range(2)]
        kt = [L.at(n0 + 6272 + 2048 * i, 2048).rearrange("p (h n) -> p h n", h=HP) for i in range(2)]
        at = L.at(n0 + 10368, 17 * NS).rearrange("p (g n) -> p g n", g=17)
        osb = L.at(n0 + 11456, 256, 0, NS)
        osum = L.at(n0 + 11712, 256, 0, NS).rearrange("p (g d) -> p g d", g=4)
        om = [L.at(n0 + 11968 + DV * i, DV, 0, NS) for i in range(2)]
        coef = [L.at(n0 + 12096 + NS * i, NS) for i in range(2)]
        base = L.at(n0 + 12224, NS)
        qst = [L.at(n0 + 12288 + P * i, P).rearrange("p (h n) -> p h n", h=HP) for i in range(2)]
        own = L.at(n0 + 12544, NS)
        qbd = L.at(n0 + 12608, SB * P).rearrange("p (b h g t) -> p b h g t", b=SB, h=HP, g=4)
        mx, nm, sums, rs = self.stats[:, 0:5], self.stats[:, 8:10], self.stats[:, 10:12], self.stats[:, 12:14]

        with nc.Block() as block:
            def looped(eng, step):
                step(0, 0, True, False)
                step(1, 1, True, True)
                step(2, 0, True, True)
                with eng.Fori(0, SB // 2 - 2) as i:
                    step(2 * i + 3, 1, True, True)
                    step(2 * i + 4, 0, True, True)
                step(SB - 1, 1, True, True)
                step(SB, 0, False, True)

            @block.sync
            def _(sp):
                sp.wait_ge(k_tr, 16 * (SB - 1))
                for c in range(2):
                    sp.dma_start(L.ring[W_OUT[c]].rearrange("p (k n) -> p k n", k=KC),
                                 a["w_out"][0, :, 512 * c:512 * c + 512].rearrange("(p k) n -> p k n", k=KC)
                                 ).then_inc(self.ring_full[W_OUT[c]], 16)

            @block.gpsimd
            def _(pool):
                def refill(b, par, k, count):
                    if k:
                        for half in range(2):
                            pool.wait_ge(k_tr, 16 * b + 8 * half + 8)
                            self.load_pages(pool, self.ck, b + 2, half, K_SLOT[par][half], count + half)
                    if differs(b, 0):
                        for half in range(2):
                            if half == 0:
                                pool.wait_ge(pv_done, b)
                            if differs(b, SB):
                                self.load_pages(pool, self.cv, b, half, V_SLOT[half], count + (2 if k else 0) + half)
                        pool.wait_ge(o_ready, b)
                        self.stand_apart(pool)
                        pool.dma_start(self.o_sample[bass.ds(b - 1, 1)].rearrange("a r d -> r (a d)"),
                                       om[1 - par]).then_inc(o_out[1 - par], 16)

                refill(0, 0, True, 6)
                with pool.Fori(0, 2) as i:
                    refill(2 * i + 1, 1, True, 8 * i + 8)
                    refill(2 * i + 2, 0, True, 8 * i + 12)
                refill(5, 1, True, 24)
                refill(6, 0, False, 28)
                refill(7, 1, False, 30)
                refill(8, 0, False, 32)
                pool.wait_ge(o_out[0], 16 * 4)
                pool.wait_ge(o_out[1], 16 * 4)

            @block.scalar
            def _(act):
                act.dma_start(past, a["past_bias"]).then_inc(past_in, 16)

                def evac(b, ch):
                    for h in range(2):
                        act.wait_ge(k_tr, 16 * b + 4 * ch + h + 1)
                        if ch >= 2:
                            act.wait_ge(s_done, 5 * b + ch - 1)
                        elif differs(b, 0):
                            act.wait_ge(s_done, 5 * b - 2 + ch)
                        act.activation(kt[ch % 2][:, h, :], PS[:, h, :], ACT.Copy).then_inc(kt_act, 1)

                def step(b, par, keys, vals):
                    f = b - 1
                    if keys:
                        evac(b, 0)
                        evac(b, 1)
                        evac(b, 2)
                    if vals:
                        act.wait_ge(pt_done, 3 * f + 1)
                        if differs(f, 0):
                            act.wait_ge(pv_done, f)
                        act.activation(at[:, 0:8, :], PS[:, 6, :].rearrange("p (g n) -> p g n", g=8),
                                       ACT.Copy).then_inc(at_act, 1)
                    if keys:
                        evac(b, 3)
                    if vals:
                        act.wait_ge(pt_done, 3 * f + 3)
                        act.activation(at[0:NS, 16, :], PS[0:NS, 6, 0:NS], ACT.Copy).then_inc(at_act, 1)
                        act.wait_ge(pv_done, f + 1)
                        act.activation(osb, PS[NS:P, 7, 0:256], ACT.Copy).then_inc(o_hi, 1)
                    if keys:
                        act.wait_ge(m_ready, b + 1)
                        act.activation(S[par], S[par], ACT.Exp, bias=nm[:, par:par + 1],
                                       accum_out=sums[:, par:par + 1]).then_inc(exp_done, 1)
                looped(act, step)

            @block.vector
            def _(dve):
                for h in range(HP):
                    last = dve.tensor_tensor(qbd[:, :, h, :, :],
                                             L.qT[:, h, SEQ:TOK].rearrange("p (b t) -> p b t", b=SB).unsqueeze(2)
                                             .to_broadcast([P, SB, 4, ST]),
                                             L.cst("group").unsqueeze(1).unsqueeze(3).to_broadcast([P, SB, 4, ST]),
                                             ALU.mult)
                last = dve.scalar_tensor_tensor(base, L.cst("sel2"), self.lam[:, 133:134], L.cst("sel1"),
                                                ALU.mult, ALU.add)
                last.then_inc(dchain, 1)
                dve.wait_ge(dchain, 1)

                def evac(b, ch):
                    for h in (2, 3):
                        dve.wait_ge(k_tr, 16 * b + 4 * ch + h + 1)
                        if ch >= 2:
                            dve.wait_ge(s_done, 5 * b + ch - 1)
                        elif differs(b, 0):
                            dve.wait_ge(s_done, 5 * b - 2 + ch)
                        dve.tensor_copy(kt[ch % 2][:, h, :], PS[:, h, :]).then_inc(kt_dve, 1)

                def bias_max(b, ch, par):
                    n = 512 if ch < 4 else NS
                    dve.wait_ge(s_done, 5 * b + ch + 1)
                    self.stand_apart(dve)
                    dve.tensor_tensor_reduce(out=S[par][:, 512 * ch:512 * ch + n],
                                             in0=PS[:, 4 + (par + ch) % 2, 0:n],
                                             in1=past[:, 512 * ch:512 * ch + n] if ch < 4 else own,
                                             scale=1.0, scalar=-3e38, op0=ALU.add, op1=ALU.max,
                                             accum_out=mx[:, ch:ch + 1]).then_inc(s_read, 1)

                dve.wait_ge(past_in, 16)

                def step(b, par, keys, vals):
                    f = b - 1
                    if keys:
                        if differs(b, 0) and differs(b, 1):
                            dve.wait_ge(s_done, 5 * b - 5)
                        dve.tensor_copy(qst[par], qbd[:, bass.ds(b, 1)].rearrange("p b h g t -> p (b h) (g t)")
                                        ).then_inc(q_st, 1)
                        if differs(b, 0):
                            dve.wait_ge(s_read, 5 * b)
                        dve.tensor_copy(own, L.cst("own")[:, bass.ds(56 - ST * b, NS)]).then_inc(own_st, 1)
                    if vals:
                        dve.wait_ge(exp_done, f + 1)
                        dve.reciprocal(rs[:, 1 - par:2 - par], sums[:, 1 - par:2 - par]).then_inc(rs_done, 1)
                        dve.wait_ge(rs_done, f + 1)
                        if differs(f, 0) and differs(f, 1):
                            dve.wait_ge(pt_done, 3 * (f - 1))
                        dve.tensor_scalar_mul(coef[1 - par], base, rs[:, 1 - par:2 - par]).then_inc(c_ready, 1)
                    if keys:
                        evac(b, 0)
                        evac(b, 1)
                        if not isinstance(b, int) or b >= 2:
                            dve.wait_ge(pt_done, 3 * (b - 1))
                        bias_max(b, 0, par)
                        evac(b, 2)
                        bias_max(b, 1, par)
                        evac(b, 3)
                        bias_max(b, 2, par)
                    if vals:
                        dve.wait_ge(pt_done, 3 * f + 2)
                        if differs(f, 0):
                            dve.wait_ge(pv_done, f)
                        dve.tensor_copy(at[:, 8:16, :], PS[:, 6, :].rearrange("p (g n) -> p g n", g=8)
                                        ).then_inc(at_dve, 1)
                    if keys:
                        bias_max(b, 3, par)
                        dve.wait_ge(own_st, b + 1)
                        bias_max(b, 4, par)
                        dve.wait_ge(s_read, 5 * b + 5)
                        dve.tensor_reduce(nm[:, par:par + 1], mx, AX, ALU.max, negate=True).then_inc(m_ready, 1)
                    if vals:
                        dve.wait_ge(o_hi, f + 1)
                        dve.wait_ge(pv_done, f + 1)
                        dve.tensor_tensor(osum.rearrange("p g d -> p (g d)"), PS[0:NS, 7, 0:256], osb,
                                          ALU.add).then_inc(o_lo, 1)
                        dve.wait_ge(o_lo, f + 1)
                        dve.tensor_tensor(osum, osum, L.cst("diag", NS).unsqueeze(2).to_broadcast([NS, 4, DV]),
                                          ALU.mult).then_inc(o_own, 1)
                        dve.wait_ge(o_own, f + 1)
                        if not isinstance(f, int) or f >= 2:
                            dve.wait_ge(o_out[1 - par], 8 * (f - (1 - par)))
                        dve.tensor_reduce(om[1 - par], osum.rearrange("p g d -> p d g"), AX, ALU.add
                                          ).then_inc(o_ready, 1)
                looped(dve, step)

            @block.tensor
            def _(pe):
                def transposes(b, ch, par):
                    slot = K_SLOT[par][ch // 2]
                    if ch % 2 == 0:
                        pe.wait_ge(self.pages_full[slot], 16 + 8 * (b - par))
                    kp = L.ring[slot].rearrange("p (g n) -> p g n", g=NPAGE // 2)
                    for h in range(HP):
                        done = kt_act if h < 2 else kt_dve
                        if ch or differs(b, 0):
                            pe.wait_ge(done, 2 * (4 * b + ch) - 1 + h % 2)
                        for g in range(4):
                            last = pe.transpose(PS[:, h, P * g:P * g + P], kp[:, 4 * (ch % 2) + g, P * h:P * h + P],
                                                L.cst("ident"))
                        last.then_inc(k_tr, 1)

                def scores(b, ch, par):
                    bank = PS[:, 4 + (par + ch) % 2, :]
                    if ch < 4:
                        pe.wait_ge(kt_act, 2 * (4 * b + ch + 1))
                        pe.wait_ge(kt_dve, 2 * (4 * b + ch + 1))
                    if ch >= 2 or differs(b, 0):
                        pe.wait_ge(s_read, 5 * b + ch - 1)
                    for h in range(HP):
                        rhs = kt[ch % 2][:, h, :] if ch < 4 else L.kT[:, h, SEQ:TOK]
                        last = pe.matmul(bank[32 * h:32 * h + 32, 0:512 if ch < 4 else NS], qst[par][:, h, :], rhs,
                                         start=True, stop=True)
                    last.then_inc(s_done, 1)

                def weights(f, part, par):
                    if part:
                        pe.wait_ge(at_act if part == 1 else at_dve, 2 * f + 1 if part == 1 else f + 1)
                    else:
                        pe.wait_ge(c_ready, f + 1)
                        if differs(f, 0):
                            pe.wait_ge(at_act, 2 * f)
                    if part < 2:
                        for g in range(8):
                            page = 8 * part + g
                            for c in COLS:
                                last = pe.matmul(PS[c:c + 64, 6, NS * g:NS * g + NS],
                                                 S[par][:, P * page + c:P * page + c + 64], coef[par],
                                                 start=True, stop=True)
                    else:
                        last = pe.matmul(PS[0:NS, 6, 0:NS], S[par][:, PAST:PAST + NS], coef[par], start=True, stop=True)
                    last.then_inc(pt_done, 1)

                def values(f):
                    if differs(f, 0):
                        pe.wait_ge(o_lo, f)
                        pe.wait_ge(o_hi, f)
                    pe.wait_ge(at_act, 2 * f + 2)
                    pe.wait_ge(at_dve, f + 1)
                    for half in range(2):
                        pe.wait_ge(self.pages_full[V_SLOT[half]], 16 + 16 * f)
                        vp = L.ring[V_SLOT[half]].rearrange("p (g n) -> p g n", g=NPAGE // 2)
                        for g in range(NPAGE // 2):
                            page = half * 8 + g
                            for quad in range(2):
                                c = 64 * (g % 2) + 32 * quad
                                pe.matmul(PS[c:c + 32, 7, 0:256], at[:, page, 32 * quad:32 * quad + 32],
                                          vp[:, g, 256 * quad:256 * quad + 256], start=page < 2, stop=page == 15)
                    for quad in range(2):
                        last = pe.matmul(PS[32 * quad:32 * quad + 32, 7, 0:256], at[0:NS, 16, 32 * quad:32 * quad + 32],
                                         L.v[0:NS, 4, 256 * quad:256 * quad + 256], start=False, stop=True)
                    last.then_inc(pv_done, 1)

                def step(b, par, keys, vals):
                    f = b - 1
                    if keys:
                        transposes(b, 0, par)
                        transposes(b, 1, par)
                        pe.wait_ge(q_st, b + 1)
                        scores(b, 0, par)
                        transposes(b, 2, par)
                        scores(b, 1, par)
                    if vals:
                        weights(f, 0, 1 - par)
                    if keys:
                        transposes(b, 3, par)
                        scores(b, 2, par)
                    if vals:
                        weights(f, 1, 1 - par)
                    if keys:
                        scores(b, 3, par)
                    if vals:
                        weights(f, 2, 1 - par)
                    if keys:
                        scores(b, 4, par)
                    if vals:
                        values(f)
                looped(pe, step)


    def load_expert(self, sp, e, par, kind):
        w = self.a[("w_gate", "w_up", "w_down")[kind]][0]
        slot = EXPERT[par][kind]
        k = FC if kind == 2 else KC
        sp.dma_start(self.L.ring[slot], w[bass.ds(e, 1)].rearrange("a (p k) n -> p (a k n)", k=k)
                     ).then_inc(self.ring_full[slot], 16)

    def merge(self, block):
        nc, a, L, PS = self.nc, self.a, self.L, self.PS
        (o_in, ss_ready, ss_power, mix_ready, mod_in, tr_done, ev_a, ev_d, proj_done, sq1, rs1, x1_done,
         sq2, rs2, h2_done, h2_tr, h2_ev, log_done, log_read, h2_out, exp_in, exp_out, hot_done, rank_done,
         picks_done, table_done) = (
             self.sem("e_" + n) for n in (
                 "o_in", "ss_ready", "ss_power", "mix_ready", "mod_in", "tr", "ev_a", "ev_d", "proj",
                 "sq1", "rs1", "x1", "sq2", "rs2", "h2", "h2_tr", "h2_ev", "log", "log_read", "h2_out",
                 "exp_in", "exp_out", "hot", "rank", "picks", "table"))
        x_in = [self.sem(f"e_x_in{t}") for t in range(NT)]
        mod_in_s = self.sem("e_mod_in_samples")
        self.table_done = table_done
        h2_ev2 = self.sem("e_h2_ev_dve")
        h2_out2 = self.h2_outs = [h2_out, self.sem("e_h2_out1")]
        dchain, pchain = self.sem("dve_chain_e"), self.sem("pool_chain_e")
        mod = [L.at(L.MP + D * i, D) for i in range(6)]
        g_post, g_pre = L.at(L.QKT + 2048, D), L.at(L.QKT + 3072, D)
        sq = L.at(L.QKT + 4096, 512, 0, NS)
        hv = [L.at(L.V + D * i, D) for i in range(2)]
        osb = L.at(L.V + 2048, 512, 0, NS)
        mixT = [L.at(L.HT + D * i, D).rearrange("p (k t) -> p k t", k=KC) for i in range(2)]
        h2T = [L.at(L.HT + 2048 + D * i, D).rearrange("p (k t) -> p k t", k=KC) for i in range(2)]
        st = self.stats
        ss8, ss1, ss2 = st[:, 16:24], self.ssq, self.rstd
        x_of = [a["x_prompt"][0, t * P:(t + 1) * P, :] for t in range(4)] + \
            [a["x_sample"].rearrange("b t n -> (b t) n")]
        r0 = L.QKT + 4096
        buf = {}

        def take(name, n, base=[r0, L.HT + 4096]):
            room = buf.setdefault("", [0, 0])
            k = 0 if room[0] + n <= 512 else 1
            v = L.at(base[k] + room[k], n)
            room[k] += n
            assert room[k] <= 512
            return v

        t4 = lambda x: x.rearrange("p (t n) -> p t n", t=NT)
        eg, ee = t4(take("eg", 20)), t4(take("ee", 20))
        og, o1, o2 = (t4(take(n, 20)) for n in ("og", "o1", "o2"))
        gm, gs, rk = take("gm", 5), take("gs", 5), take("rk", 5)
        m12 = take("m12", 10).rearrange("p (t j) -> p t j", t=NT)
        ws = take("ws", 5)
        hot_all = take("hot", 256)
        hot = hot_all[:, 0:240].rearrange("p (j t e) -> p j t e", j=3, t=NT)
        both = hot_all[:, 160:256]
        prod = take("prod", 80).rearrange("p (t e) -> p t e", t=NT)
        over, ovpre, delta = take("over", 16), take("ovpre", 16), take("delta", 16)
        ovall = take("ovall", 256)
        slotf = take("slotf", 10).rearrange("p (t j) -> p t j", t=NT)
        eid = take("eid", OVER + 1)
        G = L.at(L.MIX, 10 * (NTILE + 1)).rearrange("p (n c) -> p n c", n=10)
        C = L.at(L.MIX + 256, 10 * NTILE).rearrange("p (n c) -> p n c", n=10)
        row, below = L.at(L.MIX + 500, 10), L.at(L.MIX + 512, 10)
        R = L.at(L.MIX + 640, 10 * P).rearrange("p (n r) -> p n r", n=10)

        self.ga_in = self.sem("e_ga_in")
        self.ga = [L.at(L.MIX + 2 * D + D * i, D) for i in range(3)]
        halves, summed = self.sem("e_halves"), self.sem("e_summed")
        half = L.mix[0:NS, 3, 0:512]
        RK = 128
        table_made = self.sem("e_table_made")

        def proj_bank(t, c):
            return 3 if c == 1 - t % 2 else (4 if c else 2)

        def proj(t, n):
            return PS[0:n, 2 + t % 2:4 + t % 2, :].rearrange("p b n -> p (b n)")

        @block.sync
        def _(sp):
            sp.wait_ge(mod_in, 16 * 5)
            for i in range(NT):
                sp.wait_ge(x_in[i], 16)
            for kind in range(3):
                self.load_expert(sp, 0, 0, kind)
            self.load_expert(sp, 1, 1, 0)
            sp.wait_ge(halves, 2)
            self.load_expert(sp, 1, 1, 1)
            self.load_expert(sp, 1, 1, 2)

        @block.gpsimd
        def _(pool):
            link = chain(pool, pchain)
            for t in range(NT):
                n = rows(t)
                for s, ready, done in ((ss1, sq1, rs1), (ss2, sq2, rs2)):
                    pool.wait_ge(ready, t + 1)
                    self.power(pool, link, s[:, t:t + 1], 1, n, 1.0 / D, done)
                if t == 1:
                    pool.wait_ge(ss_ready, 1)
                    self.power(pool, link, ss8, H, NS, 1.0 / DV, ss_power)

        @block.scalar
        def _(act):
            def evac_mix(t):
                n = rows(t)
                act.wait_ge(tr_done, t + 1)
                if t >= 2:
                    act.wait_ge(proj_done, t - 1)
                act.activation(mixT[t % 2][:, 0:4, 0:n],
                               PS[:, 0, :].rearrange("p (k t) -> p k t", k=4)[:, :, 0:n], ACT.Copy).then_inc(ev_a, 1)

            def evac_h2(t):
                m = rows(t)
                act.wait_ge(h2_tr, t + 1)
                if t >= 2:
                    act.wait_ge(log_done, t - 1)
                act.activation(h2T[t % 2][:, 0:4, 0:m],
                               PS[:, 5, :].rearrange("p (k t) -> p k t", k=4)[:, :, 0:m], ACT.Copy).then_inc(h2_ev, 1)

            evac_mix(0)
            row_of = lambda c: self.mod[NS, c * D:(c + 1) * D].partition_broadcast(P)
            act.dma_start(g_post, a["g_post_mix"].partition_broadcast(P)).then_inc(mod_in, 16)
            act.dma_start(mod[0], row_of(2)).then_inc(mod_in, 16)
            act.dma_start(self.x1[:, 0, :], x_of[0]).then_inc(x_in[0], 16)
            act.dma_start(g_pre, a["g_pre_ffn"].partition_broadcast(P)).then_inc(mod_in, 16)
            act.dma_start(mod[1], row_of(4)).then_inc(mod_in, 16)
            act.dma_start(mod[2], row_of(3)).then_inc(mod_in, 16)
            for t in range(1, NT):
                act.dma_start(self.x1[0:rows(t), t, :], x_of[t]).then_inc(x_in[t], 16)
            for b in range(SB):
                act.dma_start(osb[ST * b:ST * b + ST].rearrange("t (h d) -> t h d", h=H),
                              self.o_sample[b].rearrange("(h t) d -> t h d", h=H)).then_inc(o_in, 16)
            for i, c in enumerate((2, 4, 3)):
                act.dma_start(mod[3 + i][0:NS], self.mod[0:NS, c * D:(c + 1) * D]).then_inc(mod_in_s, 16)

            for t in range(NT):
                n = rows(t)
                if t < 4:
                    act.wait_ge(proj_done, t + 1)
                else:
                    act.wait_ge(summed, 2)
                if t >= 2:
                    act.wait_ge(h2_tr, t - 1)
                    act.wait_ge(h2_out2[t % 2], 16 * (t // 2))
                act.activation(hv[t % 2][0:n], proj(t, n), ACT.Square, accum_out=ss1[0:n, t:t + 1]).then_inc(sq1, 1)
                if t >= 1:
                    evac_h2(t - 1)
                if t + 1 < NT:
                    evac_mix(t + 1)
                act.wait_ge(x1_done, t + 1)
                act.activation(hv[t % 2][0:n], self.x1[0:n, t, :], ACT.Square,
                               accum_out=ss2[0:n, t:t + 1]).then_inc(sq2, 1)
                act.wait_ge(h2_done, t + 1)
                act.dma_start(self.h2[P * t:P * t + n, :], hv[t % 2][0:n]).then_inc(h2_out2[t % 2], 16)
            evac_h2(NT - 1)
            act.wait_ge(exp_in, 1)
            act.activation(eg, eg, ACT.Exp).then_inc(exp_out, 1)
            act.wait_ge(exp_in, 2)
            act.activation(ee, ee, ACT.Exp).then_inc(exp_out, 1)
            act.wait_ge(tr_done, NT)
            act.dma_start(self.ga[0], self.mod[NS, 5 * D:6 * D].partition_broadcast(P)).then_inc(self.ga_in, 16)
            act.dma_start(self.ga[1][0:NS], self.mod[0:NS, 5 * D:6 * D]).then_inc(self.ga_in, 16)
            act.dma_start(self.ga[2], self.a["g_post_ffn"].partition_broadcast(P)).then_inc(self.ga_in, 16)

        @block.vector
        def _(dve):
            link = chain(dve, dchain)

            def evac_mix(t):
                n = rows(t)
                dve.wait_ge(tr_done, t + 1)
                if t >= 2:
                    dve.wait_ge(proj_done, t - 1)
                dve.tensor_copy(mixT[t % 2][:, 4:8, 0:n],
                                PS[:, 1, :].rearrange("p (k t) -> p k t", k=4)[:, :, 0:n]).then_inc(ev_d, 1)

            def evac_h2(t):
                n = rows(t)
                dve.wait_ge(h2_tr, t + 1)
                if t >= 2:
                    dve.wait_ge(log_done, t - 1)
                dve.tensor_copy(h2T[t % 2][:, 4:8, 0:n],
                                PS[:, 6, :].rearrange("p (k t) -> p k t", k=4)[:, :, 0:n]).then_inc(h2_ev2, 1)

            def read_logits(t):
                n = rows(t)
                dve.wait_ge(log_done, t + 1)
                dve.tensor_tensor(self.logits[0:n, t, :], PS[0:n, 7, 20 * t:20 * t + 20], self.b_r[0:n], ALU.add
                                  ).then_inc(log_read, 1)

            def modulation(i, n):
                dve.tensor_tensor(mod[i][0:n], mod[i][0:n], g_post[0:n], ALU.mult)
                link(dve.scalar_tensor_tensor(mod[i + 1][0:n], mod[i + 1][0:n], 1.0, g_pre[0:n], ALU.add, ALU.mult))

            dve.wait_ge(self.table_in, 64)
            link(dve.memset(self.logits, 0.0))
            link(dve.memset(both[:, 80:96], 0.0))
            evac_mix(0)
            dve.wait_ge(mod_in, 16 * 5)
            modulation(0, P)
            for t in range(NT):
                n = rows(t)
                i = 0 if t < 4 else 3
                x1 = self.x1[0:n, t, :]
                h = hv[t % 2][0:n]
                if t == 4:
                    for c in range(2):
                        bank = proj_bank(t, c)
                        dve.wait_ge(halves, c + 1)
                        link(dve.tensor_copy(half, PS[NS:P, bank, :]))
                        dve.tensor_tensor(PS[0:NS, bank, :], PS[0:NS, bank, :], half, ALU.add).then_inc(summed, 1)
                        dve.wait_ge(summed, c + 1)
                if t >= 1:
                    evac_h2(t - 1)
                if t + 1 < NT:
                    evac_mix(t + 1)
                dve.wait_ge(rs1, t + 1)
                dve.wait_ge(x_in[t], 16)
                link(dve.scalar_tensor_tensor(h, proj(t, n), ss1[0:n, t:t + 1], mod[i][0:n], ALU.mult, ALU.mult))
                dve.tensor_tensor(x1, x1, h, ALU.add).then_inc(x1_done, 1)
                if t >= 1:
                    read_logits(t - 1)
                dve.wait_ge(rs2, t + 1)
                dve.wait_ge(x1_done, t + 1)
                link(dve.scalar_tensor_tensor(h, x1, ss2[0:n, t:t + 1], mod[i + 1][0:n], ALU.mult, ALU.mult))
                dve.tensor_tensor(h, h, mod[i + 2][0:n], ALU.add).then_inc(h2_done, 1)
                if t == 1:
                    dve.wait_ge(o_in, 16 * SB)
                    self.head_norm(dve, link, osb, sq, ss8, L.mix[0:NS, 4, 0:512], NS, ss_ready, ss_power, 1
                                   ).then_inc(mix_ready, 1)
                    dve.wait_ge(mod_in_s, 16 * 3)
                    modulation(3, NS)
            evac_h2(NT - 1)
            read_logits(NT - 1)
            dve.wait_ge(log_read, NT)

            def bc(x, k):
                return x.unsqueeze(2).to_broadcast([P, NT, k])

            def first_max(dst, vals, top):
                link(dve.tensor_tensor(dst, vals, bc(top, 4), ALU.is_equal))
                link(dve.tensor_tensor(dst, dst, L.cst("desc").unsqueeze(1).to_broadcast([P, NT, 4]), ALU.mult))
                link(dve.tensor_reduce(rk, dst, AX, ALU.max))
                link(dve.tensor_tensor(dst, dst, bc(rk, 4), ALU.is_equal))

            lg, le = self.logits[:, :, 0:4], self.logits[:, :, 4:20]
            link(dve.tensor_reduce(gm, lg, AX, ALU.max))
            dve.tensor_tensor(eg, lg, bc(gm, 4), ALU.subtract).then_inc(exp_in, 1)
            first_max(og, lg, gm)
            by_group = lambda x: x.rearrange("p t (g j) -> p t g j", g=4)
            ogb = og.unsqueeze(3).to_broadcast([P, NT, 4, 4])
            link(dve.tensor_tensor(by_group(prod), by_group(le), ogb, ALU.mult))
            link(dve.tensor_reduce(ee, prod.rearrange("p t (g j) -> p t j g", g=4), AX, ALU.add))
            link(dve.tensor_reduce(gs, ee, AX, ALU.max))
            dve.tensor_tensor(ee, ee, bc(gs, 4), ALU.subtract).then_inc(exp_in, 1)
            dve.wait_ge(exp_out, 2)
            link(dve.tensor_reduce(m12[:, :, 0], ee, AX, ALU.max))
            first_max(o1, ee, m12[:, :, 0])
            link(dve.scalar_tensor_tensor(ee, o1, -2.0, ee, ALU.mult, ALU.add))
            link(dve.tensor_reduce(m12[:, :, 1], ee, AX, ALU.max))
            first_max(o2, ee, m12[:, :, 1])
            link(dve.tensor_tensor(ws, m12[:, :, 0], m12[:, :, 1], ALU.add))
            link(dve.tensor_reduce(gs, eg, AX, ALU.add))
            link(dve.tensor_tensor(ws, ws, gs, ALU.mult))
            link(dve.reciprocal(ws, ws))
            link(dve.tensor_tensor(self.weights, m12, bc(ws, 2), ALU.mult))
            for j, oj in ((0, o1), (1, o2)):
                link(dve.tensor_tensor(by_group(hot[:, j]), ogb, oj.unsqueeze(2).to_broadcast([P, NT, 4, 4]), ALU.mult))
                link(dve.memset(hot[NS:P, j, 4, :], 0.0))
            dve.tensor_tensor(hot[:, 2], hot[:, 0], hot[:, 1], ALU.add).then_inc(hot_done, 1)
            dve.wait_ge(rank_done, 1)
            total = PS[:, 7, RK + 80:RK + 96]
            link(dve.tensor_scalar(over, total, float(P), None, ALU.is_gt))
            for i in range(2, -(-TOK // P)):
                link(dve.tensor_scalar(delta, total, float(P * i), None, ALU.is_gt))
                link(dve.tensor_tensor(over, over, delta, ALU.add))
            oa = ovall.rearrange("p (e f) -> p e f", e=NE)
            link(dve.tensor_tensor(oa, over.unsqueeze(1).to_broadcast([P, NE, NE]),
                                   L.cst("earlier").rearrange("p (e f) -> p e f", e=NE), ALU.mult))
            link(dve.tensor_reduce(ovpre, oa, AX, ALU.add))
            link(dve.tensor_scalar(delta, ovpre, float(P), float(P * (MAIN - 1)), ALU.mult, ALU.add))
            link(dve.tensor_tensor(delta, delta, L.cst("mainbase"), ALU.subtract))
            rank = PS[:, 7, RK:RK + 80].rearrange("p (t e) -> p t e", t=NT)
            link(dve.tensor_scalar(prod, rank, float(P), None, ALU.is_ge))
            link(dve.tensor_tensor(prod, prod, delta.unsqueeze(1).to_broadcast([P, NT, NE]), ALU.mult))
            link(dve.tensor_tensor(prod, rank, prod, ALU.add))
            link(dve.tensor_tensor(prod, prod, L.cst("mainbase").unsqueeze(1).to_broadcast([P, NT, NE]), ALU.add))
            link(dve.tensor_tensor(hot[:, 0:2], hot[:, 0:2], prod.unsqueeze(1).to_broadcast([P, 2, NT, NE]), ALU.mult))
            link(dve.tensor_reduce(slotf.rearrange("p t j -> p j t"), hot[:, 0:2], AX, ALU.add))
            sl = slotf.rearrange("p t j -> p (t j)")
            link(dve.tensor_tensor(G, sl.unsqueeze(2).to_broadcast([P, 10, NTILE + 1]),
                                   L.cst("tilestart").unsqueeze(1).to_broadcast([P, 10, NTILE + 1]), ALU.is_ge))
            link(dve.tensor_reduce(below, G, AX, ALU.add))
            dve.tensor_tensor(C, G[:, :, 0:NTILE], G[:, :, 1:], ALU.subtract)
            link(dve.scalar_tensor_tensor(row, below, -float(P), sl, ALU.mult, ALU.add))
            link(dve.tensor_scalar(row, row, float(P), None, ALU.add))
            dve.tensor_tensor(R, row.unsqueeze(2).to_broadcast([P, 10, P]),
                              L.cst("row").unsqueeze(1).to_broadcast([P, 10, P]), ALU.is_equal).then_inc(picks_done, 1)
            C4 = C.rearrange("p (t j) c -> p t j c", j=2)
            dve.tensor_tensor(C4, C4, L.cst("token").unsqueeze(2).unsqueeze(3).to_broadcast([P, NT, 2, NTILE]),
                              ALU.mult).then_inc(dchain, 1)
            link.count[0] += 1
            dve.wait_ge(dchain, link.count[0])
            dve.memset(C[NS:P, 8:10, :], 0.0).then_inc(picks_done, 1)
            dve.tensor_copy(self.ints[:, 32:42], sl)
            dve.wait_ge(table_made, 1)
            dve.tensor_copy(self.ints[:, 0:NTILE], PS[:, 6, 0:NTILE]).then_inc(table_done, 1)
            link(dve.tensor_tensor(ovpre, ovpre, over, ALU.add))
            ob = ovall[:, 0:OVER * NE].rearrange("p (j e) -> p j e", j=OVER)
            link(dve.tensor_tensor(ob, ovpre.unsqueeze(1).to_broadcast([P, OVER, NE]),
                                   L.cst("index").unsqueeze(2).to_broadcast([P, OVER, NE]), ALU.is_le))
            link(dve.tensor_reduce(eid[:, 0:OVER], ob, AX, ALU.add))
            link(dve.tensor_scalar_min(eid[:, 0:OVER], eid[:, 0:OVER], float(NE - 1)))
            link(dve.tensor_copy(eid[:, OVER:OVER + 1], ovpre[:, NE - 1:NE]))
            link(dve.tensor_copy(self.ints[:, 48:49 + OVER], eid))

        @block.tensor
        def _(pe):
            def mix_tr(t):
                n = rows(t)
                if t >= 1:
                    pe.wait_ge(ev_a, t)
                    pe.wait_ge(ev_d, t)
                if t == 4:
                    pe.wait_ge(mix_ready, 1)
                for k in range(KC):
                    last = pe.transpose(PS[:, k // 4, (k % 4) * P:(k % 4) * P + n], L.mix[0:n, t, k::KC],
                                        L.cst("ident", n)[:, 0:n])
                last.then_inc(tr_done, 1)

            def h2_tr_of(t):
                n = rows(t)
                pe.wait_ge(h2_done, t + 1)
                if t >= 1:
                    pe.wait_ge(h2_ev, t)
                    pe.wait_ge(h2_ev2, t)
                for k in range(KC):
                    last = pe.transpose(PS[:, 5 + k // 4, (k % 4) * P:(k % 4) * P + n], hv[t % 2][0:n, k::KC],
                                        L.cst("ident", n)[:, 0:n])
                last.then_inc(h2_tr, 1)

            def logits_of(t):
                n = rows(t)
                pe.wait_ge(h2_ev, t + 1)
                pe.wait_ge(h2_ev2, t + 1)
                for c in COLS[:-(-n // 64)]:
                    for k in range(KC):
                        last = pe.matmul(PS[c:c + 64, 7, 20 * t:20 * t + 20], h2T[t % 2][:, k, c:c + 64],
                                         self.w_r[:, k, :], start=k == 0, stop=k == KC - 1)
                last.then_inc(log_done, 1)

            mix_tr(0)
            for t in range(NT):
                n = rows(t)
                pe.wait_ge(ev_a, t + 1)
                pe.wait_ge(ev_d, t + 1)
                for i, c in enumerate((t % 2, 1 - t % 2)):
                    if t == 0:
                        pe.wait_ge(self.ring_full[W_OUT[c]], 16 * STATIC_USES[W_OUT[c]] + 16)
                    if t >= 2 - i:
                        pe.wait_ge(x1_done, t - 1 + i)
                    w = L.ring[W_OUT[c]].rearrange("p (k n) -> p k n", k=KC)
                    if t < 4:
                        for k in range(KC):
                            last = pe.matmul(PS[:, proj_bank(t, c), :], mixT[t % 2][:, k, :], w[:, k, :],
                                             start=k == 0, stop=k == KC - 1)
                    else:
                        for k in range(KC // 2):
                            for c0, kk in ((0, k), (NS, k + KC // 2)):
                                last = pe.matmul(PS[c0:c0 + NS, proj_bank(t, c), :], mixT[t % 2][:, kk, 0:NS],
                                                 w[:, kk, :], start=k == 0, stop=k == KC // 2 - 1)
                        last.then_inc(halves, 1)
                if t < 4:
                    last.then_inc(proj_done, 1)
                if t >= 1:
                    h2_tr_of(t - 1)
                if t + 1 < NT:
                    mix_tr(t + 1)
                if t >= 1:
                    logits_of(t - 1)
            h2_tr_of(NT - 1)
            logits_of(NT - 1)
            pe.wait_ge(hot_done, 1)
            pe.matmul(PS[:, 7, RK:RK + 96], L.cst("before"), both, start=True, stop=False)
            for d in range(1, NT + 1):
                last = pe.matmul(PS[:, 7, RK + 16 * d:RK + 96], L.cst("ones"), both[:, 0:96 - 16 * d], start=False,
                                 stop=d == NT)
            last.then_inc(rank_done, 1)
            pe.wait_ge(picks_done, 2)
            for c in COLS:
                for n in range(2 * NT):
                    last = pe.matmul(PS[c:c + 64, 6, 0:NTILE], R[:, n, c:c + 64], C[:, n, :], start=n == 0,
                                     stop=n == 2 * NT - 1)
            last.then_inc(table_made, 1)

    def expert_buffers(self):
        L = self.L
        n = L.HT
        out = {}
        for name, size in (("xg", D), ("xT", D), ("sg", DE), ("h", DE), ("hT", DE), ("y", D)):
            out[name] = [L.at(n + size * i, size) for i in range(2)]
            n += 2 * size
        return out

    def experts(self, block):
        nc, L, PS = self.nc, self.L, self.PS
        (x_tr, xt_a, xt_d, g_done, u_done, sg_done, h_done, h_tr, ht_ev, d_done, y_a, y_d, ix_done) = (
            self.sem("f_" + n) for n in ("x_tr", "xt_a", "xt_d", "gate", "up", "silu", "h", "h_tr", "ht_ev", "down",
                                         "y_a", "y_d", "index"))
        xg_in = [self.sem("f_xg_in0"), self.sem("f_xg_in1")]
        y_out = [self.sem("f_y_out0"), self.sem("f_y_out1")]
        B = self.expert_buffers()
        k3 = lambda x, k: x.rearrange("p (k t) -> p k t", k=k)
        xT, hT = [k3(x, KC) for x in B["xT"]], [k3(x, FC) for x in B["hT"]]
        full0 = [16 * (STATIC_USES[s] + (s in W_OUT)) for s in range(6)]

        def looped(eng, step):
            for e in range(3):
                step(e, e % 2, True, True)
            with eng.Fori(0, (MAIN - 4) // 2) as i:
                step(2 * i + 3, 1, True, True)
                step(2 * i + 4, 0, True, True)
            step(MAIN - 1, 1, True, False)
            step(MAIN, 0, False, False)

        @block.sync
        def _(sp):
            def store(e, par):
                sp.wait_ge(y_a, e + 1)
                sp.wait_ge(y_d, e + 1)
                sp.dma_start(self.y_rows[bass.ds(e * P, P)], B["y"][par]).then_inc(y_out[par], 16)

            def step(e, par):
                for kind, free in ((0, g_done), (1, u_done), (2, d_done)):
                    sp.wait_ge(free, e + 1)
                    self.load_expert(sp, e + 2, par, kind)
                store(e, par)
            with sp.Fori(0, (MAIN - 2) // 2) as i:
                step(2 * i, 0)
                step(2 * i + 1, 1)
            store(MAIN - 2, 0)
            store(MAIN - 1, 1)
            sp.wait_ge(y_out[0], 16 * MAIN // 2)
            sp.wait_ge(y_out[1], 16 * MAIN // 2)

        @block.gpsimd
        def _(pool):
            def gather(e, par):
                if differs(e, 0) and differs(e, 1):
                    pool.wait_ge(x_tr, e - 1)
                index = self.ints[:, 60 + par:61 + par]
                pool.tensor_copy(index, self.ints[:, bass.ds(e, 1)]).then_inc(ix_done, 1)
                pool.wait_ge(ix_done, e + 1)
                self.stand_apart(pool)
                pool.indirect_dma_start(B["xg"][par], None, self.h2,
                                        bass.IndirectOffsetOnAxis(ap=index, axis=0)).then_inc(xg_in[par], 16)

            pool.wait_ge(self.table_done, 1)
            pool.wait_ge(self.h2_outs[0], 48)
            pool.wait_ge(self.h2_outs[1], 32)
            gather(0, 0)

            def step(e, par, here, ahead):
                if ahead:
                    gather(e + 1, 1 - par)
            looped(pool, step)

        @block.scalar
        def _(act):
            def evac_x(e, par):
                act.wait_ge(x_tr, e + 1)
                act.activation(xT[par][:, 0:4, :], k3(PS[:, 2, :], 4), ACT.Copy).then_inc(xt_a, 1)

            evac_x(0, 0)

            def step(e, par, here, ahead):
                if here:
                    act.wait_ge(g_done, e + 1)
                    if differs(e, 0) and differs(e, 1):
                        act.wait_ge(h_done, e - 1)
                    act.activation(B["sg"][par], PS[:, 0, :], ACT.Silu).then_inc(sg_done, 1)
                if ahead:
                    evac_x(e + 1, 1 - par)
                if differs(e, 0):
                    act.wait_ge(d_done, e)
                    if differs(e, 1) and differs(e, 2):
                        act.wait_ge(y_out[1 - par], 8 * (e - 1 - (1 - par)))
                    act.activation(B["y"][1 - par][:, 0:512], PS[:, 5, :], ACT.Copy).then_inc(y_a, 1)
                if here:
                    act.wait_ge(h_tr, e + 1)
                    act.activation(hT[par], k3(PS[:, 4, :], FC), ACT.Copy).then_inc(ht_ev, 1)
            looped(act, step)

        @block.vector
        def _(dve):
            def evac_x(e, par):
                dve.wait_ge(x_tr, e + 1)
                dve.tensor_copy(xT[par][:, 4:8, :], k3(PS[:, 3, :], 4)).then_inc(xt_d, 1)

            evac_x(0, 0)

            def step(e, par, here, ahead):
                if here:
                    dve.wait_ge(sg_done, e + 1)
                    dve.wait_ge(u_done, e + 1)
                    if differs(e, 0) and differs(e, 1):
                        dve.wait_ge(h_tr, e - 1)
                    dve.tensor_tensor(B["h"][par], B["sg"][par], PS[:, 1, :], ALU.mult).then_inc(h_done, 1)
                if ahead:
                    evac_x(e + 1, 1 - par)
                if differs(e, 0):
                    dve.wait_ge(d_done, e)
                    if differs(e, 1) and differs(e, 2):
                        dve.wait_ge(y_out[1 - par], 8 * (e - 1 - (1 - par)))
                    dve.tensor_copy(B["y"][1 - par][:, 512:1024], PS[:, 6, :]).then_inc(y_d, 1)
            looped(dve, step)

        @block.tensor
        def _(pe):
            def tokens(e, par):
                pe.wait_ge(xg_in[par], 16 + 8 * (e - par))
                if differs(e, 0):
                    pe.wait_ge(xt_a, e)
                    pe.wait_ge(xt_d, e)
                for k in range(KC):
                    last = pe.transpose(PS[:, 2 + k // 4, (k % 4) * P:(k % 4 + 1) * P], B["xg"][par][:, k::KC],
                                        L.cst("ident"))
                last.then_inc(x_tr, 1)

            def gate_up(e, par):
                pe.wait_ge(xt_a, e + 1)
                pe.wait_ge(xt_d, e + 1)
                if differs(e, 0):
                    pe.wait_ge(h_done, e)
                for kind, done in ((0, g_done), (1, u_done)):
                    slot = EXPERT[par][kind]
                    pe.wait_ge(self.ring_full[slot], full0[slot] + 16 + 8 * (e - par))
                    w = k3(L.ring[slot], KC)
                    for k in range(KC):
                        last = pe.matmul(PS[:, kind, :], xT[par][:, k, :], w[:, k, :], start=k == 0, stop=k == KC - 1)
                    last.then_inc(done, 1)

            def down(e, par):
                pe.wait_ge(ht_ev, e + 1)
                if differs(e, 0):
                    pe.wait_ge(y_a, e)
                    pe.wait_ge(y_d, e)
                slot = EXPERT[par][2]
                pe.wait_ge(self.ring_full[slot], full0[slot] + 16 + 8 * (e - par))
                w = k3(L.ring[slot], FC)
                for c in range(2):
                    for k in range(FC):
                        last = pe.matmul(PS[:, 5 + c, :], hT[par][:, k, :], w[:, k, 512 * c:512 * c + 512],
                                         start=k == 0, stop=k == FC - 1)
                last.then_inc(d_done, 1)

            def step(e, par, here, ahead):
                if here:
                    gate_up(e, par)
                if ahead:
                    tokens(e + 1, 1 - par)
                if differs(e, 0):
                    down(e - 1, 1 - par)
                if here:
                    pe.wait_ge(h_done, e + 1)
                    if differs(e, 0):
                        pe.wait_ge(ht_ev, e)
                    for k in range(FC):
                        last = pe.transpose(PS[:, 4, P * k:P * k + P], B["h"][par][:, k::FC], L.cst("ident"))
                    last.then_inc(h_tr, 1)
            tokens(0, 0)
            looped(pe, step)

    def later_tiles(self, block):
        nc, L, PS = self.nc, self.L, self.PS
        (ix, xg_in, x_tr, xt, gate, silu, h_done, h_tr, ht, down, y_ready, y_out, up) = (
            self.sem("g_" + n) for n in ("index", "xg_in", "x_tr", "xt", "gate", "silu", "h", "h_tr", "ht", "down",
                                         "y_ready", "y_out", "up"))
        B = self.expert_buffers()
        k3 = lambda x, k: x.rearrange("p (k t) -> p k t", k=k)
        xg, xT, sg, h, hT, y = (B[n][0] for n in ("xg", "xT", "sg", "h", "hT", "y"))
        w_in = [self.sem("g_w_in" + str(i)) for i in range(3)]

        def looped(eng, tile):
            many = eng.value_load(self.ints[0:1, 48 + OVER:49 + OVER], min_val=0, max_val=OVER)
            with eng.If(many > 0):
                with eng.Fori(0, OVER) as j:
                    with eng.If(many > j):
                        tile(j)
                        eng.wait_ge(y_out, 16 * j + 16)
                        self.stand_apart(eng)

        @block.sync
        def _(sp):
            def tile(j):
                e = sp.value_load(self.ints[0:1, bass.ds(48 + j, 1)], min_val=0, max_val=NE - 1)
                for kind, n in enumerate(("w_gate", "w_up", "w_down")):
                    sp.dma_start(L.ring[EXPERT[0][kind]], self.a[n][0][bass.ds(e, 1)].rearrange(
                        "a (p k) n -> p (a k n)", k=FC if kind == 2 else KC)).then_inc(w_in[kind], 16)
                sp.wait_ge(y_ready, 2 * j + 2)
                sp.dma_start(self.y_rows[bass.ds((j + MAIN) * P, P)], y).then_inc(y_out, 16)
            looped(sp, tile)

        @block.gpsimd
        def _(pool):
            def tile(j):
                index = self.ints[:, 60:61]
                pool.tensor_copy(index, self.ints[:, bass.ds(j + MAIN, 1)]).then_inc(ix, 1)
                pool.wait_ge(ix, j + 1)
                self.stand_apart(pool)
                pool.indirect_dma_start(xg, None, self.h2,
                                        bass.IndirectOffsetOnAxis(ap=index, axis=0)).then_inc(xg_in, 16)
            looped(pool, tile)

        @block.scalar
        def _(act):
            def tile(j):
                act.wait_ge(x_tr, j + 1)
                act.activation(xT[:, 0:512], PS[:, 2, :], ACT.Copy).then_inc(xt, 1)
                act.wait_ge(gate, j + 1)
                act.activation(sg, PS[:, 0, :], ACT.Silu).then_inc(silu, 1)
                act.wait_ge(h_tr, j + 1)
                act.activation(hT, PS[:, 4, :], ACT.Copy).then_inc(ht, 1)
                act.wait_ge(down, j + 1)
                act.activation(y[:, 0:512], PS[:, 5, :], ACT.Copy).then_inc(y_ready, 1)
            looped(act, tile)

        @block.vector
        def _(dve):
            def tile(j):
                dve.wait_ge(x_tr, j + 1)
                dve.tensor_copy(xT[:, 512:1024], PS[:, 3, :]).then_inc(xt, 1)
                dve.wait_ge(silu, j + 1)
                dve.wait_ge(up, j + 1)
                dve.tensor_tensor(h, sg, PS[:, 1, :], ALU.mult).then_inc(h_done, 1)
                dve.wait_ge(down, j + 1)
                dve.tensor_copy(y[:, 512:1024], PS[:, 6, :]).then_inc(y_ready, 1)
            looped(dve, tile)

        @block.tensor
        def _(pe):
            def tile(j):
                pe.wait_ge(xg_in, 16 * j + 16)
                for k in range(KC):
                    last = pe.transpose(PS[:, 2 + k // 4, (k % 4) * P:(k % 4 + 1) * P], xg[:, k::KC], L.cst("ident"))
                last.then_inc(x_tr, 1)
                pe.wait_ge(xt, 2 * j + 2)
                for kind, done in ((0, gate), (1, up)):
                    pe.wait_ge(w_in[kind], 16 * j + 16)
                    for k in range(KC):
                        last = pe.matmul(PS[:, kind, :], k3(xT, KC)[:, k, :], k3(L.ring[EXPERT[0][kind]], KC)[:, k, :],
                                         start=k == 0, stop=k == KC - 1)
                    last.then_inc(done, 1)
                pe.wait_ge(h_done, j + 1)
                for k in range(FC):
                    last = pe.transpose(PS[:, 4, P * k:P * k + P], h[:, k::FC], L.cst("ident"))
                last.then_inc(h_tr, 1)
                pe.wait_ge(ht, j + 1)
                pe.wait_ge(w_in[2], 16 * j + 16)
                for c in range(2):
                    for k in range(FC):
                        last = pe.matmul(PS[:, 5 + c, :], k3(hT, FC)[:, k, :],
                                         k3(L.ring[EXPERT[0][2]], FC)[:, k, 512 * c:512 * c + 512],
                                         start=k == 0, stop=k == FC - 1)
                last.then_inc(down, 1)
            looped(pe, tile)

    def combine(self, block):
        nc, a, o, L = self.nc, self.a, self.o, self.L
        y_in = [self.sem(f"h_y_in{t}") for t in range(NT)]
        sq, rs, out_done, stored = (self.sem("h_" + n) for n in ("sq", "rs", "out", "stored"))
        dchain, pchain, y_done = self.sem("dve_chain_h"), self.sem("pool_chain_h"), self.sem("h_y")
        yb = [[L.at(D * (2 * t + j), D) for j in range(2)] for t in range(NT)]
        ga, g, scaled = self.ga[0:2], self.ga[2], self.sem("h_scaled")
        y_o = [o["y_prompt"][0, t * P:(t + 1) * P, :] for t in range(4)] + [o["y_sample"].rearrange("b t n -> (b t) n")]
        @block.gpsimd
        def _(pool):
            link = chain(pool, pchain)
            for t in range(NT):
                n = rows(t)
                for j in range(2):
                    pool.indirect_dma_start(yb[t][j][0:n], None, self.y_rows, bass.IndirectOffsetOnAxis(
                        ap=self.ints[0:n, 32 + 2 * t + j:33 + 2 * t + j], axis=0)).then_inc(y_in[t], 16)
            for t in range(NT):
                pool.wait_ge(sq, t + 1)
                self.power(pool, link, self.rstd[:, t:t + 1], 1, rows(t), 1.0 / D, rs)

        @block.scalar
        def _(act):
            def scale(t):
                act.wait_ge(y_in[t], 32)
                act.activation(yb[t][0][0:rows(t)], yb[t][0][0:rows(t)], ACT.Copy,
                               scale=self.weights[0:rows(t), t, 0:1]).then_inc(scaled, 1)

            scale(0)
            for t in range(NT):
                n = rows(t)
                if t + 1 < NT:
                    scale(t + 1)
                act.wait_ge(y_done, t + 1)
                act.activation(yb[t][1][0:n], yb[t][0][0:n], ACT.Square,
                               accum_out=self.rstd[0:n, t:t + 1]).then_inc(sq, 1)

        @block.vector
        def _(dve):
            link = chain(dve, dchain)
            dve.wait_ge(self.ga_in, 48)
            dve.tensor_tensor(ga[0], ga[0], g, ALU.mult)
            link(dve.tensor_tensor(ga[1][0:NS], ga[1][0:NS], g[0:NS], ALU.mult))

            def finish(t):
                n = rows(t)
                dve.wait_ge(rs, t + 1)
                y = yb[t][0][0:n]
                link(dve.scalar_tensor_tensor(y, y, self.rstd[0:n, t:t + 1], ga[t // 4][0:n], ALU.mult, ALU.mult))
                dve.tensor_tensor(y, y, self.x1[0:n, t, :], ALU.add).then_inc(out_done, 1)
            for t in range(NT):
                n = rows(t)
                dve.wait_ge(scaled, t + 1)
                dve.scalar_tensor_tensor(yb[t][0][0:n], yb[t][1][0:n], self.weights[0:n, t, 1:2], yb[t][0][0:n],
                                         ALU.mult, ALU.add).then_inc(y_done, 1)
                if t >= 1:
                    finish(t - 1)
            finish(NT - 1)

        @block.sync
        def _(sp):
            for t in range(NT):
                sp.wait_ge(out_done, t + 1)
                sp.dma_start(y_o[t], yb[t][0][0:rows(t)]).then_inc(stored, 16)
            sp.wait_ge(stored, 16 * NT)


INS = ["x_prompt", "x_sample", "cache_k", "cache_v", "page_table", "c_prompt", "c_sample", "w_ada", "b_ada",
       "g_pre_mix", "g_post_mix", "g_pre_ffn", "g_post_ffn", "w_in", "lam_q1", "lam_k1", "lam_q2", "lam_k2",
       "g_subln", "sgu_ln_g", "sgu_ln_b", "sgu_ws", "sgu_bs", "w_out", "w_rg", "b_rg", "w_re", "b_re",
       "w_gate", "w_up", "w_down"]
OUTS = {"y_prompt": (1, SEQ, D), "y_sample": (SB, ST, D), "k_prompt": (1, 1, SEQ, H, 2 * DQK),
        "v_prompt": (1, 1, SEQ, H, DV), "sgu_prompt": (1, 1, P, 512), "k_sample": (1, SB, ST, H, 2 * DQK),
        "v_sample": (1, SB, ST, H, DV), "sgu_sample": (1, SB, ST, 512)}


def build(nc, a, o):
    where, table, _ = constant_table()
    with ExitStack() as ctx:
        p = Program(nc, a, o, where, table.shape[1], ctx)
        with nc.Block() as block:
            p.condition(block)
            p.project(block)
            p.attend_prompt(block)
        p.attend_sample()
        p.forget()
        with nc.Block() as block:
            p.merge(block)
            p.experts(block)
        with nc.Block() as block:
            p.later_tiles(block)
            p.combine(block)


def kernel(**inputs):
    from concourse import bacc
    from concourse.bass_utils import run_bass_kernel_spmd

    nc = bacc.Bacc("TRN2", target_bir_lowering=False, num_devices=1)
    _, table, past = constant_table()
    arrays = {n: np.ascontiguousarray(inputs[n]) for n in INS}
    arrays["constants"], arrays["past_bias"] = table, past
    a = {n: nc.dram_tensor("in_" + n, x.shape, mybir.dt.from_np(x.dtype), kind="ExternalInput").ap()
         for n, x in arrays.items()}
    o = {n: nc.dram_tensor("out_" + n, s, F32, kind="ExternalOutput").ap() for n, s in OUTS.items()}
    build(nc, a, o)
    r = run_bass_kernel_spmd(nc, [{"in_" + n: x for n, x in arrays.items()}], core_ids=[0])
    return tuple(r.results[0]["out_" + n] for n in OUTS)
```
